# Optimizing a Trainium2 kernel written in Bass

```python
import jax, jax.numpy as jnp
from jax import lax
import numpy as np

D_MODEL = 1024
BATCH = 1
SEQ = 512
DEPTH = 1
DEC_BATCH = 8
DEC_SEQ = 4
PAST_LEN = 256
PAGE_SIZE = 128

A_HEADS = 4
A_DQK = 128
A_DV = 256
A_CHUNK = 64
B_HEADS = 16
B_KV = 4
B_REP = B_HEADS // B_KV
B_HD = 64
CMP_BLOCK = 64
SEL_BLOCK = 64
N_SEL = 16
WINDOW = 512
SEL_QBLOCK = 64
WIN_QBLOCK = 128
P_HEADS = 8
P_NKEYS = 128
P_EXPERTS = P_NKEYS * P_NKEYS
P_DKEY = 256
P_DHALF = P_DKEY // 2
P_TOPK = 16
P_TBLOCK = 256
DN_ALPHA = (2.0 * DEPTH) ** 0.25
DN_BETA = (8.0 * DEPTH) ** -0.25
LN_EPS = 1e-5
NEG = -1e30

SPLIT_SIZES = (A_HEADS * A_DQK, A_HEADS * A_DQK, A_HEADS * A_DV, A_HEADS, A_HEADS, A_HEADS * A_DV,
               B_HEADS * B_HD, 2 * B_KV * B_HD, 2 * B_KV * B_HD, 2 * B_KV * B_HD, 3 * B_HEADS)
D_IN = sum(SPLIT_SIZES)

kernel_name = "hybrid_mlstm_nsa_peer_step"

def layer_norm(x, g, b):
    xf = x.astype(jnp.float32)
    mu = xf.mean(-1, keepdims=True)
    var = jnp.square(xf - mu).mean(-1, keepdims=True)
    return ((xf - mu) * lax.rsqrt(var + LN_EPS) * g + b).astype(x.dtype)

def alibi_slopes():
    s = 2.0 ** (-8.0 * np.arange(1, B_HEADS + 1) / B_HEADS)
    return jnp.asarray(s, jnp.float32).reshape(B_KV, B_REP)

def in_projection(x, w_in, b_in):
    proj = jnp.einsum('btd,de->bte', x, w_in) + b_in
    return jnp.split(proj, np.cumsum(SPLIT_SIZES)[:-1].tolist(), axis=-1)

def mlstm_scan(q, k, v, i_pre, log_f, C0, n0, m0, chunk):
    b_, h_, t_, _ = q.shape
    nc = t_ // chunk

    def to_chunks(a):
        return jnp.moveaxis(a.reshape(a.shape[:2] + (nc, chunk) + a.shape[3:]), 2, 0)

    causal = jnp.tril(jnp.ones((chunk, chunk), dtype=bool))

    def step(carry, inp):
        C, n, m = carry
        qc, kc, vc, ic, fc = inp
        b = jnp.cumsum(fc, axis=-1)
        d_log = jnp.where(causal, b[..., :, None] - b[..., None, :] + ic[..., None, :], -jnp.inf)
        inter = b + m[..., None]
        m_t = jnp.maximum(inter, d_log.max(-1))
        s = jnp.einsum('bhtd,bhsd->bhts', qc, kc) * jnp.exp(d_log - m_t[..., None])
        w_inter = jnp.exp(inter - m_t)
        num = w_inter[..., None] * jnp.einsum('bhtd,bhdv->bhtv', qc, C) + jnp.einsum('bhts,bhsv->bhtv', s, vc)
        den = w_inter * jnp.einsum('bhtd,bhd->bht', qc, n) + s.sum(-1)
        h = num / jnp.maximum(jnp.abs(den), jnp.exp(-m_t))[..., None]
        b_end = b[..., -1]
        g = b_end[..., None] - b + ic
        m_new = jnp.maximum(b_end + m, g.max(-1))
        a = jnp.exp(b_end + m - m_new)
        w = jnp.exp(g - m_new[..., None])
        C_new = a[..., None, None] * C + jnp.einsum('bhs,bhsd,bhsv->bhdv', w, kc, vc)
        n_new = a[..., None] * n + jnp.einsum('bhs,bhsd->bhd', w, kc)
        return (C_new, n_new, m_new), h

    (C, n, m), h = lax.scan(step, (C0, n0, m0), tuple(to_chunks(a) for a in (q, k, v, i_pre, log_f)))
    h = jnp.moveaxis(h, 0, 2).reshape(b_, h_, t_, v.shape[-1])
    return h, C, n, m

def mlstm_branch(a_q, a_k, a_v, a_i, a_f, a_o, C0, n0, m0, chunk, norm_a_g):
    B, T, _ = a_q.shape
    f32 = jnp.float32

    def heads(a, d):
        return a.reshape(B, T, A_HEADS, d).transpose(0, 2, 1, 3).astype(f32)

    q = heads(a_q, A_DQK)
    k = heads(a_k, A_DQK) * (A_DQK ** -0.5)
    v = heads(a_v, A_DV)
    i_pre = a_i.astype(f32).transpose(0, 2, 1)
    log_f = jax.nn.log_sigmoid(a_f.astype(f32)).transpose(0, 2, 1)
    h, C, n, m = mlstm_scan(q, k, v, i_pre, log_f, C0.astype(f32), n0.astype(f32), m0.astype(f32), chunk)
    mu = h.mean(-1, keepdims=True)
    var = jnp.square(h - mu).mean(-1, keepdims=True)
    h = ((h - mu) * lax.rsqrt(var + LN_EPS)).transpose(0, 2, 1, 3).reshape(B, T, A_HEADS * A_DV) * norm_a_g
    y = (h * jax.nn.sigmoid(a_o.astype(f32))).astype(a_q.dtype)
    return y, C, n, m

def dense_attn(q, k, v, q_pos, k_pos, slopes, window):
    s = jnp.einsum('...qgrd,...kgd->...grqk', q, k).astype(jnp.float32) * (B_HD ** -0.5)
    dist = q_pos[..., None, None, :, None] - k_pos[..., None, None, None, :]
    s = s - slopes[:, :, None, None] * dist.astype(jnp.float32)
    mask = (dist >= 0) & (k_pos >= 0)[..., None, None, None, :]
    if window is not None:
        mask = mask & (dist < window)
    p = jnp.where(mask, jax.nn.softmax(jnp.where(mask, s, NEG), axis=-1), 0.0)
    o = jnp.einsum('...grqk,...kgd->...qgrd', p.astype(v.dtype), v)
    return o, p

def pad_blocks(a):
    pad = (-a.shape[1]) % SEL_BLOCK
    return jnp.pad(a, ((0, 0), (0, pad)) + ((0, 0),) * (a.ndim - 2))

def compress(kv, pe, w_cmp):
    B, Tp, G, d = kv.shape
    blk = kv.reshape(B, Tp // CMP_BLOCK, CMP_BLOCK, G, d) + pe[:, None, :]
    return jnp.einsum('bnlgd,lde->bnge', blk, w_cmp)

def select_attn(q, k, v, q_pos, blk_idx, slopes):
    B, Tq, G, R, d = q.shape
    qb = SEL_QBLOCK if Tq % SEL_QBLOCK == 0 else Tq
    nq = Tq // qb
    n_sel = blk_idx.shape[-1]
    kt = k.transpose(0, 2, 1, 3)
    vt = v.transpose(0, 2, 1, 3)
    b_ix = jnp.arange(B)[:, None, None]
    g_ix = jnp.arange(G)[None, :, None]
    offs = jnp.arange(SEL_BLOCK)

    def one_block(args):
        qi, ii, pi = args
        tok = (ii[..., None] * SEL_BLOCK + offs).reshape(B, G, qb * n_sel * SEL_BLOCK)
        kg = kt[b_ix, g_ix, tok].reshape(B, G, qb, n_sel * SEL_BLOCK, d)
        vg = vt[b_ix, g_ix, tok].reshape(B, G, qb, n_sel * SEL_BLOCK, d)
        tok = tok.reshape(B, G, qb, n_sel * SEL_BLOCK)
        s = jnp.einsum('bqgrd,bgqkd->bgrqk', qi, kg).astype(jnp.float32) * (B_HD ** -0.5)
        dist = (pi[None, None, :, None] - tok)[:, :, None]
        s = s - slopes[None, :, :, None, None] * dist.astype(jnp.float32)
        mask = dist >= 0
        p = jnp.where(mask, jax.nn.softmax(jnp.where(mask, s, NEG), axis=-1), 0.0)
        return jnp.einsum('bgrqk,bgqkd->bqgrd', p.astype(v.dtype), vg)

    q_blocks = jnp.moveaxis(q.reshape(B, nq, qb, G, R, d), 1, 0)
    i_blocks = jnp.moveaxis(blk_idx.reshape(B, G, nq, qb, n_sel), 2, 0)
    p_blocks = q_pos.reshape(nq, qb)
    o = lax.map(one_block, (q_blocks, i_blocks, p_blocks))
    return jnp.moveaxis(o, 0, 1).reshape(B, Tq, G, R, d)

def nsa_cmp_slc(q, k_cmp, v_cmp, k_slc, v_slc, q_pos, nsa_pe, nsa_w_cmp, slopes):
    k_cmp, v_cmp, k_slc, v_slc = pad_blocks(k_cmp), pad_blocks(v_cmp), pad_blocks(k_slc), pad_blocks(v_slc)
    nb = k_cmp.shape[1] // CMP_BLOCK
    kc = compress(k_cmp, nsa_pe[0], nsa_w_cmp[0])
    vc = compress(v_cmp, nsa_pe[1], nsa_w_cmp[1])
    blk_end = (jnp.arange(nb) + 1) * CMP_BLOCK - 1
    o_cmp, p_cmp = dense_attn(q, kc, vc, q_pos, blk_end, slopes, None)
    imp = p_cmp.sum(2)
    j = jnp.arange(nb)[None, :]
    cur = (q_pos // SEL_BLOCK)[:, None]
    imp = jnp.where((j == cur) | (j == 0), float(B_REP + 1), imp)
    imp = jnp.where(j > cur, -1.0, imp)
    _, blk_idx = lax.top_k(imp, min(N_SEL, nb))
    o_slc = select_attn(q, k_slc, v_slc, q_pos, blk_idx, slopes)
    return o_cmp, o_slc

def window_prompt(q, k, v, slopes):
    B, T, G, R, d = q.shape
    nq = T // WIN_QBLOCK
    span = WINDOW + WIN_QBLOCK
    kp = jnp.pad(k, ((0, 0), (WINDOW, 0), (0, 0), (0, 0)))
    vp = jnp.pad(v, ((0, 0), (WINDOW, 0), (0, 0), (0, 0)))
    idx = jnp.arange(nq)[:, None] * WIN_QBLOCK + jnp.arange(span)[None, :]
    q_pos = jnp.arange(T).reshape(nq, WIN_QBLOCK)
    o, _ = dense_attn(q.reshape(B, nq, WIN_QBLOCK, G, R, d), kp[:, idx], vp[:, idx], q_pos, idx - WINDOW,
                      slopes, WINDOW)
    return o.reshape(B, T, G, R, d)

def token_mixers(x, q_pos, C0, n0, m0, chunk, past_cmp, past_slc, win_buf,
                 w_in, b_in, norm_a_g, nsa_pe, nsa_w_cmp):
    B, T, _ = x.shape
    a_q, a_k, a_v, a_i, a_f, a_o, b_q, b_cmp, b_slc, b_win, b_gate = in_projection(x, w_in, b_in)
    y_a, C, n, m = mlstm_branch(a_q, a_k, a_v, a_i, a_f, a_o, C0, n0, m0, chunk, norm_a_g)
    slopes = alibi_slopes()
    q = b_q.reshape(B, T, B_KV, B_REP, B_HD)
    kv_cmp = b_cmp.reshape(B, T, 2, B_KV, B_HD)
    kv_slc = b_slc.reshape(B, T, 2, B_KV, B_HD)
    kv_win = b_win.reshape(B, T, 2, B_KV, B_HD)
    if past_cmp is None:
        all_cmp, all_slc = kv_cmp, kv_slc
        o_win = window_prompt(q, kv_win[:, :, 0], kv_win[:, :, 1], slopes)
        new_win = kv_win[:, -min(WINDOW, T):]
    else:
        all_cmp = jnp.concatenate([past_cmp, kv_cmp], axis=1)
        all_slc = jnp.concatenate([past_slc, kv_slc], axis=1)
        buf = jnp.concatenate([win_buf, kv_win], axis=1)
        wb = win_buf.shape[1]
        k_pos = past_cmp.shape[1] - wb + jnp.arange(buf.shape[1])
        o_win, _ = dense_attn(q, buf[:, :, 0], buf[:, :, 1], q_pos, k_pos, slopes, WINDOW)
        new_win = buf[:, -wb:]
    o_cmp, o_slc = nsa_cmp_slc(q, all_cmp[:, :, 0], all_cmp[:, :, 1], all_slc[:, :, 0], all_slc[:, :, 1],
                               q_pos, nsa_pe, nsa_w_cmp, slopes)
    g = jax.nn.sigmoid(b_gate.astype(jnp.float32).reshape(B, T, 3, B_KV, B_REP))[..., None]
    y_b = (g[:, :, 0] * o_cmp + g[:, :, 1] * o_slc + g[:, :, 2] * o_win).reshape(B, T, B_HEADS * B_HD)
    return y_a, y_b.astype(x.dtype), kv_cmp, kv_slc, new_win, C, n, m

def peer_ffn(x, peer_wq, peer_keys, peer_u, peer_v):
    B, T, D = x.shape
    xf = x.reshape(B * T, D)
    n_tok = B * T
    xf = jnp.pad(xf, ((0, (-n_tok) % P_TBLOCK), (0, 0)))

    def one(xb):
        q = (xb @ peer_wq).reshape(P_TBLOCK, P_HEADS, 2, P_DHALF)
        s = jnp.einsum('tpcd,pckd->tpck', q, peer_keys).astype(jnp.float32)
        s1, i1 = lax.top_k(s[:, :, 0], P_TOPK)
        s2, i2 = lax.top_k(s[:, :, 1], P_TOPK)
        cand = (s1[..., :, None] + s2[..., None, :]).reshape(P_TBLOCK, P_HEADS, P_TOPK * P_TOPK)
        cidx = (i1[..., :, None] * P_NKEYS + i2[..., None, :]).reshape(P_TBLOCK, P_HEADS, P_TOPK * P_TOPK)
        top_s, j = lax.top_k(cand, P_TOPK)
        eidx = jnp.take_along_axis(cidx, j, axis=-1)
        gate = jax.nn.softmax(top_s, axis=-1)
        u = peer_u[eidx]
        v = peer_v[eidx]
        act = jax.nn.gelu(jnp.einsum('td,tpkd->tpk', xb, u).astype(jnp.float32), approximate=False)
        return jnp.einsum('tpk,tpkd->td', (gate * act).astype(v.dtype), v)

    out = lax.map(one, xf.reshape(-1, P_TBLOCK, D)).reshape(-1, D)[:n_tok]
    return out.reshape(B, T, D)

def layer_tail(x, y_a, y_b, w_br_a, w_br_b, w_merge, w_out, ln1_g, ln1_b,
               peer_wq, peer_keys, peer_u, peer_v, ln2_g, ln2_b):
    B, T, D = x.shape
    gates = jax.nn.sigmoid(jnp.einsum('btd,de->bte', x, w_merge)).reshape(B, T, 2, D)
    merged = gates[:, :, 0] * (y_a @ w_br_a) + gates[:, :, 1] * (y_b @ w_br_b)
    h = layer_norm(DN_ALPHA * x + merged @ w_out, ln1_g, ln1_b)
    return layer_norm(DN_ALPHA * h + peer_ffn(h, peer_wq, peer_keys, peer_u, peer_v), ln2_g, ln2_b)

def setup_inputs(seed: int = 0) -> dict:
    key = jax.random.key(seed)
    ks = jax.random.split(key, 28)
    nrm = jax.random.normal
    n_pages = PAST_LEN // PAGE_SIZE
    n_used = DEC_BATCH * n_pages
    n_pool = n_used + n_used // 4
    win_buf = min(WINDOW, PAST_LEN)
    f_start = int(np.cumsum(SPLIT_SIZES)[3])
    b_in = 0.02 * nrm(ks[10], (D_IN,))
    b_in = b_in.at[f_start:f_start + A_HEADS].add(jnp.linspace(3.0, 6.0, A_HEADS))
    return {
        'x_prompt': nrm(ks[0], (BATCH, SEQ, D_MODEL)),
        'x_sample': nrm(ks[1], (DEC_BATCH, DEC_SEQ, D_MODEL)),
        'cache_cmp_kv': nrm(ks[2], (n_pool, PAGE_SIZE, 2, B_KV, B_HD)),
        'cache_slc_kv': nrm(ks[3], (n_pool, PAGE_SIZE, 2, B_KV, B_HD)),
        'cache_win_kv': nrm(ks[4], (DEC_BATCH, win_buf, 2, B_KV, B_HD)),
        'state_C': 0.1 * nrm(ks[5], (DEC_BATCH, A_HEADS, A_DQK, A_DV)),
        'state_n': 0.1 * nrm(ks[6], (DEC_BATCH, A_HEADS, A_DQK)),
        'state_m': 0.5 * nrm(ks[7], (DEC_BATCH, A_HEADS)),
        'page_table': jax.random.permutation(ks[8], n_pool)[:n_used].reshape(DEC_BATCH, n_pages).astype(jnp.int32),
        'w_in': nrm(ks[9], (D_MODEL, D_IN)) * D_MODEL ** -0.5,
        'b_in': b_in,
        'norm_a_g': 1.0 + 0.02 * nrm(ks[11], (A_HEADS * A_DV,)),
        'nsa_pe': 0.02 * nrm(ks[12], (2, CMP_BLOCK, B_HD)),
        'nsa_w_cmp': nrm(ks[13], (2, CMP_BLOCK, B_HD, B_HD)) * (CMP_BLOCK * B_HD) ** -0.5,
        'w_br_a': nrm(ks[14], (A_HEADS * A_DV, D_MODEL)) * (A_HEADS * A_DV) ** -0.5 * DN_BETA,
        'w_br_b': nrm(ks[15], (B_HEADS * B_HD, D_MODEL)) * (B_HEADS * B_HD) ** -0.5 * DN_BETA,
        'w_merge': nrm(ks[16], (D_MODEL, 2 * D_MODEL)) * D_MODEL ** -0.5,
        'w_out': nrm(ks[17], (D_MODEL, D_MODEL)) * D_MODEL ** -0.5 * DN_BETA,
        'ln1_g': 1.0 + 0.02 * nrm(ks[18], (D_MODEL,)),
        'ln1_b': 0.02 * nrm(ks[19], (D_MODEL,)),
        'peer_wq': nrm(ks[20], (D_MODEL, P_HEADS * P_DKEY)) * D_MODEL ** -0.5,
        'peer_keys': nrm(ks[21], (P_HEADS, 2, P_NKEYS, P_DHALF)) * P_DHALF ** -0.5,
        'peer_u': nrm(ks[22], (P_EXPERTS, D_MODEL)) * D_MODEL ** -0.5,
        'peer_v': nrm(ks[23], (P_EXPERTS, D_MODEL)) * P_HEADS ** -0.5 * DN_BETA,
        'ln2_g': 1.0 + 0.02 * nrm(ks[24], (D_MODEL,)),
        'ln2_b': 0.02 * nrm(ks[25], (D_MODEL,)),
    }

def reference(x_prompt, x_sample, cache_cmp_kv, cache_slc_kv, cache_win_kv, state_C, state_n, state_m,
              page_table, w_in, b_in, norm_a_g, nsa_pe, nsa_w_cmp, w_br_a, w_br_b, w_merge, w_out,
              ln1_g, ln1_b, peer_wq, peer_keys, peer_u, peer_v, ln2_g, ln2_b):
    Bp, Tp, _ = x_prompt.shape
    dt = x_prompt.dtype
    C0 = jnp.zeros((Bp, A_HEADS, A_DQK, A_DV), jnp.float32)
    n0 = jnp.zeros((Bp, A_HEADS, A_DQK), jnp.float32)
    m0 = jnp.zeros((Bp, A_HEADS), jnp.float32)
    ya, yb, p_cmp, p_slc, p_win, p_C, p_n, p_m = token_mixers(
        x_prompt, jnp.arange(Tp), C0, n0, m0, A_CHUNK, None, None, None,
        w_in, b_in, norm_a_g, nsa_pe, nsa_w_cmp)
    y_prompt = layer_tail(x_prompt, ya, yb, w_br_a, w_br_b, w_merge, w_out, ln1_g, ln1_b,
                          peer_wq, peer_keys, peer_u, peer_v, ln2_g, ln2_b)
    Bs, Ts, _ = x_sample.shape
    past_len = page_table.shape[1] * PAGE_SIZE
    past_cmp = cache_cmp_kv[page_table].reshape(Bs, past_len, 2, B_KV, B_HD)
    past_slc = cache_slc_kv[page_table].reshape(Bs, past_len, 2, B_KV, B_HD)
    ya_s, yb_s, s_cmp, s_slc, s_win, s_C, s_n, s_m = token_mixers(
        x_sample, past_len + jnp.arange(Ts), state_C, state_n, state_m, Ts, past_cmp, past_slc, cache_win_kv,
        w_in, b_in, norm_a_g, nsa_pe, nsa_w_cmp)
    y_sample = layer_tail(x_sample, ya_s, yb_s, w_br_a, w_br_b, w_merge, w_out, ln1_g, ln1_b,
                          peer_wq, peer_keys, peer_u, peer_v, ln2_g, ln2_b)
    sd = state_C.dtype
    return (y_prompt, y_sample, p_cmp, p_slc, p_win, p_C.astype(dt), p_n.astype(dt), p_m.astype(dt),
            s_cmp, s_slc, s_win, s_C.astype(sd), s_n.astype(sd), s_m.astype(sd))


_drawn_inputs = setup_inputs


def setup_inputs(seed=0):
    import zlib

    import numpy as np

    out = dict(_drawn_inputs(seed))
    spreads = {}
    factors = {'norm_a_g': 29.527, 'nsa_pe': 30.957, 'ln2_g': 8.155, 'ln2_b': 8.02, 'cache_slc_kv': 2.915}
    for name, (base, spread) in spreads.items():
        noise = np.random.default_rng([zlib.crc32(name.encode()), seed]).standard_normal(out[name].shape)
        drawn = base * np.exp(spread * noise) if base else spread * noise
        out[name] = __import__('jax').numpy.asarray(drawn.astype(out[name].dtype))
    for name, factor in factors.items():
        out[name] = (out[name] * factor).astype(out[name].dtype)
    return out
```

```python
from contextlib import ExitStack

import numpy as np

import concourse.bass as bass
from concourse import mybir

ALU = mybir.AluOpType
ACT = mybir.ActivationFunctionType
AX = mybir.AxisListType
F32 = mybir.dt.float32
F32R = mybir.dt.float32r
I32 = mybir.dt.int32
U32 = mybir.dt.uint32

P = 128
D = 1024
DC = D // P
TP = 512
DB, DS = 8, 4
TS = DB * DS
T = TP + TS
NT = 5
ROWS = [P] * 4 + [TS]
HALF = T // 2
PAST = 256
PAGE = 128
NPG = PAST // PAGE

AH, DQK, DV = 4, 128, 256
BH, KV, REP, HD = 16, 4, 4, 64
CB = 64
PH, PK, TOPK = 8, 128, 16
DN_ALPHA = 2.0 ** 0.25
LN_EPS = 1e-5
BIG = 1e34

SLOPES = [2.0 ** (-8.0 * (h + 1) / BH) for h in range(BH)]

SB0 = 16512


class Names:
    pass


class Count:

    def __init__(self):
        self.n = 0

    def add(self, k=1):
        self.n += k
        return self.n


def chunks(total, size):
    return [(a, min(size, total - a)) for a in range(0, total, size)]


class Semaphores:

    def __init__(self, nc):
        self.nc, self.made = nc, []

    def __call__(self, name):
        self.made.append(self.nc.alloc_semaphore(name))
        return self.made[-1]

    def clear(self):
        self.nc.clear_and_free_semaphores(self.made)
        self.nc.all_engine_barrier()


def place(nc):

    def at(name, off, shape, dt=F32):
        return nc.alloc_sbuf_tensor_at(name, shape, dt, offset=SB0 + 4 * off)

    s = Names()
    s.at = at
    s.ident = at("ident", 0, [P, P])
    s.ones = at("ones", 128, [P, P])
    s.upper = at("upper", 256, [P, P])
    s.pairs = at("pairs", 384, [TS, TS])
    s.member = at("member", 416, [TS, DB])
    s.head_row = at("head_row", 424, [AH, AH, P])
    s.xT = at("xT", 1280, [P, DC, T])
    s.bqT = at("bqT", 5632, [HD, BH, T])
    s.kslT = at("kslT", 14336, [HD, KV, T])
    s.kwiT = at("kwiT", 16512, [HD, KV, T])
    s.cmpT = at("cmpT", 18688, [HD, 2, 33, CB])
    s.vsl = at("vsl", 22912, [P, NT, KV * HD])
    s.vwi = at("vwi", 24192, [P, NT, KV * HD])
    s.gat = at("gat", 25472, [P, NT, 48])
    s.qT = at("qT", 25728, [P, AH, T])
    s.kT = at("kT", 27904, [P, AH, T])
    s.kn = at("kn", 30080, [P, NT, AH * DQK])
    s.vn = at("vn", 32640, [P, NT, AH, DV + 1])
    s.ifn = at("ifn", 37784, [P, NT, 8])
    s.on = at("on", 37848, [P, NT, AH * DV])
    s.yaT = at("yaT", 32640, [P, DC, T])
    s.free = 42968
    return s


def stage_load(nc, s, io):
    at = s.at
    xn = at("xn", 5632, [P, NT, D])
    sem = Semaphores(nc)
    with ExitStack() as ctx:
        x_in = [sem(f"x_in{i}") for i in range(NT)]
        const_step = sem("const_step")
        ident_ready = sem("ident_ready")
        xt_psum = sem("xt_psum")
        xt_even = sem("xt_even")
        xt_odd = sem("xt_odd")
        ps = ctx.enter_context(nc.psum_tensor("ps_x", [P, 8, 512], F32))
        block = ctx.enter_context(nc.Block())

        @block.sync
        def _(sp):
            for i in range(4):
                sp.dma_start(xn[:, i, :], io.x_prompt[0, i * P:(i + 1) * P, :]).then_inc(x_in[i], 16)
            sp.dma_start(xn[0:TS, 4, :], io.x_sample.rearrange("b t d -> (b t) d")).then_inc(x_in[4], 16)

        @block.gpsimd
        def _(pool):
            step = Count()

            def link(ins):
                ins.then_inc(const_step, 1)
                pool.wait_ge(const_step, step.add())

            pool.memset(s.ones[:, :], 1.0)
            link(pool.memset(s.ident[:, :], 0.0))
            pool.affine_select(out=s.ident[:, :], in_=s.ident[:, :], compare_op=ALU.not_equal, fill=1.0, base=0,
                               pattern=[[-1, P]], channel_multiplier=1).then_inc(ident_ready, 1)
            link(pool.affine_select(out=s.upper[:, :], in_=s.ones[:, :], compare_op=ALU.is_ge, fill=0.0, base=0,
                                    pattern=[[1, P]], channel_multiplier=-1))
            pr = s.pairs[:, :].rearrange("s (b t) -> s b t", b=DB)
            link(pool.affine_select(out=pr, in_=s.ones[0:TS, 0:TS].rearrange("s (b t) -> s b t", b=DB),
                                    compare_op=ALU.is_ge, fill=0.0, base=0,
                                    pattern=[[-DS, DB], [0, DS]], channel_multiplier=1))
            link(pool.affine_select(out=pr, in_=pr, compare_op=ALU.is_ge, fill=0.0, base=0,
                                    pattern=[[DS, DB], [1, DS]], channel_multiplier=-1))
            link(pool.affine_select(out=s.member[:, :], in_=s.ones[0:TS, 0:DB], compare_op=ALU.is_ge, fill=0.0,
                                    base=0, pattern=[[-DS, DB]], channel_multiplier=1))
            link(pool.affine_select(out=s.member[:, :], in_=s.member[:, :], compare_op=ALU.is_ge, fill=0.0,
                                    base=DS - 1, pattern=[[DS, DB]], channel_multiplier=-1))
            for h in range(AH):
                link(pool.affine_select(out=s.head_row[:, h, :], in_=s.ones[0:AH, :], compare_op=ALU.is_equal,
                                        fill=0.0, base=-h, pattern=[[0, P]], channel_multiplier=1))

        @block.tensor
        def _(pe):
            pe.wait_ge(ident_ready, 1)
            for n in range(2 * NT):
                i, rows = n // 2, ROWS[n // 2]
                if n % 2 == 0:
                    pe.wait_ge(x_in[i], 16)
                if n >= 8:
                    pe.wait_ge([xt_even, xt_odd][n % 2], (n - 8) // 2 + 1)
                for c in range(4):
                    dc = 4 * (n % 2) + c
                    last = pe.transpose(ps[:, n % 8, c * P:c * P + rows], xn[0:rows, i, dc * P:(dc + 1) * P],
                                        s.ident[0:rows, 0:rows])
                last.then_inc(xt_psum, 1)

        def evacuate(eng, copy, parity, done):
            for n in range(parity, 2 * NT, 2):
                i, rows = n // 2, ROWS[n // 2]
                eng.wait_ge(xt_psum, n + 1)
                src = ps[:, n % 8, :].rearrange("p (c t) -> p c t", c=4)[:, :, 0:rows]
                copy(s.xT[:, 4 * parity:4 * parity + 4, i * P:i * P + rows], src).then_inc(done, 1)

        @block.vector
        def _(dve):
            evacuate(dve, dve.tensor_copy, 0, xt_even)

        @block.scalar
        def _(act):
            evacuate(act, act.copy, 1, xt_odd)
    sem.clear()


COLS = ([("q", 0, 512), ("k", 512, 512), ("v", 1024, 512), ("v", 1536, 512), ("if", 2048, 8),
         ("o", 2056, 512), ("o", 2568, 512), ("bq", 3080, 512), ("bq", 3592, 512),
         ("cmp", 4104, 512), ("slc", 4616, 512), ("win", 5128, 512), ("gate", 5640, 48)])
NCB = len(COLS)
TURNS = {"q": 1, "k": 1, "bq": 2, "cmp": 2, "slc": 1, "win": 1}
STAGED = {"q", "bq", "cmp", "slc", "win"}
OUTPUT = {"cmp", "slc", "win"}


def stage_project(nc, s, io):
    at = s.at
    wr = at("w_ring", s.free, [P, 4, 4, 512])
    stage = at("stage", s.free + 8192, [P, 2, 512])
    bias = at("bias", s.free + 9216, [P, 2, 512])
    groups = [(b, t) for b in range(NCB) for t in range(NT)]
    turn_at, staged_at, out_at = {}, {}, {}
    nturn = nst = nout = 0
    for b, t in groups:
        name = COLS[b][0]
        turn_at[b, t] = nturn
        staged_at[b, t] = nst
        out_at[b, t] = nout
        if name in TURNS and not (name == "cmp" and t == 4):
            nturn += TURNS[name]
        if name in STAGED:
            nst += 1
        if name in OUTPUT:
            nout += 1
    staged = [(b, t) for b, t in groups if COLS[b][0] in STAGED]

    def turns(b, t):
        name = COLS[b][0]
        return 0 if name == "cmp" and t == 4 else TURNS.get(name, 0)

    sem = Semaphores(nc)
    with ExitStack() as ctx:
        w_in = [sem(f"w_in{i}") for i in range(4)]
        b_in = [sem(f"bias_in{i}") for i in range(2)]
        proj_psum = sem("proj_psum")
        proj_done = sem("proj_done")
        turn_psum = sem("turn_psum")
        turn_done = sem("turn_done")
        rows_out = [sem(f"rows_out{i}") for i in range(2)]
        ones_set = sem("ones_set")
        win_copy = sem("win_copy")
        gm = ctx.enter_context(nc.psum_tensor("ps_proj", [P, 4, 512], F32))
        tr = ctx.enter_context(nc.psum_tensor("ps_turn", [P, 4, 512], F32))
        block = ctx.enter_context(nc.Block())

        @block.sync
        def _(sp):
            for b, (_, c0, n) in enumerate(COLS):
                if b >= 2:
                    sp.wait_ge(proj_psum, NT * (b - 1))
                    sp.wait_ge(proj_done, NT * (b - 1))
                for half in range(2):
                    src = io.w_in[half * 512:(half + 1) * 512, c0:c0 + n].rearrange("(c p) n -> p c n", p=P)
                    sp.dma_start(wr[:, 2 * (b % 2) + half, :, 0:n], src).then_inc(w_in[2 * (b % 2) + half], 16)
                sp.dma_start(bias[:, b % 2, 0:n], io.b_in[c0:c0 + n].partition_broadcast(P)).then_inc(b_in[b % 2], 16)

        @block.tensor
        def _(pe):
            def turn(b, t):
                name, rows = COLS[b][0], ROWS[t]
                if not turns(b, t):
                    return
                pe.wait_ge(proj_done, NT * b + t + 1)
                src = s.kn[:, t, :] if name == "k" else stage[:, staged_at[b, t] % 2, :]
                width = P if name in ("q", "k") else HD
                for i in range(turns(b, t)):
                    r = turn_at[b, t] + i
                    if r >= 4:
                        pe.wait_ge(turn_done, r - 3)
                    for c in range(4):
                        last = pe.transpose(tr[0:width, r % 4, c * P:c * P + rows],
                                            src[0:rows, (4 * i + c) * width:(4 * i + c + 1) * width],
                                            s.ident[0:rows, 0:rows])
                    last.then_inc(turn_psum, 1)

            before = None
            for g, (b, t) in enumerate(groups):
                n, rows = COLS[b][2], ROWS[t]
                if g >= 4:
                    pe.wait_ge(proj_done, g - 3)
                for dc in range(DC):
                    if t == 0 and dc % 4 == 0:
                        pe.wait_ge(w_in[2 * (b % 2) + dc // 4], 16 * (b // 2 + 1))
                    last = pe.matmul(gm[0:rows, g % 4, 0:n], s.xT[:, dc, t * P:t * P + rows],
                                     wr[:, 2 * (b % 2) + dc // 4, dc % 4, 0:n], start=(dc == 0), stop=(dc == DC - 1))
                last.then_inc(proj_psum, 1)
                if before:
                    turn(*before)
                before = (b, t)

        @block.vector
        def _(dve):
            dve.memset(s.vn[:, :, :, DV:DV + 1], 1.0).then_inc(ones_set, 1)
            dve.memset(s.ifn[:, :, :], 0.0).then_inc(ones_set, 1)
            dve.wait_ge(ones_set, 2)
            for g, (b, t) in enumerate(groups):
                name, _, n = COLS[b]
                rows = ROWS[t]
                if t == 0:
                    dve.wait_ge(b_in[b % 2], 16 * (b // 2 + 1))
                dve.wait_ge(proj_psum, g + 1)
                slot = staged_at[b, t] % 2
                if name in STAGED and staged_at[b, t] >= 2:
                    pb, pt = staged[staged_at[b, t] - 2]
                    if turns(pb, pt):
                        dve.wait_ge(turn_psum, turn_at[pb, pt] + turns(pb, pt))
                    if COLS[pb][0] in OUTPUT:
                        dve.wait_ge(rows_out[slot], 16 * (out_at[pb, pt] // 2 + 1))
                src = gm[0:rows, g % 4, 0:n]
                add = bias[0:rows, b % 2, 0:n]
                if name in STAGED:
                    dst = stage[0:rows, slot, :]
                elif name == "k":
                    dst = s.kn[0:rows, t, :]
                elif name == "v":
                    h0 = 2 * (b - 2)
                    dst = s.vn[0:rows, t, h0:h0 + 2, 0:DV]
                    src = src.rearrange("p (h d) -> p h d", h=2)
                    add = add.rearrange("p (h d) -> p h d", h=2)
                elif name == "if":
                    dst = s.ifn[0:rows, t, :]
                elif name == "o":
                    dst = s.on[0:rows, t, 512 * (b - 5):512 * (b - 4)]
                else:
                    dst = s.gat[0:rows, t, :]
                if name in ("slc", "win"):
                    v = s.vsl if name == "slc" else s.vwi
                    dve.tensor_tensor(v[0:rows, t, :], src[:, 256:512], add[:, 256:512], ALU.add)
                dve.tensor_tensor(dst, src, add, ALU.add).then_inc(proj_done, 1)

        @block.scalar
        def _(act):
            scale = {"q": 1.0, "k": DQK ** -0.5, "bq": HD ** -0.5}
            for b, t in groups:
                name, rows = COLS[b][0], ROWS[t]
                for i in range(turns(b, t)):
                    r = turn_at[b, t] + i
                    act.wait_ge(turn_psum, r + 1)
                    width = P if name in ("q", "k") else HD
                    src = tr[0:width, r % 4, :].rearrange("p (c t) -> p c t", c=4)[:, :, 0:rows]
                    tok = slice(t * P, t * P + rows)
                    if name == "cmp":
                        view = s.cmpT[:, i, 0:32, :].rearrange("p (g n) l -> p g (n l)", g=KV)
                        act.copy(view[:, :, tok], src).then_inc(turn_done, 1)
                        continue
                    dst = {"q": s.qT, "k": s.kT, "slc": s.kslT, "win": s.kwiT}.get(name)
                    dst = s.bqT[:, 8 * (b - 7) + 4 * i:8 * (b - 7) + 4 * i + 4, tok] if name == "bq" else dst[:, :, tok]
                    act.mul(dst, src, scale.get(name, 1.0)).then_inc(turn_done, 1)

        @block.gpsimd
        def _(pool):
            prompt = {"cmp": [io.p_cmp], "slc": [io.p_slc], "win": [io.p_win]}
            sample = {"cmp": io.s_cmp, "slc": io.s_slc}
            for b in range(DB):
                pool.dma_start(io.s_win[b, 0:PAST - DS].rearrange("t a g d -> t (a g d)"),
                               io.cache_win_kv[b, DS:PAST].rearrange("t a g d -> t (a g d)")).then_inc(win_copy, 16)
            sent = [0, 0]
            for b, t in groups:
                name = COLS[b][0]
                if name not in OUTPUT:
                    continue
                slot = staged_at[b, t] % 2
                pool.wait_ge(proj_done, NT * b + t + 1)
                if t < 4:
                    out = prompt[name][0][0, t * P:(t + 1) * P].rearrange("t a g d -> t (a g d)")
                elif name == "win":
                    out = io.s_win[:, PAST - DS:PAST].rearrange("b t a g d -> b t (a g d)")
                else:
                    out = sample[name].rearrange("b t a g d -> (b t) (a g d)")
                pool.dma_start(out, stage[0:ROWS[t], slot, :]).then_inc(rows_out[slot], 16)
                sent[slot] += 1
            for slot in range(2):
                pool.wait_ge(rows_out[slot], 16 * sent[slot])
            pool.wait_ge(win_copy, 16 * DB)
    sem.clear()


def stage_mlstm(nc, s, io):
    at, r4 = s.at, s.free
    c0 = at("c0", r4, [P, 2, DB, DV + 1])
    ew = at("ew", r4 + 4128, [P, 1280])
    offs, widths = [0, 512, 896, 1152], [512, 384, 256, 128]
    ews = at("ews", r4 + 5408, [TS, TS])
    kw = at("kw", r4 + 5440, [P, 4, DQK])
    kws = at("kws", r4 + 5952, [TS, DQK])
    kwb = at("kwb", r4 + 6080, [TS, DB, DQK])
    qb = at("qb", r4 + 7104, [P, DB * 36])
    gn = at("gn", r4 + 7392, [P, AH * DV])
    mrow = at("mrow", r4 + 8416, [AH, T])
    brow = at("brow", r4 + 8960, [AH, T])
    ping = at("ping", r4 + 4128, [AH, T])
    pong = at("pong", r4 + 4672, [AH, T])
    irow = at("irow", r4 + 5216, [AH, T])
    small = [r4 + 9504]

    def tiny(name, shape):
        off, size = small[0], int(np.prod(shape[1:]))
        small[0] += -(-size // 8) * 8
        return at(name, off, shape)

    lf = tiny("lf", [P, NT, AH])
    t1 = tiny("gt1", [P, NT, AH])
    t2 = tiny("gt2", [P, NT, AH])
    an = tiny("an", [P, NT, AH])
    en = tiny("en", [P, NT, AH])
    wt = tiny("wt", [P, 4])
    wsi = tiny("wsi", [TS, 2, AH])
    ab = tiny("ab", [P, AH, DB])
    n0T = tiny("n0T", [P, DB, AH])
    nout = tiny("nout", [P, DB, AH])
    pn = tiny("pn", [P, AH])
    mv = tiny("mv", [P, AH, NT, 2])
    st6 = tiny("st6", [P, 6])
    rstd = tiny("rstd", [P, AH, NT])
    dd = tiny("dd", [P, 4])
    m0 = tiny("m0", [AH, DB])
    mt = tiny("mt", [AH, DB])
    srow = tiny("srow", [AH, 2, TS])
    abr = tiny("abr", [AH, DB])
    mT = tiny("mT", [P, 1])
    wsl = tiny("wsl", [TS, AH])
    n0 = at("n0", 1000, [DB * AH, DQK])
    nrow = at("nrow", 1128, [DB * AH, DQK])
    nds = at("nds", r4 + 9976, [TS, DV + 1])
    pnrow = at("pnrow", r4 + 4128, [AH, DQK])

    sem = Semaphores(nc)
    with ExitStack() as ctx:
        v = Names()
        v.gate_ready = sem("gate_ready")
        v.lf_ready = sem("lf_ready")
        v.rows_psum = sem("rows_psum")
        v.b_psum = sem("b_psum")
        v.m_ready = sem("m_ready")
        v.cols_psum = sem("cols_psum")
        v.cols_read = sem("cols_read")
        v.m_bcast = sem("m_bcast")
        v.dist_ready = sem("dist_ready")
        v.weight_ready = sem("weight_ready")
        v.wt_in = sem("wt_in")
        v.wt_ready = sem("wt_ready")
        v.scores = sem("scores")
        v.p_ready = sem("p_ready")
        v.kw_ready = sem("kw_ready")
        v.c_psum = sem("c_psum")
        v.out_psum = sem("out_psum")
        v.out_used = sem("out_used")
        v.upd_psum = sem("upd_psum")
        v.upd_used = sem("upd_used")
        v.c_new = sem("c_new")
        v.n_turned = sem("n_turned")
        v.chain = sem("chain")
        v.stat_done = sem("stat_done")
        v.sqrt_done = sem("sqrt_done")
        v.sig_ready = sem("sig_ready")
        v.norm_done = sem("norm_done")
        v.y_psum = sem("y_psum")
        v.y_even = sem("y_even")
        v.y_odd = sem("y_odd")
        v.n_copied = sem("n_copied")
        v.c_out = sem("c_out")
        v.act_chain = sem("act_chain")
        v.gn_in = sem("gn_in")
        v.m0_in = sem("m0_in")
        v.n0_in = sem("n0_in")
        v.small_out = sem("small_out")
        v.pc_ready = sem("pc_ready")
        v.mrow_done = sem("mrow_done")
        c_in = [sem(f"c_in{i}") for i in range(2)]
        c_sent = [sem(f"c_sent{i}") for i in range(2)]
        ps = ctx.enter_context(nc.psum_tensor("ps_m", [P, 8, 512], F32))
        block = ctx.enter_context(nc.Block())
        score_at = [(2, 0), (3, 0), (4, 0), (4, 256)]

        @block.sync
        def _(sp):
            sp.dma_start(m0[:, :], io.state_m.rearrange("b h -> h b"), allow_slow_non_contiguous=True).then_inc(v.m0_in, 16)
            sp.dma_start(n0[:, :], io.state_n.rearrange("b h d -> (b h) d")).then_inc(v.n0_in, 16)
            sp.dma_start(gn[:, :], io.norm_a_g.partition_broadcast(P)).then_inc(v.gn_in, 16)
            for h in range(AH):
                if h >= 2:
                    sp.wait_ge(c_sent[h % 2], 16 * (h // 2))
                sp.dma_start(c0[:, h % 2, :, 0:DV], io.state_C[:, h].rearrange("b p v -> p b v")).then_inc(c_in[h % 2], 16)

        @block.gpsimd
        def _(pool):
            pool.wait_ge(v.m_ready, 1)
            pool.dma_start(io.p_m.rearrange("a h -> h a"), brow[:, TP - 1:TP], allow_slow_non_contiguous=True).then_inc(v.small_out, 16)
            pool.dma_start(io.s_m.rearrange("b h -> h b"),
                           brow[:, TP:T].rearrange("h (b t) -> h b t", b=DB)[:, :, DS - 1],
                           allow_slow_non_contiguous=True).then_inc(v.small_out, 16)
            for h in range(AH):
                pool.wait_ge(v.pc_ready, h + 1)
                pool.dma_start(io.p_C[0, h].rearrange("p (a b) -> p a b", a=4), s.kn[:, 0:4, h * DQK:h * DQK + 64]).then_inc(v.c_out, 16)
                pool.wait_ge(v.c_new, h + 1)
                pool.dma_start(io.s_C[:, h].rearrange("b p v -> p b v"), c0[:, h % 2, :, 0:DV]).then_inc(c_sent[h % 2], 16)
            pool.wait_ge(v.n_copied, 1)
            pool.dma_start(io.s_n.rearrange("b h d -> (b h) d"), nrow[:, :]).then_inc(v.small_out, 16)
            pool.dma_start(io.p_n[0], pnrow[:, :]).then_inc(v.small_out, 16)
            pool.wait_ge(v.small_out, 64)
            pool.wait_ge(v.c_out, 16 * AH)
            for i in range(2):
                pool.wait_ge(c_sent[i], 32)

        @block.tensor
        def _(pe):
            for j in range(NT):
                r = ROWS[j]
                dst = ps[0:AH, 0, j * P:j * P + r] if j < 4 else ps[0:AH, 2, 0:TS]
                last = pe.transpose(dst, s.ifn[0:r, j, 0:AH], s.ident[0:r, 0:r])
            last.then_inc(v.rows_psum, 1)
            pe.wait_ge(v.lf_ready, 1)
            for j in range(4):
                for i in range(j + 1):
                    mask = s.upper if i == j else s.ones
                    pe.matmul(ps[0:AH, 1, j * P:(j + 1) * P], lf[:, i, :], mask[:, :], start=(i == 0), stop=(i == j))
            pe.matmul(ps[0:AH, 2, TS:2 * TS], lf[0:TS, 4, :], s.pairs[:, :], start=True, stop=True)
            for j in range(4):
                for i in range(j + 1):
                    mask = s.upper if i == j else s.ones
                    pe.matmul(ps[:, 3, 4 * j:4 * j + 4], mask[:, :], lf[:, i, :], start=(i == 0), stop=(i == j))
            pe.matmul(ps[0:TS, 3, 16:20], s.pairs[:, :], lf[0:TS, 4, :], start=True, stop=True).then_inc(v.b_psum, 1)
            pe.wait_ge(v.m_ready, 1)
            for j in range(NT):
                r = ROWS[j]
                pe.transpose(ps[0:r, 4, 4 * j:4 * j + 4], brow[:, j * P:j * P + r], s.ident[0:AH, 0:AH])
            for i in range(2):
                pe.transpose(ps[0:TS, 4, 20 + 4 * i:24 + 4 * i], srow[:, i, :], s.ident[0:AH, 0:AH])
            for h in range(AH):
                pe.matmul(ps[:, 5, h * DB:(h + 1) * DB], s.head_row[:, h, :], abr[:, :], start=True, stop=True)
            pe.wait_ge(v.n0_in, 16)
            pe.transpose(ps[:, 5, TS:2 * TS], n0[:, :], s.ident[0:TS, 0:TS]).then_inc(v.cols_psum, 1)
            pe.wait_ge(v.cols_read, 1)
            out = 0
            for h in range(AH):
                if h:
                    pe.wait_ge(v.upd_used, DB * h)
                pe.matmul(ps[:, 0, :], s.head_row[:, h, :], mrow[:, 0:TP], start=True, stop=True)
                pe.matmul(ps[0:TS, 1, 0:TS], s.head_row[:, h, 0:TS], mrow[:, TP:T], start=True, stop=True)\
                  .then_inc(v.m_bcast, 1)
                if h:
                    pe.wait_ge(v.p_ready, h)
                for i in range(4):
                    bank, o = score_at[i]
                    pe.matmul(ps[:, bank, o:o + widths[i]], s.kT[:, h, i * P:(i + 1) * P], s.qT[:, h, i * P:TP],
                              start=True, stop=True)
                pe.matmul(ps[0:TS, 4, 384:384 + TS], s.kT[:, h, TP:T], s.qT[:, h, TP:T], start=True, stop=True)\
                  .then_inc(v.scores, 1)
                pe.wait_ge(v.kw_ready, h + 1)
                if h:
                    pe.wait_ge(v.pc_ready, h)
                for i in range(4):
                    last = pe.matmul(ps[:, 5, 0:DV + 1], kw[:, i, :], s.vn[:, i, h, :], start=(i == 0), stop=(i == 3))
                last.then_inc(v.c_psum, 1)
                pe.wait_ge(v.p_ready, h + 1)
                for j in (3, 2, 1, 0):
                    if out >= 2:
                        pe.wait_ge(v.out_used, out - 1)
                    for i in range(j + 1):
                        last = pe.matmul(ps[:, 6 + out % 2, 0:DV + 1], ew[:, offs[i] + (j - i) * P:offs[i] + (j - i + 1) * P],
                                         s.vn[:, i, h, :], start=(i == 0), stop=(i == j))
                    last.then_inc(v.out_psum, 1)
                    out += 1
                pe.wait_ge(v.out_used, out - 1)
                pe.matmul(ps[0:TS, 6, 0:DV + 1], ews[:, :], s.vn[0:TS, 4, h, :], start=True, stop=True)\
                  .then_inc(v.out_psum, 1)
                pe.wait_ge(c_in[h % 2], 16 * (h // 2 + 1))
                pe.wait_ge(v.out_used, out)
                for b in range(DB):
                    last = pe.matmul(ps[0:TS, 7, 0:DV + 1], qb[:, b * TS:(b + 1) * TS], c0[:, h % 2, b, :],
                                     start=(b == 0), stop=(b == DB - 1))
                last.then_inc(v.out_psum, 1)
                out += 2
                for b in range(DB):
                    u = DB * h + b
                    if b >= 2:
                        pe.wait_ge(v.upd_used, u - 1)
                    pe.matmul(ps[:, b % 2, 0:DV + 1], kwb[:, b, :], s.vn[0:TS, 4, h, :], start=True, stop=True)\
                      .then_inc(v.upd_psum, 1)
            pe.wait_ge(v.stat_done, 1)
            pe.transpose(ps[0:TS, 5, 0:DQK], nout[:, :, :].rearrange("p b h -> p (b h)"), s.ident[:, :])
            pe.transpose(ps[0:AH, 4, 0:DQK], pn[:, :], s.ident[:, :]).then_inc(v.n_turned, 1)
            pe.wait_ge(v.norm_done, 1)
            for n in range(2 * NT):
                i, rows = n // 2, ROWS[n // 2]
                if n >= 4:
                    pe.wait_ge([v.y_even, v.y_odd][n % 2], (n - 4) // 2 + 1)
                for c in range(4):
                    fc = 4 * (n % 2) + c
                    last = pe.transpose(ps[:, n % 4, c * P:c * P + rows], s.on[0:rows, i, fc * P:(fc + 1) * P],
                                        s.ident[0:rows, 0:rows])
                last.then_inc(v.y_psum, 1)

        def y_out(eng, copy, parity, done):
            for n in range(parity, 2 * NT, 2):
                i, rows = n // 2, ROWS[n // 2]
                eng.wait_ge(v.y_psum, n + 1)
                src = ps[:, n % 4, :].rearrange("p (c t) -> p c t", c=4)[:, :, 0:rows]
                copy(s.yaT[:, 4 * parity:4 * parity + 4, i * P:i * P + rows], src).then_inc(done, 1)

        @block.vector
        def _(dve):
            step = Count()

            def link(ins):
                ins.then_inc(v.chain, 1)
                dve.wait_ge(v.chain, step.add())

            f = s.ifn[:, :, AH:2 * AH]
            link(dve.tensor_scalar(t1[:, :, :], f, -1.0, None, ALU.mult))
            link(dve.tensor_tensor(t1[:, :, :], t1[:, :, :], f, ALU.max))
            dve.tensor_scalar(t2[:, :, :], f, 0.0, None, ALU.min).then_inc(v.gate_ready, 1)
            dve.memset(qb[:, :], 0.0)
            dve.wait_ge(v.act_chain, 2)
            dve.tensor_tensor(lf[:, :, :], t2[:, :, :], lf[:, :, :], ALU.subtract).then_inc(v.lf_ready, 1)
            dve.wait_ge(v.rows_psum, 1)
            dve.wait_ge(v.b_psum, 1)
            dve.tensor_copy(brow[:, 0:TP], ps[0:AH, 1, :])
            link(dve.tensor_copy(brow[:, TP:T], ps[0:AH, 2, TS:2 * TS]))
            dve.tensor_tensor(ping[:, 0:TP], ps[0:AH, 0, :], brow[:, 0:TP], ALU.subtract)
            dve.tensor_tensor(ping[:, TP:T], ps[0:AH, 2, 0:TS], brow[:, TP:T], ALU.subtract)
            dve.tensor_tensor(an[:, 0:4, :], s.ifn[:, 0:4, 0:AH], ps[:, 3, 0:16].rearrange("p (j h) -> p j h", j=4),
                              ALU.subtract)
            link(dve.tensor_tensor(an[0:TS, 4, :], s.ifn[0:TS, 4, 0:AH], ps[0:TS, 3, 16:20], ALU.subtract))
            a, b = ping, pong
            w = 1
            while w < TP:
                dve.tensor_tensor(b[:, w:TP], a[:, w:TP], a[:, 0:TP - w], ALU.max)
                if w < DS:
                    sa = a[:, TP:T].rearrange("h (b t) -> h b t", b=DB)
                    sb = b[:, TP:T].rearrange("h (b t) -> h b t", b=DB)
                    dve.tensor_tensor(sb[:, :, w:DS], sa[:, :, w:DS], sa[:, :, 0:DS - w], ALU.max)
                    dve.tensor_copy(sb[:, :, 0:w], sa[:, :, 0:w])
                elif w == DS:
                    dve.tensor_copy(irow[:, TP:T], a[:, TP:T])
                link(dve.tensor_copy(b[:, 0:w], a[:, 0:w]))
                a, b = b, a
                w *= 2
            dve.tensor_scalar(mrow[:, 0:TP], a[:, 0:TP], 0.0, None, ALU.max)
            dve.wait_ge(v.m0_in, 16)
            ms = mrow[:, TP:T].rearrange("h (b t) -> h b t", b=DB)
            m0b = m0[:, :].unsqueeze(2).broadcast_to([AH, DB, DS])
            link(dve.tensor_tensor(ms, irow[:, TP:T].rearrange("h (b t) -> h b t", b=DB), m0b, ALU.max))
            link(dve.tensor_tensor(brow[:, :], brow[:, :], mrow[:, :], ALU.add))
            mtb = ms[:, :, DS - 1:DS].broadcast_to([AH, DB, DS])
            dve.tensor_copy(srow[:, 0, :].rearrange("h (b t) -> h b t", b=DB), mtb)
            dve.tensor_tensor(srow[:, 1, :].rearrange("h (b t) -> h b t", b=DB), m0b, ms, ALU.subtract)
            dve.tensor_tensor(abr[:, :], m0[:, :], ms[:, :, DS - 1], ALU.subtract).then_inc(v.m_ready, 1)
            dve.wait_ge(v.cols_psum, 1)
            dve.tensor_tensor(wsl[:, :], an[0:TS, 4, :], ps[0:TS, 4, 20:24], ALU.subtract)
            dve.tensor_copy(n0T[:, :, :].rearrange("p b h -> p (b h)"), ps[:, 5, TS:2 * TS]).then_inc(v.mrow_done, 1)
            dve.wait_ge(v.mrow_done, 1)
            out = 0
            for h in range(AH):
                dve.wait_ge(v.m_bcast, h + 1)
                if h:
                    dve.wait_ge(v.out_psum, 6 * h)
                    dve.wait_ge(v.upd_psum, DB * h)
                for i in range(4):
                    dve.tensor_scalar(ew[:, offs[i]:offs[i] + widths[i]], ps[:, 0, i * P:TP], an[:, i, h:h + 1], 0.0,
                                      ALU.subtract, ALU.max).then_inc(v.dist_ready, 1)
                dve.tensor_scalar(ews[:, :], ps[0:TS, 1, 0:TS], an[0:TS, 4, h:h + 1], 0.0, ALU.subtract, ALU.max)\
                   .then_inc(v.dist_ready, 1)
                link(dve.tensor_copy(mT[:, :], ps[:, 0, TP - 1:TP]))
                dve.tensor_scalar(wt[:, :], an[:, 0:4, h], mT[:, 0:1], None, ALU.subtract).then_inc(v.wt_in, 1)
                dve.wait_ge(v.wt_ready, h + 1)
                for i in range(4):
                    dve.tensor_scalar(kw[:, i, :], s.kn[:, i, h * DQK:(h + 1) * DQK], wt[:, i:i + 1], DQK ** -0.5,
                                      ALU.mult, ALU.mult)
                dve.tensor_copy(qb[:, :].rearrange("p (b x) -> p b x", b=DB)[:, :, 0:DS],
                                s.qT[:, h, TP:T].rearrange("p (b t) -> p b t", b=DB))
                link(dve.tensor_scalar(kws[:, :], s.kn[0:TS, 4, h * DQK:(h + 1) * DQK], wsi[:, 0, h:h + 1], DQK ** -0.5,
                                       ALU.mult, ALU.mult))
                dve.tensor_tensor(kwb[:, :, :], kws[:, :].unsqueeze(1).broadcast_to([TS, DB, DQK]),
                                  s.member[:, :].unsqueeze(2).broadcast_to([TS, DB, DQK]), ALU.mult)
                dve.wait_ge(c_in[h % 2], 16 * (h // 2 + 1))
                dve.tensor_copy(c0[:, h % 2, :, DV:DV + 1], n0T[:, :, h:h + 1]).then_inc(v.kw_ready, 1)
                dve.wait_ge(v.scores, h + 1)
                dve.wait_ge(v.weight_ready, 5 * h + 5)
                for i in range(4):
                    dve.tensor_tensor(ew[:, offs[i]:offs[i] + P], ew[:, offs[i]:offs[i] + P], s.upper[:, :], ALU.mult)
                link(dve.tensor_tensor(ews[:, :], ews[:, :], s.pairs[:, :], ALU.mult))
                for i in range(4):
                    bank, o = score_at[i]
                    dst = ew[:, offs[i]:offs[i] + widths[i]]
                    dve.tensor_tensor(dst, ps[:, bank, o:o + widths[i]], dst, ALU.mult)
                dve.tensor_tensor(ews[:, :], ps[0:TS, 4, 384:384 + TS], ews[:, :], ALU.mult).then_inc(v.p_ready, 1)
                dve.wait_ge(v.c_psum, h + 1)
                dve.tensor_copy(pn[:, h:h + 1], ps[:, 5, DV:DV + 1])
                dve.tensor_copy(s.kn[:, 0:4, h * DQK:h * DQK + 64], ps[:, 5, 0:DV].rearrange("p (a b) -> p a b", a=4))\
                   .then_inc(v.pc_ready, 1)

                def normalise(num, j, rows):
                    den = num[:, DV:DV + 1]
                    link(dve.tensor_scalar(dd[0:rows, 0:1], den, -1.0, None, ALU.mult))
                    link(dve.scalar_tensor_tensor(out=dd[0:rows, 1:2], in0=dd[0:rows, 0:1], scalar=den,
                                                  in1=en[0:rows, j, h:h + 1], op0=ALU.max, op1=ALU.max))
                    link(dve.reciprocal(dd[0:rows, 2:3], dd[0:rows, 1:2]))
                    dst = s.vn[0:rows, j, h, 0:DV]
                    return dve.tensor_scalar(dst, num[:, 0:DV], dd[0:rows, 2:3], None, ALU.mult)

                def stats(j, rows):
                    link(dve.bn_stats(st6[0:rows, :], s.vn[0:rows, j, h, 0:DV]))
                    return dve.bn_aggr(mv[0:rows, h, j, :], st6[0:rows, :])

                for j in (3, 2, 1, 0):
                    dve.wait_ge(v.out_psum, out + 1)
                    normalise(ps[:, 6 + out % 2, 0:DV + 1], j, P).then_inc(v.out_used, 1)
                    out += 1
                    dve.wait_ge(v.out_used, out)
                    stats(j, P)
                dve.wait_ge(v.out_psum, out + 2)
                link(dve.tensor_scalar(nds[:, :], ps[0:TS, 7, 0:DV + 1], wsi[:, 1, h:h + 1], None, ALU.mult))
                link(dve.tensor_tensor(nds[:, :], ps[0:TS, 6, 0:DV + 1], nds[:, :], ALU.add))
                for b in range(DB):
                    dve.wait_ge(v.upd_psum, DB * h + b + 1)
                    dve.scalar_tensor_tensor(out=c0[:, h % 2, b, :], in0=c0[:, h % 2, b, :], scalar=ab[:, h, b:b + 1],
                                             in1=ps[:, b % 2, 0:DV + 1], op0=ALU.mult, op1=ALU.add)\
                       .then_inc(v.upd_used, 1)
                dve.wait_ge(v.upd_used, DB * (h + 1))
                dve.tensor_copy(nout[:, :, h:h + 1], c0[:, h % 2, :, DV:DV + 1]).then_inc(v.c_new, 1)
                normalise(nds[:, :], 4, TS).then_inc(v.out_used, 1)
                dve.wait_ge(v.out_used, out + 1)
                stats(4, TS).then_inc(v.out_used, 1)
                out += 2
            dve.wait_ge(v.c_new, AH)
            dve.wait_ge(v.out_used, out)
            link(dve.tensor_scalar(rstd[:, :, 0:4], mv[:, :, 0:4, 1], LN_EPS, None, ALU.add))
            dve.tensor_scalar(rstd[0:TS, :, 4], mv[0:TS, :, 4, 1], LN_EPS, None, ALU.add).then_inc(v.stat_done, 1)
            dve.wait_ge(v.sqrt_done, 1)
            dve.reciprocal(rstd[:, :, 0:4], rstd[:, :, 0:4])
            link(dve.reciprocal(rstd[0:TS, :, 4], rstd[0:TS, :, 4]))
            dve.wait_ge(v.gn_in, 16)
            dve.wait_ge(v.sig_ready, NT)
            for j in range(NT):
                r = ROWS[j]
                dve.tensor_tensor(s.on[0:r, j, :], s.on[0:r, j, :], gn[0:r, :], ALU.mult)
                for h in range(AH):
                    x = s.vn[0:r, j, h, 0:DV]
                    last = dve.tensor_scalar(x, x, mv[0:r, h, j, 0:1], rstd[0:r, h, j:j + 1], ALU.subtract, ALU.mult)
                link(last)
                last = dve.tensor_tensor(s.on[0:r, j, :].rearrange("p (h d) -> p h d", h=AH),
                                         s.on[0:r, j, :].rearrange("p (h d) -> p h d", h=AH), s.vn[0:r, j, :, 0:DV],
                                         ALU.mult)
            last.then_inc(v.norm_done, 1)
            dve.wait_ge(v.n_turned, 1)
            dve.tensor_copy(nrow[:, :], ps[0:TS, 5, 0:DQK])
            dve.tensor_copy(pnrow[:, :], ps[0:AH, 4, 0:DQK]).then_inc(v.n_copied, 1)
            y_out(dve, dve.tensor_copy, 0, v.y_even)

        @block.scalar
        def _(act):
            act.wait_ge(v.gate_ready, 1)
            act.activation(t1[:, :, :], t1[:, :, :], ACT.Exp, scale=-1.0).then_inc(v.act_chain, 1)
            act.wait_ge(v.act_chain, 1)
            act.activation(lf[:, :, :], t1[:, :, :], ACT.Ln, bias=1.0).then_inc(v.act_chain, 1)
            act.wait_ge(v.mrow_done, 1)
            act.activation(en[:, 0:4, :], ps[:, 4, 0:16].rearrange("p (j h) -> p j h", j=4), ACT.Exp, scale=-1.0)
            act.activation(en[0:TS, 4, :], ps[0:TS, 4, 16:20], ACT.Exp, scale=-1.0)
            act.activation(wsi[:, 1, :], ps[0:TS, 4, 24:28], ACT.Exp)
            act.activation(ab[:, :, :], ps[:, 5, 0:TS].rearrange("p (h b) -> p h b", h=AH), ACT.Exp)
            act.activation(wsi[:, 0, :], wsl[:, :], ACT.Exp).then_inc(v.cols_read, 1)
            for h in range(AH):
                for i in range(5):
                    act.wait_ge(v.dist_ready, 5 * h + i + 1)
                    x = ew[:, offs[i]:offs[i] + widths[i]] if i < 4 else ews[:, :]
                    act.activation(x, x, ACT.Exp, scale=-1.0).then_inc(v.weight_ready, 1)
                act.wait_ge(v.wt_in, h + 1)
                act.activation(wt[:, :], wt[:, :], ACT.Exp).then_inc(v.wt_ready, 1)
            for j in range(NT):
                r = ROWS[j]
                act.activation(s.on[0:r, j, :], s.on[0:r, j, :], ACT.Sigmoid).then_inc(v.sig_ready, 1)
            act.wait_ge(v.stat_done, 1)
            act.activation(rstd[:, :, 0:4], rstd[:, :, 0:4], ACT.Sqrt)
            act.activation(rstd[0:TS, :, 4], rstd[0:TS, :, 4], ACT.Sqrt).then_inc(v.sqrt_done, 1)
            y_out(act, act.copy, 1, v.y_odd)
    sem.clear()


def place_attention(s):
    at = s.at
    s.ybT = at("ybT", 25728, [P, DC, T])
    s.kcP = at("kcP", 30080, [HD, KV, 8])
    s.kcS = at("kcS", 30112, [HD, DB, KV, 4])
    s.vbd = at("vbd", 30240, [P, BH, HD])
    s.vcn = at("vcn", 31264, [8, 4, KV, HD])
    s.hm = at("hm", 32288, [P, BH])
    s.gden = at("gden", 32304, [P, NT, 48])
    s.att = 36992


def stage_compress(nc, s, io):
    place_attention(s)
    at, a0 = s.at, s.att
    xs = at("xs", a0, [HD, DB * KV * 4, CB])
    wc = at("wc", a0 + 8192, [HD, CB, HD])
    page = at("page", a0 + 12288, [P, 4, KV * HD])
    pes = at("pes", a0 + 13312, [CB, HD])
    vcT = at("vcT", a0 + 13376, [HD, KV, REP, 8])
    vsT = at("vsT", a0 + 13504, [HD, KV, DB, 4])
    pcol = at("pcol", a0 + 13632, [HD, 2])
    table = at("table_c", a0 + 13640, [1, DB * NPG], I32)
    slope_row = s.slope_row = at("slope_row", 936, [P, BH])
    sem = Semaphores(nc)
    with ExitStack() as ctx:
        page_in = [sem(f"page_in{i}") for i in range(4)]
        table_in, w_in, pe_in = sem("table_in"), sem("cmp_w_in"), sem("pos_in")
        page_psum, page_even, page_odd = sem("page_psum"), sem("page_even"), sem("page_odd")
        pos_psum, pos_done = sem("pos_psum"), sem("pos_done")
        sums, sums_read, v_psum, v_read, chain, masks = (sem("cmp_sums"), sem("cmp_read"), sem("vc_psum"),
                                                        sem("vc_read"), sem("cmp_chain"), sem("cmp_masks"))
        vrep_ready = sem("vrep_ready")
        ps = ctx.enter_context(nc.psum_tensor("ps_c", [P, 8, 512], F32))
        block = ctx.enter_context(nc.Block())
        NPAGES = DB * NPG

        @block.sync
        def _(sp):
            sp.dma_start(table[:, :], io.page_table.rearrange("b n -> (b n)").unsqueeze(0)).then_inc(table_in, 16)
            sp.wait_ge(table_in, 16)
            for kv in range(2):
                if kv:
                    sp.wait_ge(sums, 1)
                    sp.wait_ge(pos_psum, 1)
                sp.dma_start(pes[:, :], io.nsa_pe[kv]).then_inc(pe_in, 16)
                for i in range(NPAGES):
                    n = NPAGES * kv + i
                    pg = sp.value_load(table[0:1, i:i + 1], min_val=0, max_val=io.cache_cmp_kv.shape[0] - 1)
                    if n >= 4:
                        sp.wait_ge(page_psum, n - 3)
                    src = io.cache_cmp_kv[bass.ds(pg, 1), :, kv].rearrange("o t g d -> (o t) (g d)")
                    sp.dma_start(page[:, n % 4, :], src).then_inc(page_in[n % 4], 16)
                    if i == 3:
                        sp.dma_start(wc[:, :, :], io.nsa_w_cmp[kv].rearrange("l d e -> d l e")).then_inc(w_in, 16)

        @block.gpsimd
        def _(pool):
            pool.affine_select(out=s.hm[:, :], in_=s.ones[:, 0:BH], compare_op=ALU.is_ge, fill=0.0, base=0,
                               pattern=[[-8, BH]], channel_multiplier=1).then_inc(masks, 1)
            pool.wait_ge(masks, 1)
            pool.affine_select(out=s.hm[:, :], in_=s.hm[:, :], compare_op=ALU.is_ge, fill=0.0, base=7,
                               pattern=[[8, BH]], channel_multiplier=-1)
            for h in range(BH):
                last = pool.memset(slope_row[:, h:h + 1], -SLOPES[h])
            last.then_inc(masks, 1)

        @block.tensor
        def _(pe):
            for kv in range(2):
                pe.wait_ge(pe_in, 16 * (kv + 1))
                if kv:
                    pe.wait_ge(pos_done, 1)
                pe.transpose(ps[0:HD, 6, 0:CB], pes[:, :], s.ident[0:CB, 0:CB]).then_inc(pos_psum, 1)
                for i in range(NPAGES):
                    n = NPAGES * kv + i
                    pe.wait_ge(page_in[n % 4], 16 * (n // 4 + 1))
                    if n >= 4:
                        pe.wait_ge([page_even, page_odd][n % 2], (n - 4) // 2 + 1)
                    for g in range(KV):
                        last = pe.transpose(ps[0:HD, n % 4, g * P:(g + 1) * P], page[:, n % 4, g * HD:(g + 1) * HD],
                                            s.ident[:, :])
                    last.then_inc(page_psum, 1)
                pe.wait_ge(w_in, 16 * (kv + 1))
                pe.wait_ge(page_even, (kv + 1) * NPAGES // 2)
                pe.wait_ge(page_odd, (kv + 1) * NPAGES // 2)
                pe.wait_ge(pos_done, kv + 1)
                if kv:
                    pe.wait_ge(sums_read, 1)
                for l in range(CB):
                    pe.matmul(ps[0:HD, 4, 0:P], wc[:, l, :], xs[:, :, l], start=(l == 0), stop=(l == CB - 1))
                    last = pe.matmul(ps[0:HD, 5, 0:33], wc[:, l, :], s.cmpT[:, kv, :, l], start=(l == 0),
                                     stop=(l == CB - 1))
                last.then_inc(sums, 1)
            pe.wait_ge(vrep_ready, 1)
            pe.transpose(ps[:, 7, 0:HD], vcT[:, :, :, :].rearrange("e g r n -> e (g r n)"), s.ident[0:HD, 0:HD])
            for j in range(4):
                for g in range(KV):
                    last = pe.transpose(ps[0:8, j // 2, ((j % 2) * KV + g) * HD:((j % 2) * KV + g + 1) * HD],
                                        vsT[:, g, 2 * j:2 * j + 2, :].rearrange("e b n -> e (b n)"), s.ident[0:HD, 0:HD])
            last.then_inc(v_psum, 1)

        def pages_out(eng, copy, parity, done, kv):
            for i in range(parity, NPAGES, 2):
                n = NPAGES * kv + i
                b, half = i // NPG, i % NPG
                eng.wait_ge(page_psum, n + 1)
                if kv and i == parity:
                    eng.wait_ge(sums, 1)
                dst = xs[:, :, :].rearrange("d (b g n) l -> d b g (n l)", b=DB, g=KV)[:, b, :, half * P:(half + 1) * P]
                copy(dst, ps[0:HD, n % 4, :].rearrange("d (g t) -> d g t", g=KV)).then_inc(done, 1)

        @block.vector
        def _(dve):
            step = Count()

            def link(ins):
                ins.then_inc(chain, 1)
                dve.wait_ge(chain, step.add())

            for kv in range(2):
                dve.wait_ge(pos_psum, kv + 1)
                dve.tensor_copy(s.cmpT[:, kv, 32, :], ps[0:HD, 6, 0:CB]).then_inc(pos_done, 1)
                pages_out(dve, dve.tensor_copy, 0, page_even, kv)
                dve.wait_ge(sums, kv + 1)
                link(dve.tensor_copy(pcol[:, kv:kv + 1], ps[0:HD, 5, 32:33]))
                pos = pcol[:, kv:kv + 1]
                if kv == 0:
                    dve.tensor_scalar(s.kcP[:, :, :], ps[0:HD, 5, 0:32].rearrange("e (g n) -> e g n", g=KV), pos, None,
                                      ALU.add)
                    dve.tensor_scalar(s.kcS[:, :, :, :].rearrange("e b g n -> e (b g n)"), ps[0:HD, 4, 0:P], pos, None,
                                      ALU.add).then_inc(sums_read, 1)
                    continue
                src = ps[0:HD, 5, 0:32].rearrange("e (g n) -> e g n", g=KV)
                for r in range(REP):
                    dve.tensor_scalar(vcT[:, :, r, :], src, pos, None, ALU.add)
                dve.tensor_scalar(vsT[:, :, :, :].rearrange("e g b n -> e b g n"),
                                  ps[0:HD, 4, 0:P].rearrange("e (b g n) -> e b g n", b=DB, g=KV), pos, None,
                                  ALU.add).then_inc(vrep_ready, 1)
            dve.wait_ge(v_psum, 1)
            dve.wait_ge(masks, 2)
            link(dve.tensor_copy(s.vbd[:, 0, :], ps[:, 7, 0:HD]))
            for h in range(BH - 1, -1, -1):
                dve.tensor_scalar(s.vbd[:, h, :], s.vbd[:, 0, :], s.hm[:, h:h + 1], None, ALU.mult)
            last = None
            for q in range(2):
                last = dve.tensor_copy(s.vcn[:, 2 * q:2 * q + 2, :, :].rearrange("k j g e -> k (j g e)"), ps[0:8, q, :])
            last.then_inc(v_read, 1)

        @block.scalar
        def _(act):
            for kv in range(2):
                pages_out(act, act.copy, 1, page_odd, kv)
    sem.clear()


def stage_attend_prompt(nc, s, io):
    at, a0 = s.at, s.att
    dist = at("dist", a0, [P, TP])
    bias = at("abias", a0 + 512, [P, 2, TP])
    ex = at("ex", a0 + 1536, [P, 2, 2, TP])
    pt = at("pt", a0 + 3584, [P, 2, 2, TP])
    pc = at("pc", a0 + 5632, [P, 4, BH, 8])
    pcT = at("pcT", a0 + 6144, [P, TP])
    cdist = at("cdist", a0 + 6656, [P, 4, 8])
    valid = at("cvalid", a0 + 6688, [P, 4, 8])
    cb = at("cbias", a0 + 6720, [P, 4, BH, 8])
    cm = at("cmax", a0 + 7232, [P, 4, BH])
    mx = at("amx", a0 + 7296, [P, 4])
    nm = at("anm", a0 + 7304, [P, 4])
    rs = at("ars", a0 + 7312, [P, 4])
    rr = at("arr", a0 + 7320, [P, 4])
    keysT = [s.kslT, s.kwiT]
    vals = [s.vsl, s.vwi]
    units = [(h, i) for h in range(BH) for i in range(4)]
    NU = len(units)
    sem = Semaphores(nc)
    with ExitStack() as ctx:
        made, dist_ready, chain = sem("dist_made"), sem("dist_ready2"), sem("att_chain")
        cs_psum, cexp_in, cexp_done, pc_ready, pcT_psum, pcT_ready = (sem("cs_psum"), sem("cexp_in"), sem("cexp_done"),
                                                                     sem("pc_ready2"), sem("pcT_psum"), sem("pcT_ready"))
        gate_exp, bias_ready = sem("gate_exp"), sem("bias_ready")
        s_psum, s_max, s_exp, s_scaled, t_psum, t_done, o_psum, o_done = (
            sem("s_psum"), sem("s_max"), sem("s_exp"), sem("s_scaled"), sem("t_psum"), sem("t_done"), sem("o_psum"),
            sem("o_done"))
        ps = ctx.enter_context(nc.psum_tensor("ps_a", [P, 8, 512], F32))
        block = ctx.enter_context(nc.Block())

        @block.gpsimd
        def _(pool):
            pool.iota(dist[:, :], pattern=[[-1, TP]], base=384, channel_multiplier=1,
                      allow_small_or_imprecise_dtypes=True)
            pool.iota(cdist[:, :, :], pattern=[[P, 4], [-CB, 8]], base=1 - CB, channel_multiplier=1,
                      allow_small_or_imprecise_dtypes=True).then_inc(made, 1)
            pool.wait_ge(made, 1)
            pool.affine_select(out=dist[:, :], in_=dist[:, :], compare_op=ALU.is_ge, fill=BIG, base=384,
                               pattern=[[-1, TP]], channel_multiplier=1)
            pool.affine_select(out=valid[:, :, :], in_=s.ones[:, 0:32].rearrange("p (i n) -> p i n", i=4),
                               compare_op=ALU.is_ge, fill=0.0, base=1 - CB, pattern=[[P, 4], [-CB, 8]],
                               channel_multiplier=1)
            pool.affine_select(out=cdist[:, :, :], in_=cdist[:, :, :], compare_op=ALU.is_ge, fill=BIG, base=1 - CB,
                               pattern=[[P, 4], [-CB, 8]], channel_multiplier=1).then_inc(dist_ready, 1)

        @block.tensor
        def _(pe):
            for i in range(4):
                for h in range(BH):
                    last = pe.matmul(ps[:, 6, (i * BH + h) * 8:(i * BH + h + 1) * 8], s.bqT[:, h, i * P:(i + 1) * P],
                                     s.kcP[:, h // REP, :], start=True, stop=True)
            last.then_inc(cs_psum, 1)

            def scores(u):
                h, i = units[u]
                if u >= 2:
                    pe.wait_ge(s_max, u - 1)
                for br in range(2):
                    last = pe.matmul(ps[:, 2 * (u % 2) + br, 0:(i + 1) * P], s.bqT[:, h, i * P:(i + 1) * P],
                                     keysT[br][:, h // REP, 0:(i + 1) * P], start=True, stop=True)
                last.then_inc(s_psum, 1)

            def turn(u):
                h, i = units[u]
                pe.wait_ge(s_scaled, u + 1)
                if u >= 1:
                    pe.wait_ge(t_done, u)
                for br in range(2):
                    for c in range(i + 1):
                        last = pe.transpose(ps[:, 4 + br, c * P:(c + 1) * P], ex[:, u % 2, br, c * P:(c + 1) * P],
                                            s.ident[:, :])
                last.then_inc(t_psum, 1)

            def output(u):
                h, i = units[u]
                pair = h // 2
                if u == 0:
                    pe.wait_ge(pcT_ready, 1)
                if h % 2 == 0 and i == 0 and pair >= 2:
                    pe.wait_ge(o_done, pair - 1)
                pe.wait_ge(t_done, u + 1)
                out = ps[64 * (h % 2):64 * (h % 2) + HD, 6 + pair % 2, i * P:(i + 1) * P]
                pe.matmul(out, s.vbd[:, h, :], pcT[:, i * P:(i + 1) * P], start=True, stop=False)
                g = h // REP
                for br in range(2):
                    for c in range(i + 1):
                        last = pe.matmul(out, vals[br][:, c, g * HD:(g + 1) * HD], pt[:, u % 2, br, c * P:(c + 1) * P],
                                         start=False, stop=(br == 1 and c == i))
                last.then_inc(o_psum, 1)

            scores(0)
            scores(1)
            pe.wait_ge(pc_ready, 1)
            for i in range(4):
                last = pe.transpose(ps[:, 7, i * P:(i + 1) * P], pc[:, i, :, :].rearrange("p h n -> p (h n)"),
                                    s.ident[:, :])
            last.then_inc(pcT_psum, 1)
            for u in range(NU):
                turn(u)
                if u + 2 < NU:
                    scores(u + 2)
                if u >= 1:
                    output(u - 1)
            output(NU - 1)

        @block.vector
        def _(dve):
            step = Count()

            def link(ins):
                ins.then_inc(chain, 1)
                dve.wait_ge(chain, step.add())

            dve.wait_ge(gate_exp, 1)
            dve.tensor_scalar(s.gden[:, 0:4, :], s.gden[:, 0:4, :], 1.0, None, ALU.add)
            link(dve.tensor_scalar(s.gden[0:TS, 4, :], s.gden[0:TS, 4, :], 1.0, None, ALU.add))
            dve.wait_ge(dist_ready, 1)
            for i in range(4):
                last = dve.tensor_tensor(cb[:, i, :, :], cdist[:, i, :].unsqueeze(1).broadcast_to([P, BH, 8]),
                                         s.slope_row[:, :].unsqueeze(2).broadcast_to([P, BH, 8]), ALU.mult)
            link(last)

            def flat(x):
                return x[:, :, :, :].rearrange("p i h n -> p (i h) n")

            dve.wait_ge(cs_psum, 1)
            link(dve.tensor_tensor(flat(pc), ps[:, 6, :].rearrange("p (x n) -> p x n", n=8), flat(cb), ALU.add))
            cmf = cm[:, :, :].rearrange("p i h -> p (i h)")
            link(dve.tensor_reduce(cmf, flat(pc), AX.X, ALU.max))
            dve.tensor_tensor(flat(pc), flat(pc), cmf.unsqueeze(2).broadcast_to([P, 64, 8]), ALU.subtract)\
               .then_inc(cexp_in, 1)
            dve.wait_ge(cexp_done, 1)
            link(dve.tensor_reduce(cmf, flat(pc), AX.X, ALU.add))
            link(dve.tensor_tensor(cm[:, :, :], cm[:, :, :], s.gden[:, 0:4, 0:BH], ALU.mult))
            link(dve.reciprocal(cmf, cmf))
            link(dve.tensor_tensor(flat(pc), flat(pc), cmf.unsqueeze(2).broadcast_to([P, 64, 8]), ALU.mult))
            for i in range(4):
                last = dve.tensor_tensor(pc[:, i, :, :], pc[:, i, :, :],
                                         valid[:, i, :].unsqueeze(1).broadcast_to([P, BH, 8]), ALU.mult)
            last.then_inc(pc_ready, 1)

            def maxima(u):
                h, i = units[u]
                w = (i + 1) * P
                if i == 0:
                    dve.wait_ge(bias_ready, h + 1)
                dve.wait_ge(s_psum, u + 1)
                if u >= 2:
                    dve.wait_ge(t_psum, u - 1)
                o = 2 * (u % 2)
                for br in range(2):
                    last = dve.tensor_tensor_reduce(out=ex[:, u % 2, br, 0:w], in0=ps[:, o + br, 0:w],
                                                    in1=bias[:, h % 2, TP - w:TP], scale=1.0, scalar=-3e38, op0=ALU.add,
                                                    op1=ALU.max, accum_out=mx[:, o + br:o + br + 1])
                link(last)
                dve.tensor_scalar(nm[:, o:o + 2], mx[:, o:o + 2], -1.0, None, ALU.mult).then_inc(s_max, 1)

            def scale(u):
                h, i = units[u]
                w, o = (i + 1) * P, 2 * (u % 2)
                dve.wait_ge(s_exp, u + 1)
                gd = s.gden[:, i, :].rearrange("p (b h) -> p b h", b=3)[:, 1:3, h]
                link(dve.tensor_tensor(rr[:, o:o + 2], rs[:, o:o + 2], gd, ALU.mult))
                link(dve.reciprocal(rr[:, o:o + 2], rr[:, o:o + 2]))
                for br in range(2):
                    x = ex[:, u % 2, br, 0:w]
                    last = dve.tensor_scalar(x, x, rr[:, o + br:o + br + 1], None, ALU.mult)
                last.then_inc(s_scaled, 1)

            dve.wait_ge(pcT_psum, 1)
            dve.tensor_copy(pcT[:, :], ps[:, 7, :]).then_inc(pcT_ready, 1)
            maxima(0)
            for u in range(NU):
                if u + 1 < NU:
                    maxima(u + 1)
                scale(u)

        @block.scalar
        def _(act):
            act.activation(s.gden[:, 0:4, :], s.gat[:, 0:4, :], ACT.Exp, scale=-1.0)
            act.activation(s.gden[0:TS, 4, :], s.gat[0:TS, 4, :], ACT.Exp, scale=-1.0).then_inc(gate_exp, 1)
            act.wait_ge(cexp_in, 1)
            act.activation(pc[:, :, :, :], pc[:, :, :, :], ACT.Exp).then_inc(cexp_done, 1)
            act.wait_ge(dist_ready, 1)
            for h in range(2):
                act.mul(bias[:, h, :], dist[:, :], -SLOPES[h]).then_inc(bias_ready, 1)

            def copy_turned(u):
                h, i = units[u]
                w = (i + 1) * P
                act.wait_ge(t_psum, u + 1)
                if u >= 2:
                    act.wait_ge(o_psum, u - 1)
                for br in range(2):
                    last = act.copy(pt[:, u % 2, br, 0:w], ps[:, 4 + br, 0:w])
                last.then_inc(t_done, 1)
                if h % 2 == 1 and i == 3:
                    pair = h // 2
                    act.wait_ge(o_psum, u + 1)
                    act.copy(s.ybT[:, pair, 0:TP], ps[:, 6 + pair % 2, :]).then_inc(o_done, 1)

            for u, (h, i) in enumerate(units):
                act.wait_ge(s_max, u + 1)
                w, o = (i + 1) * P, 2 * (u % 2)
                for br in range(2):
                    x = ex[:, u % 2, br, 0:w]
                    last = act.activation(x, x, ACT.Exp, bias=nm[:, o + br:o + br + 1],
                                          accum_out=rs[:, o + br:o + br + 1])
                last.then_inc(s_exp, 1)
                if i == 3 and h + 2 < BH:
                    act.mul(bias[:, h % 2, :], dist[:, :], -SLOPES[h + 2]).then_inc(bias_ready, 1)
                if u >= 1:
                    copy_turned(u - 1)
            copy_turned(NU - 1)
    sem.clear()


def stage_attend_samples(nc, s, io):
    at, a0, f0 = s.at, s.att, 30240
    W = 2 * PAST + TS
    qs = at("qs", a0, [HD, 4, BH, 8])
    rows = at("kv_rows", a0 + 512, [P, 2, 2, 4, 2 * KV * HD])
    kt = at("kt_s", a0 + 8704, [HD, 2, 2, KV, PAST])
    ex = at("ex_s", a0 + 12800, [P, 2, W])
    pt = at("pt_s", a0 + 13888, [P, 2, 4 * P])
    ptn = at("ptn", a0 + 14912, [TS, 2, P])
    pcs = at("pcs", a0 + 15168, [P, 8])
    pctT = at("pcsT", a0 + 15176, [8, P])
    bias = at("bias_s", a0 + 15304, [P, W])
    newd = at("newd", a0 + 15848, [P, 4, TS])
    gd = at("gd", a0 + 15976, [P, 4, 4])
    tmp = at("gtmp", a0 + 15992, [P, 3, BH])
    cbias = at("cbias_s", a0 + 16040, [P, 8])
    cols = at("cols_s", a0 + 16048, [P, 16])
    icol = at("icol", a0 + 16064, [P, 8], I32)
    mx = at("mx_s", a0 + 16072, [P, 8])
    table = at("table_s", a0 + 16080, [1, DB * NPG], I32)
    nv = at("nv", a0 + 16096, [P, 4])
    sel = at("sel", f0, [TS, 4, BH, 8])
    v1 = at("nv1", f0 + 512, [P, 4, TS])
    v2 = at("nv2", f0 + 640, [P, 4, TS])
    keysT = [s.kslT, s.kwiT]
    vals = [s.vsl, s.vwi]
    slope, t4, b2, nb2, t8 = (cols[:, i:i + 1] for i in range(5))
    sem = Semaphores(nc)
    with ExitStack() as ctx:
        made, sel_ready, chain, table_in = sem("s_made"), sem("sel_ready"), sem("s_chain"), sem("s_table")
        rows_in = [sem("kv_in0"), sem("kv_in1")]
        gd_psum, gd_read, qs_ready = sem("gd_psum"), sem("gd_read"), sem("qs_ready")
        k_psum, k_even, k_odd = sem("k_psum"), sem("k_even"), sem("k_odd")
        c_psum, s_psum, s_max, s_exp, s_scaled = sem("sc_psum"), sem("ss_psum"), sem("ss_max"), sem("ss_exp"), sem("ss_scaled")
        t_psum, t_dve, t_act, o_psum, o_done = sem("st_psum"), sem("st_dve"), sem("st_act"), sem("so_psum"), sem("so_done")
        ps = ctx.enter_context(nc.psum_tensor("ps_s", [P, 8 * 512], F32))
        block = ctx.enter_context(nc.Block())

        @block.sync
        def _(sp):
            sp.dma_start(table[:, :], io.page_table.rearrange("b n -> (b n)").unsqueeze(0)).then_inc(table_in, 16)
            sp.wait_ge(table_in, 16)
            for j in range(4):
                if j >= 2:
                    sp.wait_ge(o_psum, j - 1)
                for c in range(4):
                    i = 4 * j + c
                    pg = sp.value_load(table[0:1, i:i + 1], min_val=0, max_val=io.cache_slc_kv.shape[0] - 1)
                    src = io.cache_slc_kv[bass.ds(pg, 1)].rearrange("o t a g d -> (o t) (a g d)")
                    sp.dma_start(rows[:, j % 2, 0, c, :], src).then_inc(rows_in[j % 2], 16)
                src = io.cache_win_kv[2 * j:2 * j + 2].rearrange("b (c p) a g d -> p (b c) (a g d)", p=P)
                sp.dma_start(rows[:, j % 2, 1, :, :], src).then_inc(rows_in[j % 2], 16)

        @block.gpsimd
        def _(pool):
            pool.iota(icol[:, 0:1], pattern=[[0, 1]], base=0, channel_multiplier=1)
            pool.iota(bias[:, 0:512], pattern=[[0, 2], [-1, PAST]], base=PAST, channel_multiplier=0,
                      allow_small_or_imprecise_dtypes=True)
            pool.iota(newd[:, :, :], pattern=[[8, 4], [-1, TS]], base=0, channel_multiplier=0,
                      allow_small_or_imprecise_dtypes=True)
            pool.iota(cbias[:, :], pattern=[[0, 2], [-CB, 4]], base=PAST - CB + 1, channel_multiplier=0,
                      allow_small_or_imprecise_dtypes=True).then_inc(made, 1)
            pool.memset(sel[:, :, :, :], 1.0).then_inc(sel_ready, 1)
            pool.wait_ge(sel_ready, 1)
            pool.affine_select(out=sel[:, :, :, :], in_=sel[:, :, :, :], compare_op=ALU.is_equal, fill=0.0, base=0,
                               pattern=[[-8, 4], [0, BH], [-1, 8]], channel_multiplier=1).then_inc(sel_ready, 1)

        @block.tensor
        def _(pe):
            pe.wait_ge(sel_ready, 2)
            for j in range(4):
                last = pe.matmul(ps[:, 6 * 512 + 48 * j:6 * 512 + 48 * (j + 1)],
                                 sel[:, j, :, :].rearrange("w h t -> w (h t)"), s.gden[0:TS, 4, :], start=True, stop=True)
            last.then_inc(gd_psum, 1)
            for j in range(4):
                pe.wait_ge(rows_in[j % 2], 80 * (j // 2 + 1))
                for n in range(16):
                    br, c = n // 8, (n // 2) % 4
                    m = 8 * j + n // 2
                    if n % 2 == 0:
                        if j and n < 4:
                            pe.wait_ge(t_dve, j)
                            pe.wait_ge(t_act, j)
                        if m >= 2:
                            pe.wait_ge([k_even, k_odd][m % 2], (m - 2) // 2 + 1)
                    for g in (2 * (n % 2), 2 * (n % 2) + 1):
                        last = pe.transpose(ps[0:HD, (m % 2) * 512 + g * P:(m % 2) * 512 + (g + 1) * P],
                                            rows[:, j % 2, br, c, g * HD:(g + 1) * HD], s.ident[:, :])
                    if n % 2:
                        last.then_inc(k_psum, 1)
                if j == 0:
                    pe.wait_ge(qs_ready, 1)
                for g in range(KV):
                    q = qs[:, j, 4 * g:4 * g + 4, :].rearrange("d h t -> d (h t)")
                    last = pe.matmul(ps[32 * g:32 * g + 32, 7 * 512 + 384:7 * 512 + 392], q,
                                     s.kcS[:, 2 * j:2 * j + 2, g, :], start=True, stop=True)
                last.then_inc(c_psum, 1)
                pe.wait_ge(k_even, 4 * (j + 1))
                pe.wait_ge(k_odd, 4 * (j + 1))
                if j:
                    pe.wait_ge(s_max, j)
                for br in range(2):
                    o = (2 + 2 * br) * 512
                    for g in range(KV):
                        q = qs[:, j, 4 * g:4 * g + 4, :].rearrange("d h t -> d (h t)")
                        pe.matmul(ps[32 * g:32 * g + 32, o:o + 512], q, kt[:, br, :, g, :], start=True, stop=True)
                        last = pe.matmul(ps[32 * g:32 * g + 32, o + 512:o + W], q, keysT[br][:, g, TP:T], start=True,
                                         stop=True)
                last.then_inc(s_psum, 1)
                pe.wait_ge(s_scaled, j + 1)
                for br in range(2):
                    for c in range(4):
                        pe.transpose(ps[:, br * 512 + c * P:br * 512 + (c + 1) * P], ex[:, br, c * P:(c + 1) * P],
                                     s.ident[:, :])
                    pe.transpose(ps[0:TS, 7 * 512 + br * P:7 * 512 + (br + 1) * P], ex[:, br, 512:W], s.ident[:, :])
                pe.transpose(ps[0:8, 7 * 512 + 256:7 * 512 + 384], pcs[:, :], s.ident[:, :]).then_inc(t_psum, 1)
                pe.wait_ge(t_dve, j + 1)
                pe.wait_ge(t_act, j + 1)
                if j:
                    pe.wait_ge(o_done, j)
                else:
                    pe.wait_ge(gd_read, 1)
                for g in range(KV):
                    out = ps[0:HD, 6 * 512 + 32 * g:6 * 512 + 32 * (g + 1)]
                    r = slice(32 * g, 32 * (g + 1))
                    pe.matmul(out, s.vcn[:, j, g, :], pctT[:, r], start=True, stop=False)
                    for br in range(2):
                        for c in range(4):
                            pe.matmul(out, rows[:, j % 2, br, c, (KV + g) * HD:(KV + g + 1) * HD],
                                      pt[:, br, c * P + 32 * g:c * P + 32 * (g + 1)], start=False, stop=False)
                        last = pe.matmul(out, vals[br][0:TS, 4, g * HD:(g + 1) * HD], ptn[:, br, r], start=False,
                                         stop=(br == 1))
                last.then_inc(o_psum, 1)

        def keys_out(eng, copy, j, parity, done):
            for m in range(8 * j + parity, 8 * (j + 1), 2):
                eng.wait_ge(k_psum, m + 1)
                if j:
                    eng.wait_ge(s_psum, j)
                br, c = (m % 8) // 4, m % 4
                dst = kt[:, br, c // 2, :, (c % 2) * P:(c % 2 + 1) * P]
                copy(dst, ps[0:HD, (m % 2) * 512:(m % 2 + 1) * 512].rearrange("d (g t) -> d g t", g=KV)).then_inc(done, 1)

        @block.vector
        def _(dve):
            step = Count()

            def link(ins):
                ins.then_inc(chain, 1)
                dve.wait_ge(chain, step.add())

            for j in range(4):
                last = dve.tensor_copy(qs[:, j, :, :], s.bqT[:, :, TP + 8 * j:TP + 8 * (j + 1)])
            last.then_inc(qs_ready, 1)
            dve.wait_ge(made, 1)
            dve.tensor_scalar(icol[:, 1:2], icol[:, 0:1], 3, None, ALU.bitwise_and)
            dve.tensor_scalar(icol[:, 2:3], icol[:, 0:1], 2, 1, ALU.logical_shift_right, ALU.bitwise_and)
            dve.tensor_scalar(icol[:, 3:4], icol[:, 0:1], 7, None, ALU.bitwise_and)
            link(dve.tensor_tensor(tmp[:, 0, :], s.hm[:, :], s.slope_row[:, :], ALU.mult))
            dve.tensor_copy(t4, icol[:, 1:2])
            dve.tensor_copy(b2, icol[:, 2:3])
            dve.tensor_copy(t8, icol[:, 3:4])
            link(dve.tensor_reduce(slope, tmp[:, 0, :], AX.X, ALU.add))
            dve.tensor_scalar(b2, b2, BIG, None, ALU.mult)
            link(dve.tensor_scalar(newd[:, :, :], newd[:, :, :], t8, None, ALU.add))
            link(dve.tensor_scalar(nb2, b2, -1.0, BIG, ALU.mult, ALU.add))
            for wrong, c in ((b2, 0), (nb2, 1)):
                x = bias[:, c * PAST:(c + 1) * PAST]
                link(dve.tensor_scalar(x, x, t4, wrong, ALU.add, ALU.add))
                link(dve.tensor_scalar(x, x, slope, None, ALU.mult))
                x = cbias[:, 4 * c:4 * c + 4]
                link(dve.tensor_scalar(x, x, t4, wrong, ALU.add, ALU.add))
                link(dve.tensor_scalar(x, x, slope, None, ALU.mult))
            dve.tensor_scalar(v1[:, :, :], newd[:, :, :], 0.0, BIG, ALU.is_lt, ALU.mult)
            link(dve.tensor_scalar(v2[:, :, :], newd[:, :, :], t4, BIG, ALU.is_gt, ALU.mult))
            link(dve.tensor_tensor(newd[:, :, :], newd[:, :, :], v1[:, :, :], ALU.add))
            link(dve.tensor_tensor(newd[:, :, :], newd[:, :, :], v2[:, :, :], ALU.add))
            link(dve.tensor_scalar(newd[:, :, :], newd[:, :, :], slope, None, ALU.mult))
            dve.wait_ge(gd_psum, 1)
            for j in range(4):
                link(dve.tensor_tensor(tmp[:, :, :], ps[:, 6 * 512 + 48 * j:6 * 512 + 48 * (j + 1)]
                                       .rearrange("p (b h) -> p b h", b=3),
                                       s.hm[:, :].unsqueeze(1).broadcast_to([P, 3, BH]), ALU.mult))
                link(dve.tensor_reduce(gd[:, j, 0:3], tmp[:, :, :], AX.X, ALU.add))
            dve.tensor_copy(nv[:, 0:1], gd[:, 0, 0:1]).then_inc(gd_read, 1)
            for j in range(4):
                keys_out(dve, dve.tensor_copy, j, 0, k_even)
                link(dve.tensor_copy(bias[:, 512:W], newd[:, j, :]))
                dve.wait_ge(c_psum, j + 1)
                dve.tensor_tensor_reduce(out=pcs[:, :], in0=ps[:, 7 * 512 + 384:7 * 512 + 392], in1=cbias[:, :],
                                         scale=1.0, scalar=-3e38, op0=ALU.add, op1=ALU.max, accum_out=mx[:, 0:1])
                dve.wait_ge(s_psum, j + 1)
                for br in range(2):
                    o = (2 + 2 * br) * 512
                    last = dve.tensor_tensor_reduce(out=ex[:, br, :], in0=ps[:, o:o + W], in1=bias[:, :], scale=1.0,
                                                    scalar=-3e38, op0=ALU.add, op1=ALU.max,
                                                    accum_out=mx[:, 1 + br:2 + br])
                link(last)
                dve.tensor_scalar(mx[:, 0:3], mx[:, 0:3], -1.0, None, ALU.mult).then_inc(s_max, 1)
                dve.wait_ge(s_exp, j + 1)
                link(dve.tensor_tensor(cols[:, 8:11], cols[:, 8:11], gd[:, j, 0:3], ALU.mult))
                link(dve.reciprocal(cols[:, 8:11], cols[:, 8:11]))
                dve.tensor_scalar(pcs[:, :], pcs[:, :], cols[:, 8:9], None, ALU.mult)
                for br in range(2):
                    last = dve.tensor_scalar(ex[:, br, :], ex[:, br, :], cols[:, 9 + br:10 + br], None, ALU.mult)
                last.then_inc(s_scaled, 1)
                dve.wait_ge(t_psum, j + 1)
                dve.tensor_copy(pt[:, 0, :], ps[:, 0:512])
                dve.tensor_copy(pctT[:, :], ps[0:8, 7 * 512 + 256:7 * 512 + 384])
                dve.tensor_copy(ptn[:, :, :], ps[0:TS, 7 * 512:7 * 512 + 256].rearrange("w (b r) -> w b r", b=2))\
                   .then_inc(t_dve, 1)
                dve.wait_ge(o_psum, j + 1)
                o = ps[0:HD, 6 * 512:6 * 512 + P].rearrange("d (q e t) -> d q e t", q=BH // 2, e=2)
                for e in range(2):
                    last = dve.tensor_copy(s.ybT[HD * e:HD * (e + 1), :, TP + 8 * j:TP + 8 * (j + 1)], o[:, :, e, :])
                last.then_inc(o_done, 1)

        @block.scalar
        def _(act):
            for j in range(4):
                keys_out(act, act.copy, j, 1, k_odd)
                act.wait_ge(s_max, j + 1)
                act.activation(pcs[:, :], pcs[:, :], ACT.Exp, bias=mx[:, 0:1], accum_out=cols[:, 8:9])
                for br in range(2):
                    last = act.activation(ex[:, br, :], ex[:, br, :], ACT.Exp, bias=mx[:, 1 + br:2 + br],
                                          accum_out=cols[:, 9 + br:10 + br])
                last.then_inc(s_exp, 1)
                act.wait_ge(t_psum, j + 1)
                act.copy(pt[:, 1, :], ps[:, 512:1024]).then_inc(t_act, 1)
    sem.clear()


def stage_merge(nc, s, io):
    at = s.at
    MW = 256
    ring = at("m_ring", 5632, [P, 2, 4, DC, MW])
    s.mT = mT = at("mT", 36992, [P, DC, T])
    sg = at("m_gate", 41344, [P, 2, 2, HALF])
    pr = at("m_prod", 42432, [P, 2, 2, HALF])
    s.wo = at("wo", 43520, [P, DC, D])
    mats = [io.w_merge[:, 0:D], io.w_merge[:, D:2 * D], io.w_br_a, io.w_br_b]
    movs = [s.xT, s.xT, s.yaT, s.ybT]
    sem = Semaphores(nc)
    with ExitStack() as ctx:
        w_in, m_psum, g_done, p_done, m_done = [sem("m_w0"), sem("m_w1")], sem("m_psum"), sem("m_gates"), sem("m_prods"), sem("m_done")
        ps = ctx.enter_context(nc.psum_tensor("ps_g", [P, 8, 512], F32))
        block = ctx.enter_context(nc.Block())
        NS = D // MW
        UPS = 2 * (MW // P)

        @block.sync
        def _(sp):
            for q in range(NS):
                if q >= 2:
                    sp.wait_ge(m_psum, UPS * (q - 1))
                for m in range(4):
                    src = mats[m][:, q * MW:(q + 1) * MW].rearrange("(c p) n -> p c n", p=P)
                    sp.dma_start(ring[:, q % 2, m, :, :], src).then_inc(w_in[q % 2], 16)

        @block.gpsimd
        def _(pool):
            pool.dma_start(s.wo[:, :, :], io.w_out.rearrange("(c p) n -> p c n", p=P)).then_inc(s.wo_in, 16)

        @block.tensor
        def _(pe):
            for u in range(NS * UPS):
                q, e, half = u // UPS, (u % UPS) // 2, u % 2
                if u % UPS == 0:
                    pe.wait_ge(w_in[q % 2], 64 * (q // 2 + 1))
                if u >= 2:
                    pe.wait_ge(p_done, u - 1)
                for m in range(4):
                    for dc in range(DC):
                        last = pe.matmul(ps[:, 4 * (u % 2) + m, 0:HALF], ring[:, q % 2, m, dc, e * P:(e + 1) * P],
                                         movs[m][:, dc, half * HALF:(half + 1) * HALF], start=(dc == 0),
                                         stop=(dc == DC - 1))
                last.then_inc(m_psum, 1)

        @block.scalar
        def _(act):
            for u in range(NS * UPS):
                act.wait_ge(m_psum, u + 1)
                if u >= 2:
                    act.wait_ge(p_done, u - 1)
                for b in range(2):
                    last = act.activation(sg[:, u % 2, b, :], ps[:, 4 * (u % 2) + b, 0:HALF], ACT.Sigmoid)
                last.then_inc(g_done, 1)

        @block.vector
        def _(dve):
            for u in range(NS * UPS):
                ec, half = u // 2, u % 2
                dve.wait_ge(g_done, u + 1)
                if u >= 2:
                    dve.wait_ge(m_done, u - 1)
                for b in range(2):
                    last = dve.tensor_tensor(pr[:, u % 2, b, :], ps[:, 4 * (u % 2) + 2 + b, 0:HALF], sg[:, u % 2, b, :],
                                             ALU.mult)
                last.then_inc(p_done, 1)
                dve.wait_ge(p_done, u + 1)
                dve.tensor_tensor(mT[:, ec, half * HALF:(half + 1) * HALF], pr[:, u % 2, 0, :], pr[:, u % 2, 1, :],
                                  ALU.add).then_inc(m_done, 1)
    sem.clear()


def norm_rows(dve, link, x, st, mv, rs, eps_done, sqrt_done, n, g, b, rows):
    link(dve.bn_stats(st[0:rows, 0, :], x[:, 0:512]))
    link(dve.bn_stats(st[0:rows, 1, :], x[:, 512:D]))
    link(dve.bn_aggr(mv[0:rows, :], st[0:rows, :, :].rearrange("p a b -> p (a b)")))
    dve.tensor_scalar(rs[0:rows, 0:1], mv[0:rows, 1:2], LN_EPS, None, ALU.add).then_inc(eps_done, 1)
    dve.wait_ge(sqrt_done, n + 1)
    link(dve.reciprocal(rs[0:rows, 1:2], rs[0:rows, 0:1]))
    link(dve.tensor_scalar(x, x, mv[0:rows, 0:1], rs[0:rows, 1:2], ALU.subtract, ALU.mult))
    link(dve.tensor_tensor(x, x, g[0:rows, :], ALU.mult))
    return dve.tensor_tensor(x, x, b[0:rows, :], ALU.add)


def stage_norm1(nc, s, io):
    at = s.at
    xr = at("xr", 22704, [P, 2, D])
    hr = at("hr", 24752, [P, 2, D])
    gb = at("ln1_gb", 26800, [P, 2, D])
    st = at("ln1_st", 28848, [P, 2, 6])
    mv = at("ln1_mv", 28864, [P, 2])
    rs = at("ln1_rs", 28872, [P, 2])
    s.hT = at("hT", 9648, [P, DC, T])
    s.hTh = at("hTh", 944, [P, DC, T], F32R)
    s.hTl = at("hTl", 5296, [P, DC, T], F32R)
    sem = Semaphores(nc)
    with ExitStack() as ctx:
        x_in, gb_in, o_psum, o_read, chain, eps_done, sqrt_done = ([sem("n_x0"), sem("n_x1")], sem("n_gb"), sem("n_psum"),
                                                                  sem("n_read"), sem("n_chain"), sem("n_eps"), sem("n_sqrt"))
        h_ready, h_sent, t_psum, t_hi, t_lo = sem("n_h"), [sem("n_sent0"), sem("n_sent1")], sem("n_tp"), sem("n_hi"), sem("n_lo")
        ps = ctx.enter_context(nc.psum_tensor("ps_n", [P, 8, 512], F32))
        block = ctx.enter_context(nc.Block())

        def x_rows(t):
            return io.x_prompt[0, t * P:(t + 1) * P, :] if t < 4 else io.x_sample.rearrange("b t d -> (b t) d")

        @block.sync
        def _(sp):
            sp.dma_start(gb[:, 0, :], io.ln1_g.partition_broadcast(P)).then_inc(gb_in, 16)
            sp.dma_start(gb[:, 1, :], io.ln1_b.partition_broadcast(P)).then_inc(gb_in, 16)
            for t in range(NT):
                if t >= 2:
                    sp.wait_ge(h_ready, t - 1)
                sp.dma_start(xr[0:ROWS[t], t % 2, :], x_rows(t)).then_inc(x_in[t % 2], 16)

        @block.gpsimd
        def _(pool):
            for t in range(NT):
                pool.wait_ge(h_ready, t + 1)
                pool.dma_start(io.h_rows[t * P:t * P + ROWS[t], :], hr[0:ROWS[t], t % 2, :]).then_inc(h_sent[t % 2], 16)
            pool.wait_ge(h_sent[0], 48)
            pool.wait_ge(h_sent[1], 32)

        @block.tensor
        def _(pe):
            def turn(t):
                pe.wait_ge(h_ready, t + 1)
                for q in range(2):
                    n = 2 * t + q
                    if n >= 4:
                        pe.wait_ge(t_lo, n - 3)
                    for c in range(4):
                        last = pe.transpose(ps[:, 4 + n % 4, c * P:c * P + ROWS[t]],
                                            hr[0:ROWS[t], t % 2, (4 * q + c) * P:(4 * q + c + 1) * P],
                                            s.ident[0:ROWS[t], 0:ROWS[t]])
                    last.then_inc(t_psum, 1)

            pe.wait_ge(s.wo_in, 16)
            for t in range(NT):
                if t >= 2:
                    pe.wait_ge(o_read, t - 1)
                for q in range(2):
                    for dc in range(DC):
                        last = pe.matmul(ps[0:ROWS[t], 2 * (t % 2) + q, :], s.mT[:, dc, t * P:t * P + ROWS[t]],
                                         s.wo[:, dc, q * 512:(q + 1) * 512], start=(dc == 0), stop=(dc == DC - 1))
                last.then_inc(o_psum, 1)
                if t:
                    turn(t - 1)
            turn(NT - 1)

        @block.vector
        def _(dve):
            step = Count()

            def link(ins):
                ins.then_inc(chain, 1)
                dve.wait_ge(chain, step.add())

            def low(t):
                for q in range(2):
                    n = 2 * t + q
                    dve.wait_ge(t_hi, n + 1)
                    src = ps[:, 4 + n % 4, :].rearrange("p (c t) -> p c t", c=4)[:, :, 0:ROWS[t]]
                    cs, ts = slice(4 * q, 4 * q + 4), slice(t * P, t * P + ROWS[t])
                    dve.tensor_tensor(s.hTl[:, cs, ts], src, s.hTh[:, cs, ts].bitcast(F32), ALU.subtract).then_inc(t_lo, 1)

            dve.wait_ge(gb_in, 32)
            for t in range(NT):
                r = ROWS[t]
                dve.wait_ge(o_psum, t + 1)
                dve.wait_ge(x_in[t % 2], 16 * (t // 2 + 1))
                if t >= 2:
                    dve.wait_ge(h_sent[t % 2], 16 * (t // 2))
                    dve.wait_ge(t_psum, 2 * (t - 1))
                for q in range(2):
                    last = dve.scalar_tensor_tensor(out=hr[0:r, t % 2, q * 512:(q + 1) * 512],
                                                    in0=xr[0:r, t % 2, q * 512:(q + 1) * 512], scalar=DN_ALPHA,
                                                    in1=ps[0:r, 2 * (t % 2) + q, :], op0=ALU.mult, op1=ALU.add)
                last.then_inc(o_read, 1)
                dve.wait_ge(o_read, t + 1)
                norm_rows(dve, link, hr[0:r, t % 2, :], st, mv, rs, eps_done, sqrt_done, t, gb[:, 0, :], gb[:, 1, :], r)\
                    .then_inc(h_ready, 1)
                if t:
                    low(t - 1)
            low(NT - 1)

        @block.scalar
        def _(act):
            def high(t):
                for q in range(2):
                    n = 2 * t + q
                    act.wait_ge(t_psum, n + 1)
                    src = ps[:, 4 + n % 4, :].rearrange("p (c t) -> p c t", c=4)[:, :, 0:ROWS[t]]
                    cs, ts = slice(4 * q, 4 * q + 4), slice(t * P, t * P + ROWS[t])
                    act.copy(s.hT[:, cs, ts], src)
                    act.copy(s.hTh[:, cs, ts], src).then_inc(t_hi, 1)

            for t in range(NT):
                r = ROWS[t]
                act.wait_ge(eps_done, t + 1)
                act.activation(rs[0:r, 0:1], rs[0:r, 0:1], ACT.Sqrt).then_inc(sqrt_done, 1)
                if t:
                    high(t - 1)
            high(NT - 1)
    sem.clear()


def top_two(dve, link, values, tops, idxs):
    def every(f):
        for i in range(len(values)):
            last = f(i)
        link(last)

    every(lambda i: dve.max(out=tops[i][:, 0:8], in_=values[i]))
    every(lambda i: dve.max_index(out=idxs[i][:, 0:8], in_max=tops[i][:, 0:8], in_values=values[i]))
    every(lambda i: dve.match_replace(out=values[i], in_to_replace=tops[i][:, 0:8], in_values=values[i],
                                      imm_value=-3.4e38))
    every(lambda i: dve.max(out=tops[i][:, 8:16], in_=values[i]))
    every(lambda i: dve.max_index(out=idxs[i][:, 8:16], in_max=tops[i][:, 8:16], in_values=values[i]))


def stage_query(nc, s, io):
    at = s.at
    f0 = 14000
    QW = 256
    NQ = PH * 2
    ring = at("q_ring", f0, [P, 3, DC, QW])
    keys = at("keys", f0 + 6144, [P, NQ, P])
    keysT = at("keysT", f0 + 8192, [P, NQ, P])
    qt = at("q_T", f0 + 10240, [P, 4, T])
    sc = at("key_scores", f0 + 12416, [P, NT, NQ, PK])
    s.top1 = top1 = at("top1", f0 + 22656, [P, NT, NQ, TOPK])
    s.idx1 = idx1 = at("idx1", f0 + 23936, [P, NT, NQ, TOPK], U32)
    sem = Semaphores(nc)
    with ExitStack() as ctx:
        w_in, keys_in, kt_psum, kt_done = [sem(f"q_w{i}") for i in range(3)], sem("keys_in"), sem("kt_psum"), sem("kt_done")
        q_psum, q_done, sc_psum, sc_done = sem("q_psum"), sem("q_done"), sem("ksc_psum"), sem("ksc_done")
        chain = sem("q_chain")
        ps = ctx.enter_context(nc.psum_tensor("ps_q", [P, 8, 512], F32))
        block = ctx.enter_context(nc.Block())

        @block.sync
        def _(sp):
            sp.dma_start(keys[:, :, :], io.peer_keys.rearrange("h c n d -> n (h c) d")).then_inc(keys_in, 16)
            for q in range(NQ // 2):
                if q >= 3:
                    sp.wait_ge(q_psum, 4 * (q - 2))
                sp.dma_start(ring[:, q % 3, :, :], io.peer_wq[:, q * QW:(q + 1) * QW].rearrange("(c p) n -> p c n", p=P))\
                  .then_inc(w_in[q % 3], 16)

        @block.tensor
        def _(pe):
            pe.wait_ge(keys_in, 16)
            for n in range(4):
                for c in range(4):
                    last = pe.transpose(ps[:, 4 + n, c * P:(c + 1) * P], keys[:, 4 * n + c, :], s.ident[:, :])
                last.then_inc(kt_psum, 1)

            def score(grp):
                pe.wait_ge(q_done, 8 * (grp + 1))
                pe.wait_ge(kt_done, 4)
                for t in range(NT):
                    n = NT * grp + t
                    if n >= 4:
                        pe.wait_ge(sc_done, n - 3)
                    for c in range(4):
                        last = pe.matmul(ps[0:ROWS[t], 4 + n % 4, c * P:(c + 1) * P], qt[:, c, t * P:t * P + ROWS[t]],
                                         keysT[:, 4 * grp + c, :], start=True, stop=True)
                    last.then_inc(sc_psum, 1)

            for x in range(NQ):
                if x % 2 == 0:
                    pe.wait_ge(w_in[(x // 2) % 3], 16 * (x // 6 + 1))
                for half in range(2):
                    u = 2 * x + half
                    if u >= 4:
                        pe.wait_ge(q_done, u - 3)
                    for dc in range(DC):
                        last = pe.matmul(ps[:, u % 4, 0:HALF], ring[:, (x // 2) % 3, dc, (x % 2) * P:(x % 2 + 1) * P],
                                         s.hT[:, dc, half * HALF:(half + 1) * HALF], start=(dc == 0), stop=(dc == DC - 1))
                    last.then_inc(q_psum, 1)
                if x % 4 == 3:
                    score(x // 4)

        @block.scalar
        def _(act):
            for u in range(2 * NQ):
                act.wait_ge(q_psum, u + 1)
                x = u // 2
                if x >= 4:
                    act.wait_ge(sc_psum, NT * (x // 4))
                act.copy(qt[:, x % 4, (u % 2) * HALF:(u % 2 + 1) * HALF], ps[:, u % 4, 0:HALF]).then_inc(q_done, 1)
                if u % 8 == 7:
                    grp = u // 8
                    for t in range(NT):
                        n = NT * grp + t
                        act.wait_ge(sc_psum, n + 1)
                        act.copy(sc[0:ROWS[t], t, 4 * grp:4 * grp + 4, :],
                                 ps[0:ROWS[t], 4 + n % 4, :].rearrange("p (c k) -> p c k", c=4)).then_inc(sc_done, 1)

        @block.vector
        def _(dve):
            step = Count()

            def link(ins):
                ins.then_inc(chain, 1)
                dve.wait_ge(chain, step.add())

            for n in range(4):
                dve.wait_ge(kt_psum, n + 1)
                dve.tensor_copy(keysT[:, 4 * n:4 * n + 4, :], ps[:, 4 + n, :].rearrange("p (c k) -> p c k", c=4))\
                   .then_inc(kt_done, 1)
            for n in range(NT * NQ // 4):
                grp, t = n // NT, n % NT
                r = ROWS[t]
                dve.wait_ge(sc_done, n + 1)
                xs = range(4 * grp, 4 * grp + 4)
                top_two(dve, link, [sc[0:r, t, x, :] for x in xs], [top1[0:r, t, x, :] for x in xs],
                        [idx1[0:r, t, x, :] for x in xs])
    sem.clear()


def stage_select(nc, s, io):
    at = s.at
    s.chosen = chosen = at("chosen", 14000, [P, 3, T])
    b0 = 39216 + 8
    cand = at("cand", b0, [P, PH, TOPK, TOPK])
    oh = at("oh", b0 + 2048, [P, 2, PH, TOPK, TOPK])
    top2 = at("top2", b0 + 6144, [P, PH, TOPK])
    idx2 = at("idx2", b0 + 6272, [P, PH, TOPK], U32)
    part = at("part", b0 + 6400, [P, 2, PH, TOPK], U32)
    partf = at("partf", b0 + 6656, [P, 2, PH, TOPK])
    idxf = at("idxf", b0 + 6912, [P, PH, 2, TOPK])
    res = at("res", b0 + 7168, [P, 2, 3, PH, TOPK])
    sums = at("sums", b0 + 7936, [P, PH])
    i16 = at("i16", b0 + 7952, [P, TOPK])
    sem = Semaphores(nc)
    with ExitStack() as ctx:
        chain, i_ready, e_in, e_done, res_ready, r_psum, r_done = (sem("sel_chain"), sem("sel_iota"), sem("sel_ein"),
                                                                  sem("sel_edone"), sem("sel_res"), sem("sel_psum"),
                                                                  sem("sel_done"))
        ps = ctx.enter_context(nc.psum_tensor("ps_e", [P, 8, 512], F32))
        block = ctx.enter_context(nc.Block())

        @block.gpsimd
        def _(pool):
            pool.iota(i16[:, :], pattern=[[1, TOPK]], base=0, channel_multiplier=0,
                      allow_small_or_imprecise_dtypes=True).then_inc(i_ready, 1)

        @block.tensor
        def _(pe):
            for t in range(NT):
                r = ROWS[t]
                pe.wait_ge(res_ready, t + 1)
                if t >= 2:
                    pe.wait_ge(r_done, t - 1)
                for i in range(3):
                    last = pe.transpose(ps[:, t % 2, i * P:i * P + r],
                                        res[0:r, t % 2, i, :, :].rearrange("p h k -> p (h k)"), s.ident[0:r, 0:r])
                last.then_inc(r_psum, 1)

        @block.scalar
        def _(act):
            for t in range(NT):
                r = ROWS[t]
                act.wait_ge(e_in, t + 1)
                act.activation(res[0:r, t % 2, 0, :, :], res[0:r, t % 2, 0, :, :], ACT.Exp).then_inc(e_done, 1)
                act.wait_ge(r_psum, t + 1)
                act.copy(chosen[:, :, t * P:t * P + r],
                         ps[:, t % 2, 0:384].rearrange("p (i t) -> p i t", i=3)[:, :, 0:r]).then_inc(r_done, 1)

        @block.vector
        def _(dve):
            step = Count()

            def link(ins):
                ins.then_inc(chain, 1)
                dve.wait_ge(chain, step.add())

            dve.wait_ge(i_ready, 1)
            for t in range(NT):
                r = ROWS[t]
                full = [r, PH, TOPK, TOPK]
                v = s.top1[0:r, t, :, :].rearrange("p (h c) k -> p h c k", c=2)
                link(dve.tensor_tensor(cand[0:r, :, :, :], v[:, :, 0, :].unsqueeze(3).broadcast_to(full),
                                       v[:, :, 1, :].unsqueeze(2).broadcast_to(full), ALU.add))
                lists = cand[0:r, :, :, :].rearrange("p h a b -> p h (a b)")
                top_two(dve, link, [lists[:, h, :] for h in range(PH)], [top2[0:r, h, :] for h in range(PH)],
                        [idx2[0:r, h, :] for h in range(PH)])
                if t >= 2:
                    dve.wait_ge(r_psum, t - 1)
                dve.tensor_tensor(res[0:r, t % 2, 0, :, :], top2[0:r, :, :],
                                  top2[0:r, :, 0:1].broadcast_to([r, PH, TOPK]), ALU.subtract).then_inc(e_in, 1)
                dve.tensor_scalar(part[0:r, 0, :, :], idx2[0:r, :, :], 4, None, ALU.logical_shift_right)
                dve.tensor_scalar(part[0:r, 1, :, :], idx2[0:r, :, :], 15, None, ALU.bitwise_and)
                link(dve.tensor_copy(idxf[0:r, :, :, :].rearrange("p h c k -> p (h c) k"), s.idx1[0:r, t, :, :]))
                link(dve.tensor_copy(partf[0:r, :, :, :], part[0:r, :, :, :]))
                for c in range(2):
                    last = dve.tensor_tensor(oh[0:r, c, :, :, :], partf[0:r, c, :, :].unsqueeze(3).broadcast_to(full),
                                             i16[0:r, :].unsqueeze(1).unsqueeze(1).broadcast_to(full), ALU.is_equal)
                link(last)
                for c in range(2):
                    last = dve.tensor_tensor(oh[0:r, c, :, :, :], oh[0:r, c, :, :, :],
                                             idxf[0:r, :, c, :].unsqueeze(2).broadcast_to(full), ALU.mult)
                link(last)
                for c in range(2):
                    dve.tensor_reduce(res[0:r, t % 2, 1 + c, :, :], oh[0:r, c, :, :, :], AX.X, ALU.add)
                dve.wait_ge(e_done, t + 1)
                link(dve.tensor_reduce(sums[0:r, :], res[0:r, t % 2, 0, :, :], AX.X, ALU.add))
                link(dve.reciprocal(sums[0:r, :], sums[0:r, :]))
                dve.tensor_tensor(res[0:r, t % 2, 0, :, :], res[0:r, t % 2, 0, :, :],
                                  sums[0:r, :].unsqueeze(2).broadcast_to([r, PH, TOPK]), ALU.mult).then_inc(res_ready, 1)
    sem.clear()


TB = 32
GJ = 4
NG = PK // GJ


def stage_gates(nc, s, io):
    at = s.at
    c0 = 15632
    cols = at("g_cols", c0, [P, 3, TB])
    one_a = at("one_a", c0 + 96, [P, 2, 4, PK])
    one_b = at("one_b", c0 + 1120, [P, 2, 4, PK])
    i128 = at("i128", c0 + 2144, [P, PK])
    buf = at("g_buf", c0 + 2272, [P, 2, NG, TB, GJ])
    NB = T // TB
    QD = TB // 4
    sem = Semaphores(nc)
    with ExitStack() as ctx:
        i_ready, cols_ready, ab_ready, g_psum, g_done = (sem("gt_iota"), sem("gt_cols"), sem("gt_ab"), sem("gt_psum"),
                                                         sem("gt_done"))
        sent = [sem("gt_sent0"), sem("gt_sent1")]
        ps = ctx.enter_context(nc.psum_tensor("ps_t", [P, 4, 512], F32))
        block = ctx.enter_context(nc.Block())

        def blocks(eng, body):
            body(0, 0, True)
            body(1, 0, True)
            with eng.Fori(1, NB // 2) as i:
                body(0, i, False)
                body(1, i, False)
            body(0, NB // 2, False)

        @block.gpsimd
        def _(pool):
            pool.iota(i128[:, :], pattern=[[1, PK]], base=0, channel_multiplier=0,
                      allow_small_or_imprecise_dtypes=True).then_inc(i_ready, 1)

        @block.vector
        def _(dve):
            dve.wait_ge(i_ready, 1)

            def body(u, i, first):
                if not (first and u == 0):
                    dve.wait_ge(ab_ready, i * (2 * QD) + u * QD)
                dve.tensor_copy(cols[:, :, :], s.chosen[:, :, bass.ds(i * (2 * TB) + u * TB, TB)]).then_inc(cols_ready, 1)
                dve.wait_ge(cols_ready, i * 2 + (u + 1))
                for q in range(QD):
                    if not (first and u == 0 and q < 2):
                        dve.wait_ge(g_psum, i * (2 * QD) + (u * QD + q - 1))
                    for c in range(4):
                        t = 4 * q + c
                        dve.tensor_scalar(one_a[:, q % 2, c, :], i128[:, :], cols[:, 1, t:t + 1], None, ALU.is_equal)
                        last = dve.tensor_scalar(one_b[:, q % 2, c, :], i128[:, :], cols[:, 2, t:t + 1],
                                                 cols[:, 0, t:t + 1], ALU.is_equal, ALU.mult)
                    last.then_inc(ab_ready, 1)

            blocks(dve, body)

        @block.tensor
        def _(pe):
            def body(u, i, first):
                for q in range(QD):
                    pe.wait_ge(ab_ready, i * (2 * QD) + (u * QD + q + 1))
                    if not (first and u == 0 and q < 4):
                        pe.wait_ge(g_done, i * (2 * QD) + (u * QD + q - 3))
                    for c in range(4):
                        last = pe.matmul(ps[:, q % 4, c * P:(c + 1) * P], one_a[:, q % 2, c, :], one_b[:, q % 2, c, :],
                                         start=True, stop=True)
                    last.then_inc(g_psum, 1)

            blocks(pe, body)

        @block.scalar
        def _(act):
            def body(u, i, first):
                if not first:
                    act.wait_ge(sent[u], i * 16)
                for q in range(QD):
                    act.wait_ge(g_psum, i * (2 * QD) + (u * QD + q + 1))
                    act.copy(buf[:, u, :, 4 * q:4 * q + 4, :].rearrange("p g t j -> p t g j"),
                             ps[:, q % 4, :].rearrange("p (t g j) -> p t g j", t=4, j=GJ)).then_inc(g_done, 1)

            blocks(act, body)

        @block.sync
        def _(sp):
            def body(u, i, first):
                sp.wait_ge(g_done, i * (2 * QD) + (u + 1) * QD)
                dst = io.gates[:, :, bass.ds(i * (2 * TB * GJ) + u * TB * GJ, TB * GJ)].rearrange("g p x -> p g x")
                sp.dma_start(dst, buf[:, u, :, :, :].rearrange("p g t j -> p g (t j)")).then_inc(sent[u], 16)

            blocks(sp, body)
            sp.wait_ge(sent[0], 16 * (NB - NB // 2))
            sp.wait_ge(sent[1], 16 * (NB // 2))
    sem.clear()


def stage_experts(nc, s, io):
    at = s.at
    s.outT = outT = at("outT", 9648, [P, DC, T])
    vlo_raw = [at(f"v_raw{i}", 14000 + 4096 * i, [P, GJ, D]) for i in range(2)]
    vlo = [at(f"v_lo{i}", 14000 + 4096 * i, [P, GJ, D], F32R) for i in range(2)]
    vhi = [at(f"v_hi{i}", 22192 + 4096 * i, [P, GJ, D], F32R) for i in range(2)]
    ur = at("u_ring", 30384, [P, GJ, D])
    uhi = at("u_hi", 34480, [P, 2, DC, P], F32R)
    ulo = at("u_lo", 36528, [P, 2, DC, P], F32R)
    ga = at("gelu", 38576, [P, 2, HALF])
    wt = at("e_w", 39120, [P, 2, HALF])
    whi = at("e_whi", 39664, [P, 2, GJ, T], F32R)
    wlo = at("e_wlo", 44016, [P, 2, GJ, T], F32R)
    gt = at("e_gate", 48368, [P, 2, T, GJ])
    hTh, hTl = s.hTh, s.hTl
    u_v = io.peer_u.rearrange("(a b) d -> a b d", a=PK)
    v_v = io.peer_v.rearrange("(a b) d -> a b d", a=PK)
    sem = Semaphores(nc)
    with ExitStack() as ctx:
        u_in = [sem(f"u_in{i}") for i in range(GJ)]
        v_in = [sem(f"v_in{i}") for i in range(2)]
        g_in = [sem(f"g_in{i}") for i in range(2)]
        ut_psum, uh_done, ul_done, h_psum, gelu_done, w_done = (sem("ut_psum"), sem("uh_done"), sem("ul_done"),
                                                               sem("eh_psum"), sem("gelu_done"), sem("w_done"))
        wh_in, w_mul = sem("wh_in"), sem("w_mul")
        vh_done, vl_done, o_psum, o_done, zeroed = sem("vh_done"), sem("vl_done"), sem("eo_psum"), sem("eo_done"), sem("zeroed")
        ps = ctx.enter_context(nc.psum_tensor("ps_ex", [P, 8, 512], F32))
        block = ctx.enter_context(nc.Block())
        NO = 2 * DC

        def groups(eng, body):
            body(0, 0, True)
            body(1, 0, False)
            with eng.Fori(1, NG // 2) as i:
                body(0, i, None)
                body(1, i, None)

        def count(i, u, per_group, c):
            return i * (2 * per_group) + (u * per_group + c)

        @block.sync
        def _(sp):
            def body(u, i, first):
                for c in range(GJ):
                    if not (first is True):
                        sp.wait_ge(ut_psum, count(i, u, 2 * GJ, 2 * c + 2 - 2 * GJ))
                    src = u_v[:, bass.ds(i * (2 * GJ) + (u * GJ + c), 1), :].rearrange("a o d -> a (o d)")
                    sp.dma_start(ur[:, c, :], src).then_inc(u_in[c], 16)

            groups(sp, body)

        @block.gpsimd
        def _(pool):
            def body(u, i, first):
                if first is None:
                    pool.wait_ge(w_mul, count(i, u, 2 * GJ, -2 * GJ))
                src = io.gates[bass.ds(i * 2 + u, 1)].rearrange("o p x -> (o p) x")
                pool.dma_start(gt[:, u, :, :].rearrange("p t j -> p (t j)"), src).then_inc(g_in[u], 16)
                if first is None:
                    pool.wait_ge(o_psum, count(i, u, NO, -NO))
                src = v_v[:, bass.ds(i * (2 * GJ) + u * GJ, GJ), :]
                pool.dma_start(vlo_raw[u][:, :, :], src).then_inc(v_in[u], 16)

            groups(pool, body)

        @block.tensor
        def _(pe):
            def turn(u, c, i, first):
                pe.wait_ge(u_in[c], i * 32 + 16 * (u + 1))
                for b in range(2):
                    if not (first is True and c == 0):
                        pe.wait_ge(ul_done, count(i, u, 2 * GJ, 2 * c + b - 1))
                    for q in range(4):
                        dc = 4 * b + q
                        last = pe.transpose(ps[:, b, q * P:(q + 1) * P], ur[:, c, dc * P:(dc + 1) * P], s.ident[:, :])
                    last.then_inc(ut_psum, 1)

            def hidden(u, c, i, first):
                pe.wait_ge(ul_done, count(i, u, 2 * GJ, 2 * c + 2))
                for half in range(2):
                    if not (first is True and c < 2):
                        pe.wait_ge(gelu_done, count(i, u, 2 * GJ, 2 * c + half - 3))
                    out = ps[:, 2 + 2 * (c % 2) + half, 0:HALF]
                    cols = slice(half * HALF, (half + 1) * HALF)
                    for dc in range(DC):
                        pe.matmul(out, uhi[:, c % 2, dc, :], hTh[:, dc, cols], start=(dc == 0), stop=False)
                        pe.matmul(out, uhi[:, c % 2, dc, :], hTl[:, dc, cols], start=False, stop=False)
                    for dc in range(DC):
                        last = pe.matmul(out, ulo[:, c % 2, dc, :], hTh[:, dc, cols], start=False, stop=(dc == DC - 1))
                    last.then_inc(h_psum, 1)

            def outputs(u, i, first_units):
                pe.wait_ge(w_done, count(i, u, 2 * GJ, 2 * GJ))
                pe.wait_ge(vl_done, count(i, u, GJ, GJ))
                for n in range(NO):
                    dc, half = n // 2, n % 2
                    if not (first_units and n < 2):
                        pe.wait_ge(o_done, count(i, u, NO, n - 1))
                    out = ps[:, 6 + n % 2, 0:HALF]
                    cols, rows = slice(half * HALF, (half + 1) * HALF), slice(dc * P, (dc + 1) * P)
                    for c in range(GJ):
                        pe.matmul(out, vhi[u][:, c, rows], whi[:, u, c, cols], start=(c == 0), stop=False)
                        pe.matmul(out, vhi[u][:, c, rows], wlo[:, u, c, cols], start=False, stop=False)
                        last = pe.matmul(out, vlo[u][:, c, rows], whi[:, u, c, cols], start=False, stop=(c == GJ - 1))
                    last.then_inc(o_psum, 1)

            def body(u, i, first):
                for c in range(GJ):
                    if first is True and c == 0:
                        turn(u, 0, i, first)
                    if c < GJ - 1:
                        turn(u, c + 1, i, first)
                    elif u == 0:
                        turn(1, 0, i, False)
                    else:
                        turn_next(i)
                    hidden(u, c, i, first)
                    if c == 0 and first is not True:
                        outputs(1 - u, i if u == 1 else i - 1, first is False)

            def turn_next(i):
                if isinstance(i, int):
                    turn(0, 0, i + 1, False)
                    return
                turn(0, 0, i + 1, False)

            body(0, 0, True)
            body(1, 0, False)
            with pe.Fori(1, NG // 2 - 1) as i:
                body(0, i, None)
                body(1, i, None)
            last_pair = NG // 2 - 1
            body(0, last_pair, None)
            for c in range(GJ):
                if c < GJ - 1:
                    turn(1, c + 1, last_pair, None)
                hidden(1, c, last_pair, None)
                if c == 0:
                    outputs(0, last_pair, False)
            outputs(1, last_pair, False)

        @block.scalar
        def _(act):
            def high(u, c, i, first):
                for b in range(2):
                    act.wait_ge(ut_psum, count(i, u, 2 * GJ, 2 * c + b + 1))
                    if not (first is True and c < 2) and b == 0:
                        act.wait_ge(h_psum, count(i, u, 2 * GJ, 2 * c - 2))
                    act.copy(uhi[:, c % 2, 4 * b:4 * b + 4, :].rearrange("p c e -> p (c e)"), ps[:, b, :])\
                       .then_inc(uh_done, 1)

            def body(u, i, first):
                act.wait_ge(v_in[u], i * 16 + 16)
                for c in range(GJ):
                    high(u, c, i, first)
                    for half in range(2):
                        act.wait_ge(h_psum, count(i, u, 2 * GJ, 2 * c + half + 1))
                        if not (first is True and c == 0):
                            act.wait_ge(w_mul, count(i, u, 2 * GJ, 2 * c + half - 1))
                        act.activation(ga[:, half, :], ps[:, 2 + 2 * (c % 2) + half, 0:HALF], ACT.Gelu)\
                           .then_inc(gelu_done, 1)
                    if c == 0 and first is None:
                        act.wait_ge(o_psum, count(i, u, NO, -NO))
                    act.copy(vhi[u][:, c, :], vlo_raw[u][:, c, :]).then_inc(vh_done, 1)

            groups(act, body)

        @block.vector
        def _(dve):
            dve.memset(outT[:, :, :], 0.0).then_inc(zeroed, 1)
            dve.wait_ge(zeroed, 1)

            def low(u, c, i):
                for b in range(2):
                    dve.wait_ge(uh_done, count(i, u, 2 * GJ, 2 * c + b + 1))
                    dve.tensor_tensor(ulo[:, c % 2, 4 * b:4 * b + 4, :].rearrange("p c e -> p (c e)"), ps[:, b, :],
                                      uhi[:, c % 2, 4 * b:4 * b + 4, :].rearrange("p c e -> p (c e)").bitcast(F32),
                                      ALU.subtract).then_inc(ul_done, 1)

            def gather(u, i):
                for n in range(NO):
                    dc, half = n // 2, n % 2
                    dve.wait_ge(o_psum, count(i, u, NO, n + 1))
                    x = outT[:, dc, half * HALF:(half + 1) * HALF]
                    dve.tensor_tensor(x, x, ps[:, 6 + n % 2, 0:HALF], ALU.add).then_inc(o_done, 1)

            def body(u, i, first):
                dve.wait_ge(g_in[u], i * 16 + 16)
                for c in range(GJ):
                    low(u, c, i)
                    for half in range(2):
                        cols = slice(half * HALF, (half + 1) * HALF)
                        dve.wait_ge(gelu_done, count(i, u, 2 * GJ, 2 * c + half + 1))
                        if c == 0 and half == 0 and first is None:
                            dve.wait_ge(o_psum, count(i, u, NO, -NO))
                        dve.tensor_tensor(wt[:, half, :], ga[:, half, :], gt[:, u, cols, c], ALU.mult)\
                           .then_inc(w_mul, 1)
                        dve.wait_ge(w_mul, count(i, u, 2 * GJ, 2 * c + half + 1))
                        dve.tensor_copy(whi[:, u, c, cols], wt[:, half, :]).then_inc(wh_in, 1)
                        dve.wait_ge(wh_in, count(i, u, 2 * GJ, 2 * c + half + 1))
                        dve.tensor_tensor(wlo[:, u, c, cols], wt[:, half, :], whi[:, u, c, cols].bitcast(F32),
                                          ALU.subtract).then_inc(w_done, 1)
                    dve.wait_ge(vh_done, count(i, u, GJ, c + 1))
                    dve.tensor_tensor(vlo[u][:, c, :], vlo_raw[u][:, c, :], vhi[u][:, c, :].bitcast(F32), ALU.subtract)\
                       .then_inc(vl_done, 1)
                    if c == 0 and first is not True:
                        gather(1 - u, i if u == 1 else i - 1)

            groups(dve, body)
            gather(1, NG // 2 - 1)
    sem.clear()


def stage_norm2(nc, s, io):
    at = s.at
    hr = at("h2", 14000, [P, 2, D])
    yr = at("y2", 16048, [P, 2, D])
    gb = at("ln2_gb", 18096, [P, 2, D])
    st = at("ln2_st", 20144, [P, 2, 6])
    mv = at("ln2_mv", 20160, [P, 2])
    rs = at("ln2_rs", 20168, [P, 2])
    sem = Semaphores(nc)
    with ExitStack() as ctx:
        h_in, gb_in, t_psum, t_read, chain, eps_done, sqrt_done = ([sem("y_h0"), sem("y_h1")], sem("y_gb"), sem("y_tp"),
                                                                  sem("y_read"), sem("y_chain"), sem("y_eps"), sem("y_sqrt"))
        y_ready, y_sent = sem("y_ready"), [sem("y_sent0"), sem("y_sent1")]
        ps = ctx.enter_context(nc.psum_tensor("ps_y", [P, 8, 512], F32))
        block = ctx.enter_context(nc.Block())

        @block.sync
        def _(sp):
            sp.dma_start(gb[:, 0, :], io.ln2_g.partition_broadcast(P)).then_inc(gb_in, 16)
            sp.dma_start(gb[:, 1, :], io.ln2_b.partition_broadcast(P)).then_inc(gb_in, 16)
            for t in range(NT):
                if t >= 2:
                    sp.wait_ge(t_read, t - 1)
                sp.dma_start(hr[0:ROWS[t], t % 2, :], io.h_rows[t * P:t * P + ROWS[t], :]).then_inc(h_in[t % 2], 16)

        @block.gpsimd
        def _(pool):
            for t in range(NT):
                pool.wait_ge(y_ready, t + 1)
                out = io.y_prompt[0, t * P:(t + 1) * P, :] if t < 4 else io.y_sample.rearrange("b t d -> (b t) d")
                pool.dma_start(out, yr[0:ROWS[t], t % 2, :]).then_inc(y_sent[t % 2], 16)
            pool.wait_ge(y_sent[0], 48)
            pool.wait_ge(y_sent[1], 32)

        @block.tensor
        def _(pe):
            for t in range(NT):
                if t >= 2:
                    pe.wait_ge(t_read, t - 1)
                for dc in range(DC):
                    b, q = 2 * (t % 2) + dc // 4, dc % 4
                    last = pe.transpose(ps[0:ROWS[t], b, q * P:(q + 1) * P], s.outT[:, dc, t * P:t * P + ROWS[t]],
                                        s.ident[:, :])
                last.then_inc(t_psum, 1)

        @block.scalar
        def _(act):
            for t in range(NT):
                act.wait_ge(eps_done, t + 1)
                act.activation(rs[0:ROWS[t], 0:1], rs[0:ROWS[t], 0:1], ACT.Sqrt).then_inc(sqrt_done, 1)

        @block.vector
        def _(dve):
            step = Count()

            def link(ins):
                ins.then_inc(chain, 1)
                dve.wait_ge(chain, step.add())

            dve.wait_ge(gb_in, 32)
            for t in range(NT):
                r = ROWS[t]
                dve.wait_ge(t_psum, t + 1)
                dve.wait_ge(h_in[t % 2], 16 * (t // 2 + 1))
                if t >= 2:
                    dve.wait_ge(y_sent[t % 2], 16 * (t // 2))
                for q in range(2):
                    last = dve.scalar_tensor_tensor(out=yr[0:r, t % 2, q * 512:(q + 1) * 512],
                                                    in0=hr[0:r, t % 2, q * 512:(q + 1) * 512], scalar=DN_ALPHA,
                                                    in1=ps[0:r, 2 * (t % 2) + q, :], op0=ALU.mult, op1=ALU.add)
                last.then_inc(t_read, 1)
                dve.wait_ge(t_read, t + 1)
                norm_rows(dve, link, yr[0:r, t % 2, :], st, mv, rs, eps_done, sqrt_done, t, gb[:, 0, :], gb[:, 1, :], r)\
                    .then_inc(y_ready, 1)
    sem.clear()


OUTS = [("y_prompt", (1, TP, D)), ("y_sample", (DB, DS, D)),
        ("p_cmp", (1, TP, 2, KV, HD)), ("p_slc", (1, TP, 2, KV, HD)), ("p_win", (1, TP, 2, KV, HD)),
        ("p_C", (1, AH, DQK, DV)), ("p_n", (1, AH, DQK)), ("p_m", (1, AH)),
        ("s_cmp", (DB, DS, 2, KV, HD)), ("s_slc", (DB, DS, 2, KV, HD)), ("s_win", (DB, PAST, 2, KV, HD)),
        ("s_C", (DB, AH, DQK, DV)), ("s_n", (DB, AH, DQK)), ("s_m", (DB, AH))]
STAGES = [stage_load, stage_project, stage_mlstm, stage_compress, stage_attend_prompt, stage_attend_samples,
          stage_merge, stage_norm1, stage_query, stage_select, stage_gates, stage_experts, stage_norm2]


def program(nc, tensors):
    io = Names()
    io.x_prompt = tensors["x_prompt"]
    io.x_sample = tensors["x_sample"]
    io.cache_cmp_kv = tensors["cache_cmp_kv"]
    io.cache_slc_kv = tensors["cache_slc_kv"]
    io.cache_win_kv = tensors["cache_win_kv"]
    io.state_C = tensors["state_C"]
    io.state_n = tensors["state_n"]
    io.state_m = tensors["state_m"]
    io.page_table = tensors["page_table"]
    io.w_in = tensors["w_in"]
    io.b_in = tensors["b_in"]
    io.norm_a_g = tensors["norm_a_g"]
    io.nsa_pe = tensors["nsa_pe"]
    io.nsa_w_cmp = tensors["nsa_w_cmp"]
    io.w_br_a = tensors["w_br_a"]
    io.w_br_b = tensors["w_br_b"]
    io.w_merge = tensors["w_merge"]
    io.w_out = tensors["w_out"]
    io.ln1_g = tensors["ln1_g"]
    io.ln1_b = tensors["ln1_b"]
    io.peer_wq = tensors["peer_wq"]
    io.peer_keys = tensors["peer_keys"]
    io.peer_u = tensors["peer_u"]
    io.peer_v = tensors["peer_v"]
    io.ln2_g = tensors["ln2_g"]
    io.ln2_b = tensors["ln2_b"]
    io.y_prompt = tensors["y_prompt"]
    io.y_sample = tensors["y_sample"]
    io.p_cmp = tensors["p_cmp"]
    io.p_slc = tensors["p_slc"]
    io.p_win = tensors["p_win"]
    io.p_C = tensors["p_C"]
    io.p_n = tensors["p_n"]
    io.p_m = tensors["p_m"]
    io.s_cmp = tensors["s_cmp"]
    io.s_slc = tensors["s_slc"]
    io.s_win = tensors["s_win"]
    io.s_C = tensors["s_C"]
    io.s_n = tensors["s_n"]
    io.s_m = tensors["s_m"]
    s = place(nc)
    io.h_rows = nc.dram_tensor("h_rows", (T, D), F32, kind="Internal").ap()
    io.gates = nc.dram_tensor("gate_tables", (NG, P, T * GJ), F32, kind="Internal").ap()
    with ExitStack() as ctx:
        s.wo_in = ctx.enter_context(nc.semaphore("wo_in"))
        for stage in STAGES:
            stage(nc, s, io)


def kernel(**inputs):
    import concourse.bacc as bacc
    from concourse.bass_utils import run_bass_kernel_spmd

    nc = bacc.Bacc("TRN2", target_bir_lowering=False, num_devices=1)
    arrays, tensors = {}, {}
    for name, a in inputs.items():
        a = np.ascontiguousarray(a)
        arrays[f"in_{name}"] = a
        tensors[name] = nc.dram_tensor(f"in_{name}", a.shape, mybir.dt.from_np(a.dtype), kind="ExternalInput").ap()
    for name, shape in OUTS:
        tensors[name] = nc.dram_tensor(f"out_{name}", shape, F32, kind="ExternalOutput").ap()
    program(nc, tensors)
    r = run_bass_kernel_spmd(nc, [arrays], core_ids=[0])
    return tuple(r.results[0][f"out_{name}"] for name, _ in OUTS)
```

```python
from contextlib import ExitStack

import numpy as np

import concourse.bass as bass
from concourse import mybir

ALU = mybir.AluOpType
ACT = mybir.ActivationFunctionType
AX = mybir.AxisListType
F32 = mybir.dt.float32
F32R = mybir.dt.float32r
I32 = mybir.dt.int32
U32 = mybir.dt.uint32

P = 128
D = 1024
DC = D // P
TP = 512
DB, DS = 8, 4
TS = DB * DS
T = TP + TS
NT = 5
ROWS = [P] * 4 + [TS]
HALF = T // 2
PAST = 256
PAGE = 128
NPG = PAST // PAGE

AH, DQK, DV = 4, 128, 256
BH, KV, REP, HD = 16, 4, 4, 64
CB = 64
PH, PK, TOPK = 8, 128, 16
DN_ALPHA = 2.0 ** 0.25
LN_EPS = 1e-5
BIG = 1e34

SLOPES = [2.0 ** (-8.0 * (h + 1) / BH) for h in range(BH)]

SB0 = 16512


class Names:
    pass


class Count:

    def __init__(self):
        self.n = 0

    def add(self, k=1):
        self.n += k
        return self.n


class Semaphores:

    def __init__(self, nc):
        self.nc, self.made = nc, []

    def __call__(self, name):
        self.made.append(self.nc.alloc_semaphore(name))
        return self.made[-1]

    def clear(self):
        self.nc.clear_and_free_semaphores(self.made)
        self.nc.all_engine_barrier()


def place(nc):

    def at(name, off, shape, dt=F32):
        return nc.alloc_sbuf_tensor_at(name, shape, dt, offset=SB0 + 4 * off)

    s = Names()
    s.at = at
    s.ident = at("ident", 0, [P, P])
    s.ones = at("ones", 128, [P, P])
    s.upper = at("upper", 256, [P, P])
    s.pairs = at("pairs", 384, [TS, TS])
    s.member = at("member", 416, [TS, DB])
    s.head_row = at("head_row", 424, [AH, AH, P])
    s.xT = at("xT", 1280, [P, DC, T])
    s.bqT = at("bqT", 5632, [HD, BH, T])
    s.kslT = at("kslT", 14336, [HD, KV, T])
    s.kwiT = at("kwiT", 16512, [HD, KV, T])
    s.cmpT = at("cmpT", 18688, [HD, 2, 33, CB])
    s.vsl = at("vsl", 22912, [P, NT, KV * HD])
    s.vwi = at("vwi", 24192, [P, NT, KV * HD])
    s.gat = at("gat", 25472, [P, NT, 48])
    s.qT = at("qT", 25728, [P, AH, T])
    s.kT = at("kT", 27904, [P, AH, T])
    s.kn = at("kn", 30080, [P, NT, AH * DQK])
    s.vn = at("vn", 32640, [P, NT, AH, DV + 1])
    s.ifn = at("ifn", 37784, [P, NT, 8])
    s.on = at("on", 37848, [P, NT, AH * DV])
    s.yaT = at("yaT", 32640, [P, DC, T])
    s.free = 42968
    return s


def stage_load(nc, s, io):
    at = s.at
    xn = at("xn", 5632, [P, NT, D])
    sem = Semaphores(nc)
    with ExitStack() as ctx:
        x_in = [sem(f"x_in{i}") for i in range(NT)]
        const_step = sem("const_step")
        ident_ready = sem("ident_ready")
        xt_psum = sem("xt_psum")
        xt_even = sem("xt_even")
        xt_odd = sem("xt_odd")
        ps = ctx.enter_context(nc.psum_tensor("ps_x", [P, 8, 512], F32))
        block = ctx.enter_context(nc.Block())

        @block.sync
        def _(sp):
            for i in range(4):
                sp.dma_start(xn[:, i, :], io.x_prompt[0, i * P:(i + 1) * P, :]).then_inc(x_in[i], 16)
            sp.dma_start(xn[0:TS, 4, :], io.x_sample.rearrange("b t d -> (b t) d")).then_inc(x_in[4], 16)

        @block.gpsimd
        def _(pool):
            step = Count()

            def link(ins):
                ins.then_inc(const_step, 1)
                pool.wait_ge(const_step, step.add())

            pool.memset(s.ones[:, :], 1.0)
            link(pool.memset(s.ident[:, :], 0.0))
            pool.affine_select(out=s.ident[:, :], in_=s.ident[:, :], compare_op=ALU.not_equal, fill=1.0, base=0,
                               pattern=[[-1, P]], channel_multiplier=1).then_inc(ident_ready, 1)
            link(pool.affine_select(out=s.upper[:, :], in_=s.ones[:, :], compare_op=ALU.is_ge, fill=0.0, base=0,
                                    pattern=[[1, P]], channel_multiplier=-1))
            pr = s.pairs[:, :].rearrange("s (b t) -> s b t", b=DB)
            link(pool.affine_select(out=pr, in_=s.ones[0:TS, 0:TS].rearrange("s (b t) -> s b t", b=DB),
                                    compare_op=ALU.is_ge, fill=0.0, base=0,
                                    pattern=[[-DS, DB], [0, DS]], channel_multiplier=1))
            link(pool.affine_select(out=pr, in_=pr, compare_op=ALU.is_ge, fill=0.0, base=0,
                                    pattern=[[DS, DB], [1, DS]], channel_multiplier=-1))
            link(pool.affine_select(out=s.member[:, :], in_=s.ones[0:TS, 0:DB], compare_op=ALU.is_ge, fill=0.0,
                                    base=0, pattern=[[-DS, DB]], channel_multiplier=1))
            link(pool.affine_select(out=s.member[:, :], in_=s.member[:, :], compare_op=ALU.is_ge, fill=0.0,
                                    base=DS - 1, pattern=[[DS, DB]], channel_multiplier=-1))
            for h in range(AH):
                link(pool.affine_select(out=s.head_row[:, h, :], in_=s.ones[0:AH, :], compare_op=ALU.is_equal,
                                        fill=0.0, base=-h, pattern=[[0, P]], channel_multiplier=1))

        @block.tensor
        def _(pe):
            pe.wait_ge(ident_ready, 1)
            for n in range(2 * NT):
                i, rows = n // 2, ROWS[n // 2]
                if n % 2 == 0:
                    pe.wait_ge(x_in[i], 16)
                if n >= 8:
                    pe.wait_ge([xt_even, xt_odd][n % 2], (n - 8) // 2 + 1)
                for c in range(4):
                    dc = 4 * (n % 2) + c
                    last = pe.transpose(ps[:, n % 8, c * P:c * P + rows], xn[0:rows, i, dc * P:(dc + 1) * P],
                                        s.ident[0:rows, 0:rows])
                last.then_inc(xt_psum, 1)

        def evacuate(eng, copy, parity, done):
            for n in range(parity, 2 * NT, 2):
                i, rows = n // 2, ROWS[n // 2]
                eng.wait_ge(xt_psum, n + 1)
                src = ps[:, n % 8, :].rearrange("p (c t) -> p c t", c=4)[:, :, 0:rows]
                copy(s.xT[:, 4 * parity:4 * parity + 4, i * P:i * P + rows], src).then_inc(done, 1)

        @block.vector
        def _(dve):
            evacuate(dve, dve.tensor_copy, 0, xt_even)

        @block.scalar
        def _(act):
            evacuate(act, act.copy, 1, xt_odd)
    sem.clear()


COLS = ([("q", 0, 512), ("k", 512, 512), ("v", 1024, 512), ("v", 1536, 512), ("if", 2048, 8),
         ("o", 2056, 512), ("o", 2568, 512), ("bq", 3080, 512), ("bq", 3592, 512),
         ("cmp", 4104, 512), ("slc", 4616, 512), ("win", 5128, 512), ("gate", 5640, 48)])
NCB = len(COLS)
TURNS = {"q": 1, "k": 1, "bq": 2, "cmp": 2, "slc": 1, "win": 1}
STAGED = {"q", "o", "bq", "cmp", "slc", "win"}
OUTPUT = {"o", "cmp", "slc", "win"}
GC = 2
NGR = DC // GC


def stage_project(nc, s, io):
    at = s.at
    f0 = 37848
    xTh = at("xT_hi", f0, [P, DC, T], F32R)
    xTl = at("xT_lo", f0 + 4352, [P, DC, T], F32R)
    w_raw = at("w_raw", f0 + 8704, [P, 3, GC, 512])
    w_lo = at("w_lo", f0 + 8704, [P, 3, GC, 512], F32R)
    w_hi = at("w_hi", f0 + 11776, [P, 2, GC, 512], F32R)
    stage = at("stage", f0 + 13824, [P, 2, 512])
    bias = at("bias", f0 + 14848, [P, 512])
    groups = [(b, t) for b in range(NCB) for t in range(NT)]
    turn_at, staged_at, out_at = {}, {}, {}
    nturn = nst = nout = 0
    for b, t in groups:
        name = COLS[b][0]
        turn_at[b, t] = nturn
        staged_at[b, t] = nst
        out_at[b, t] = nout
        if name in TURNS and not (name == "cmp" and t == 4):
            nturn += TURNS[name]
        if name in STAGED:
            nst += 1
        if name in OUTPUT:
            nout += 1
    staged = [(b, t) for b, t in groups if COLS[b][0] in STAGED]

    def turns(b, t):
        name = COLS[b][0]
        return 0 if name == "cmp" and t == 4 else TURNS.get(name, 0)

    sem = Semaphores(nc)
    with ExitStack() as ctx:
        w_in = [sem(f"w_in{i}") for i in range(3)]
        b_in = sem("bias_in")
        xh_done, xl_done, wh_done, wl_done, load_used = (sem("pj_xh"), sem("pj_xl"), sem("pj_wh"), sem("pj_wl"),
                                                         sem("pj_used"))
        proj_psum = sem("proj_psum")
        proj_done = sem("proj_done")
        turn_psum = sem("turn_psum")
        turn_done = sem("turn_done")
        rows_out = [sem(f"rows_out{i}") for i in range(2)]
        ones_set = sem("ones_set")
        win_copy = sem("win_copy")
        gm = ctx.enter_context(nc.psum_tensor("ps_proj", [P, 6, 512], F32))
        tr = ctx.enter_context(nc.psum_tensor("ps_turn", [P, 2, 512], F32))
        block = ctx.enter_context(nc.Block())

        def wait_used(eng, g):
            b, q = g // NGR, g % NGR
            if q == NGR - 1:
                eng.wait_ge(proj_psum, NT * (b + 1))
            else:
                eng.wait_ge(load_used, (NGR - 1) * b + q + 1)

        @block.sync
        def _(sp):
            for g in range(NCB * NGR):
                b, q = g // NGR, g % NGR
                _, c0, n = COLS[b]
                if g >= 3:
                    wait_used(sp, g - 3)
                src = io.w_in[q * GC * P:(q + 1) * GC * P, c0:c0 + n].rearrange("(c p) n -> p c n", p=P)
                sp.dma_start(w_raw[:, g % 3, :, 0:n], src).then_inc(w_in[g % 3], 16)
                if q == 2:
                    if b:
                        sp.wait_ge(proj_done, NT * b)
                    sp.dma_start(bias[:, 0:n], io.b_in[c0:c0 + n].partition_broadcast(P)).then_inc(b_in, 16)

        @block.tensor
        def _(pe):
            def turn(b, t):
                name, rows = COLS[b][0], ROWS[t]
                if not turns(b, t):
                    return
                pe.wait_ge(proj_done, NT * b + t + 1)
                src = s.kn[:, t, :] if name == "k" else stage[:, staged_at[b, t] % 2, :]
                width = P if name in ("q", "k") else HD
                for i in range(turns(b, t)):
                    r = turn_at[b, t] + i
                    if r >= 2:
                        pe.wait_ge(turn_done, r - 1)
                    for c in range(4):
                        last = pe.transpose(tr[0:width, r % 2, c * P:c * P + rows],
                                            src[0:rows, (4 * i + c) * width:(4 * i + c + 1) * width],
                                            s.ident[0:rows, 0:rows])
                    last.then_inc(turn_psum, 1)

            before = None
            for g in range(NCB * NGR):
                b, q = g // NGR, g % NGR
                n = COLS[b][2]
                if b == 0:
                    pe.wait_ge(xl_done, q + 1)
                pe.wait_ge(wl_done, g + 1)
                for t in range(NT):
                    rows, u = ROWS[t], NT * b + t
                    if q == 0 and u >= 6:
                        pe.wait_ge(proj_done, u - 5)
                    for c in range(GC):
                        toks = slice(t * P, t * P + rows)
                        out, dc = gm[0:rows, u % 6, 0:n], GC * q + c
                        pe.matmul(out, xTh[:, dc, toks], w_hi[:, g % 2, c, 0:n], start=(dc == 0), stop=False)
                        pe.matmul(out, xTh[:, dc, toks], w_lo[:, g % 3, c, 0:n], start=False, stop=False)
                        last = pe.matmul(out, xTl[:, dc, toks], w_hi[:, g % 2, c, 0:n], start=False, stop=(dc == DC - 1))
                    if q == NGR - 1:
                        last.then_inc(proj_psum, 1)
                    elif t == NT - 1:
                        last.then_inc(load_used, 1)
                    if before:
                        turn(*before)
                        before = None
                    if q == NGR - 1:
                        before = (b, t)
            turn(*before)

        @block.vector
        def _(dve):
            dve.memset(s.vn[:, :, :, DV:DV + 1], 1.0).then_inc(ones_set, 1)
            dve.memset(s.ifn[:, :, :], 0.0).then_inc(ones_set, 1)
            dve.wait_ge(ones_set, 2)

            def low(g):
                n = COLS[g // NGR][2]
                dve.wait_ge(wh_done, g + 1)
                dve.tensor_tensor(w_lo[:, g % 3, :, 0:n], w_raw[:, g % 3, :, 0:n], w_hi[:, g % 2, :, 0:n].bitcast(F32),
                                  ALU.subtract).then_inc(wl_done, 1)

            for q in range(NGR):
                dcs = slice(GC * q, GC * q + GC)
                dve.wait_ge(xh_done, q + 1)
                dve.tensor_tensor(xTl[:, dcs, :], s.xT[:, dcs, :], xTh[:, dcs, :].bitcast(F32), ALU.subtract)\
                   .then_inc(xl_done, 1)
                if q == 0:
                    low(0)
            for g, (b, t) in enumerate(groups):
                name, _, n = COLS[b]
                rows = ROWS[t]
                if t == 0:
                    for q in range(1, NGR + 1):
                        if NGR * b + q < NGR * NCB:
                            low(NGR * b + q)
                    dve.wait_ge(b_in, 16 * (b + 1))
                dve.wait_ge(proj_psum, g + 1)
                slot = staged_at[b, t] % 2
                if name in STAGED and staged_at[b, t] >= 2:
                    pb, pt = staged[staged_at[b, t] - 2]
                    if turns(pb, pt):
                        dve.wait_ge(turn_psum, turn_at[pb, pt] + turns(pb, pt))
                    if COLS[pb][0] in OUTPUT:
                        dve.wait_ge(rows_out[slot], 16 * (out_at[pb, pt] // 2 + 1))
                src = gm[0:rows, g % 6, 0:n]
                add = bias[0:rows, 0:n]
                if name in STAGED:
                    dst = stage[0:rows, slot, :]
                elif name == "k":
                    dst = s.kn[0:rows, t, :]
                elif name == "v":
                    h0 = 2 * (b - 2)
                    dst = s.vn[0:rows, t, h0:h0 + 2, 0:DV]
                    src = src.rearrange("p (h d) -> p h d", h=2)
                    add = add.rearrange("p (h d) -> p h d", h=2)
                elif name == "if":
                    dst = s.ifn[0:rows, t, :]
                else:
                    dst = s.gat[0:rows, t, :]
                if name in ("slc", "win"):
                    v = s.vsl if name == "slc" else s.vwi
                    dve.tensor_tensor(v[0:rows, t, :], src[:, 256:512], add[:, 256:512], ALU.add)
                dve.tensor_tensor(dst, src, add, ALU.add).then_inc(proj_done, 1)

        @block.scalar
        def _(act):
            scale = {"q": 1.0, "k": DQK ** -0.5, "bq": HD ** -0.5}

            def high(g):
                n = COLS[g // NGR][2]
                act.wait_ge(w_in[g % 3], 16 * (g // 3 + 1))
                if g >= 2:
                    wait_used(act, g - 2)
                act.copy(w_hi[:, g % 2, :, 0:n], w_raw[:, g % 3, :, 0:n]).then_inc(wh_done, 1)

            for q in range(NGR):
                dcs = slice(GC * q, GC * q + GC)
                act.copy(xTh[:, dcs, :], s.xT[:, dcs, :]).then_inc(xh_done, 1)
                if q == 0:
                    high(0)
            for b, t in groups:
                name, rows = COLS[b][0], ROWS[t]
                if t == 0:
                    for q in range(1, NGR + 1):
                        if NGR * b + q < NGR * NCB:
                            high(NGR * b + q)
                for i in range(turns(b, t)):
                    r = turn_at[b, t] + i
                    act.wait_ge(turn_psum, r + 1)
                    width = P if name in ("q", "k") else HD
                    src = tr[0:width, r % 2, :].rearrange("p (c t) -> p c t", c=4)[:, :, 0:rows]
                    tok = slice(t * P, t * P + rows)
                    if name == "cmp":
                        view = s.cmpT[:, i, 0:32, :].rearrange("p (g n) l -> p g (n l)", g=KV)
                        act.copy(view[:, :, tok], src).then_inc(turn_done, 1)
                        continue
                    dst = {"q": s.qT, "k": s.kT, "slc": s.kslT, "win": s.kwiT}.get(name)
                    dst = s.bqT[:, 8 * (b - 7) + 4 * i:8 * (b - 7) + 4 * i + 4, tok] if name == "bq" else dst[:, :, tok]
                    act.mul(dst, src, scale.get(name, 1.0)).then_inc(turn_done, 1)

        @block.gpsimd
        def _(pool):
            prompt = {"cmp": [io.p_cmp], "slc": [io.p_slc], "win": [io.p_win]}
            sample = {"cmp": io.s_cmp, "slc": io.s_slc}
            for b in range(DB):
                pool.dma_start(io.s_win[b, 0:PAST - DS].rearrange("t a g d -> t (a g d)"),
                               io.cache_win_kv[b, DS:PAST].rearrange("t a g d -> t (a g d)")).then_inc(win_copy, 16)
            sent = [0, 0]
            for b, t in groups:
                name = COLS[b][0]
                if name not in OUTPUT:
                    continue
                slot = staged_at[b, t] % 2
                pool.wait_ge(proj_done, NT * b + t + 1)
                if name == "o":
                    out = io.o_rows[t * P:t * P + ROWS[t], 512 * (b - 5):512 * (b - 4)]
                elif t < 4:
                    out = prompt[name][0][0, t * P:(t + 1) * P].rearrange("t a g d -> t (a g d)")
                elif name == "win":
                    out = io.s_win[:, PAST - DS:PAST].rearrange("b t a g d -> b t (a g d)")
                else:
                    out = sample[name].rearrange("b t a g d -> (b t) (a g d)")
                pool.dma_start(out, stage[0:ROWS[t], slot, :]).then_inc(rows_out[slot], 16)
                sent[slot] += 1
            for slot in range(2):
                pool.wait_ge(rows_out[slot], 16 * sent[slot])
            pool.wait_ge(win_copy, 16 * DB)
    sem.clear()


def stage_mlstm(nc, s, io):
    at, r4 = s.at, s.free
    c0 = at("c0", r4, [P, 2, DB, DV + 1])
    ew = at("ew", r4 + 4128, [P, 1280])
    offs, widths = [0, 512, 896, 1152], [512, 384, 256, 128]
    ews = at("ews", r4 + 5408, [TS, TS])
    kw = at("kw", r4 + 5440, [P, 4, DQK])
    kws = at("kws", r4 + 5952, [TS, DQK])
    kwb = at("kwb", r4 + 6080, [TS, DB, DQK])
    qb = at("qb", r4 + 7104, [P, DB * 36])
    gn = at("gn", r4 + 7392, [P, AH * DV])
    mrow = at("mrow", r4 + 8416, [AH, T])
    brow = at("brow", r4 + 8960, [AH, T])
    ping = at("ping", r4 + 4128, [AH, T])
    pong = at("pong", r4 + 4672, [AH, T])
    irow = at("irow", r4 + 5216, [AH, T])
    small = [r4 + 9504]

    def tiny(name, shape):
        off, size = small[0], int(np.prod(shape[1:]))
        small[0] += -(-size // 8) * 8
        return at(name, off, shape)

    lf = tiny("lf", [P, NT, AH])
    t1 = tiny("gt1", [P, NT, AH])
    t2 = tiny("gt2", [P, NT, AH])
    an = tiny("an", [P, NT, AH])
    en = tiny("en", [P, NT, AH])
    wt = tiny("wt", [P, 4])
    wsi = tiny("wsi", [TS, 2, AH])
    ab = tiny("ab", [P, AH, DB])
    n0T = tiny("n0T", [P, DB, AH])
    nout = tiny("nout", [P, DB, AH])
    pn = tiny("pn", [P, AH])
    mv = tiny("mv", [P, AH, NT, 2])
    st6 = tiny("st6", [P, 6])
    rstd = tiny("rstd", [P, AH, NT])
    dd = tiny("dd", [P, 4])
    m0 = tiny("m0", [AH, DB])
    srow = tiny("srow", [AH, 2, TS])
    abr = tiny("abr", [AH, DB])
    mT = tiny("mT", [P, 1])
    wsl = tiny("wsl", [TS, AH])
    n0 = at("n0", 1000, [DB * AH, DQK])
    nrow = at("nrow", 1128, [DB * AH, DQK])
    nds = at("nds", r4 + 9976, [TS, DV + 1])
    pnrow = at("pnrow", r4 + 4128, [AH, DQK])

    sem = Semaphores(nc)
    with ExitStack() as ctx:
        v = Names()
        v.gate_ready = sem("gate_ready")
        v.lf_ready = sem("lf_ready")
        v.rows_psum = sem("rows_psum")
        v.b_psum = sem("b_psum")
        v.m_ready = sem("m_ready")
        v.cols_psum = sem("cols_psum")
        v.cols_read = sem("cols_read")
        v.m_bcast = sem("m_bcast")
        v.dist_ready = sem("dist_ready")
        v.weight_ready = sem("weight_ready")
        v.wt_in = sem("wt_in")
        v.wt_ready = sem("wt_ready")
        v.scores = sem("scores")
        v.p_ready = sem("p_ready")
        v.kw_ready = sem("kw_ready")
        v.c_psum = sem("c_psum")
        v.out_psum = sem("out_psum")
        v.out_used = sem("out_used")
        v.upd_psum = sem("upd_psum")
        v.upd_used = sem("upd_used")
        v.c_new = sem("c_new")
        v.n_turned = sem("n_turned")
        v.chain = sem("chain")
        v.stat_done = sem("stat_done")
        v.sqrt_done = sem("sqrt_done")
        v.sig_ready = sem("sig_ready")
        v.norm_done = sem("norm_done")
        v.y_psum = sem("y_psum")
        v.y_even = sem("y_even")
        v.y_odd = sem("y_odd")
        v.n_copied = sem("n_copied")
        v.c_out = sem("c_out")
        v.act_chain = sem("act_chain")
        v.o_in = sem("o_in")
        v.gn_in = sem("gn_in")
        v.m0_in = sem("m0_in")
        v.n0_in = sem("n0_in")
        v.small_out = sem("small_out")
        v.pc_ready = sem("pc_ready")
        v.mrow_done = sem("mrow_done")
        c_in = [sem(f"c_in{i}") for i in range(2)]
        c_sent = [sem(f"c_sent{i}") for i in range(2)]
        ps = ctx.enter_context(nc.psum_tensor("ps_m", [P, 8, 512], F32))
        block = ctx.enter_context(nc.Block())
        score_at = [(2, 0), (3, 0), (4, 0), (4, 256)]

        @block.sync
        def _(sp):
            sp.dma_start(m0[:, :], io.state_m.rearrange("b h -> h b"), allow_slow_non_contiguous=True).then_inc(v.m0_in, 16)
            sp.dma_start(n0[:, :], io.state_n.rearrange("b h d -> (b h) d")).then_inc(v.n0_in, 16)
            sp.dma_start(gn[:, :], io.norm_a_g.partition_broadcast(P)).then_inc(v.gn_in, 16)
            sp.dma_start(s.on[:, 0:4, :], io.o_rows[0:TP, :].rearrange("(i p) n -> p i n", p=P)).then_inc(v.o_in, 16)
            sp.dma_start(s.on[0:TS, 4, :], io.o_rows[TP:T, :]).then_inc(v.o_in, 16)
            for h in range(AH):
                if h >= 2:
                    sp.wait_ge(c_sent[h % 2], 16 * (h // 2))
                sp.dma_start(c0[:, h % 2, :, 0:DV], io.state_C[:, h].rearrange("b p v -> p b v")).then_inc(c_in[h % 2], 16)

        @block.gpsimd
        def _(pool):
            pool.wait_ge(v.m_ready, 1)
            pool.dma_start(io.p_m.rearrange("a h -> h a"), brow[:, TP - 1:TP], allow_slow_non_contiguous=True).then_inc(v.small_out, 16)
            pool.dma_start(io.s_m.rearrange("b h -> h b"),
                           brow[:, TP:T].rearrange("h (b t) -> h b t", b=DB)[:, :, DS - 1],
                           allow_slow_non_contiguous=True).then_inc(v.small_out, 16)
            for h in range(AH):
                pool.wait_ge(v.pc_ready, h + 1)
                pool.dma_start(io.p_C[0, h].rearrange("p (a b) -> p a b", a=4), s.kn[:, 0:4, h * DQK:h * DQK + 64]).then_inc(v.c_out, 16)
                pool.wait_ge(v.c_new, h + 1)
                pool.dma_start(io.s_C[:, h].rearrange("b p v -> p b v"), c0[:, h % 2, :, 0:DV]).then_inc(c_sent[h % 2], 16)
            pool.wait_ge(v.n_copied, 1)
            pool.dma_start(io.s_n.rearrange("b h d -> (b h) d"), nrow[:, :]).then_inc(v.small_out, 16)
            pool.dma_start(io.p_n[0], pnrow[:, :]).then_inc(v.small_out, 16)
            pool.wait_ge(v.small_out, 64)
            pool.wait_ge(v.c_out, 16 * AH)
            for i in range(2):
                pool.wait_ge(c_sent[i], 32)

        @block.tensor
        def _(pe):
            for j in range(NT):
                r = ROWS[j]
                dst = ps[0:AH, 0, j * P:j * P + r] if j < 4 else ps[0:AH, 2, 0:TS]
                last = pe.transpose(dst, s.ifn[0:r, j, 0:AH], s.ident[0:r, 0:r])
            last.then_inc(v.rows_psum, 1)
            pe.wait_ge(v.lf_ready, 1)
            for j in range(4):
                for i in range(j + 1):
                    mask = s.upper if i == j else s.ones
                    pe.matmul(ps[0:AH, 1, j * P:(j + 1) * P], lf[:, i, :], mask[:, :], start=(i == 0), stop=(i == j))
            pe.matmul(ps[0:AH, 2, TS:2 * TS], lf[0:TS, 4, :], s.pairs[:, :], start=True, stop=True)
            for j in range(4):
                for i in range(j + 1):
                    mask = s.upper if i == j else s.ones
                    pe.matmul(ps[:, 3, 4 * j:4 * j + 4], mask[:, :], lf[:, i, :], start=(i == 0), stop=(i == j))
            pe.matmul(ps[0:TS, 3, 16:20], s.pairs[:, :], lf[0:TS, 4, :], start=True, stop=True).then_inc(v.b_psum, 1)
            pe.wait_ge(v.m_ready, 1)
            for j in range(NT):
                r = ROWS[j]
                pe.transpose(ps[0:r, 4, 4 * j:4 * j + 4], brow[:, j * P:j * P + r], s.ident[0:AH, 0:AH])
            for i in range(2):
                pe.transpose(ps[0:TS, 4, 20 + 4 * i:24 + 4 * i], srow[:, i, :], s.ident[0:AH, 0:AH])
            for h in range(AH):
                pe.matmul(ps[:, 5, h * DB:(h + 1) * DB], s.head_row[:, h, :], abr[:, :], start=True, stop=True)
            pe.wait_ge(v.n0_in, 16)
            pe.transpose(ps[:, 5, TS:2 * TS], n0[:, :], s.ident[0:TS, 0:TS]).then_inc(v.cols_psum, 1)
            pe.wait_ge(v.cols_read, 1)
            out = 0
            for h in range(AH):
                if h:
                    pe.wait_ge(v.upd_used, DB * h)
                pe.matmul(ps[:, 0, :], s.head_row[:, h, :], mrow[:, 0:TP], start=True, stop=True)
                pe.matmul(ps[0:TS, 1, 0:TS], s.head_row[:, h, 0:TS], mrow[:, TP:T], start=True, stop=True)\
                  .then_inc(v.m_bcast, 1)
                if h:
                    pe.wait_ge(v.p_ready, h)
                for i in range(4):
                    bank, o = score_at[i]
                    pe.matmul(ps[:, bank, o:o + widths[i]], s.kT[:, h, i * P:(i + 1) * P], s.qT[:, h, i * P:TP],
                              start=True, stop=True)
                pe.matmul(ps[0:TS, 4, 384:384 + TS], s.kT[:, h, TP:T], s.qT[:, h, TP:T], start=True, stop=True)\
                  .then_inc(v.scores, 1)
                pe.wait_ge(v.kw_ready, h + 1)
                if h:
                    pe.wait_ge(v.pc_ready, h)
                for i in range(4):
                    last = pe.matmul(ps[:, 5, 0:DV + 1], kw[:, i, :], s.vn[:, i, h, :], start=(i == 0), stop=(i == 3))
                last.then_inc(v.c_psum, 1)
                pe.wait_ge(v.p_ready, h + 1)
                for j in (3, 2, 1, 0):
                    if out >= 2:
                        pe.wait_ge(v.out_used, out - 1)
                    for i in range(j + 1):
                        last = pe.matmul(ps[:, 6 + out % 2, 0:DV + 1], ew[:, offs[i] + (j - i) * P:offs[i] + (j - i + 1) * P],
                                         s.vn[:, i, h, :], start=(i == 0), stop=(i == j))
                    last.then_inc(v.out_psum, 1)
                    out += 1
                pe.wait_ge(v.out_used, out - 1)
                pe.matmul(ps[0:TS, 6, 0:DV + 1], ews[:, :], s.vn[0:TS, 4, h, :], start=True, stop=True)\
                  .then_inc(v.out_psum, 1)
                pe.wait_ge(c_in[h % 2], 16 * (h // 2 + 1))
                pe.wait_ge(v.out_used, out)
                for b in range(DB):
                    last = pe.matmul(ps[0:TS, 7, 0:DV + 1], qb[:, b * TS:(b + 1) * TS], c0[:, h % 2, b, :],
                                     start=(b == 0), stop=(b == DB - 1))
                last.then_inc(v.out_psum, 1)
                out += 2
                for b in range(DB):
                    u = DB * h + b
                    if b >= 2:
                        pe.wait_ge(v.upd_used, u - 1)
                    pe.matmul(ps[:, b % 2, 0:DV + 1], kwb[:, b, :], s.vn[0:TS, 4, h, :], start=True, stop=True)\
                      .then_inc(v.upd_psum, 1)
            pe.wait_ge(v.stat_done, 1)
            pe.transpose(ps[0:TS, 5, 0:DQK], nout[:, :, :].rearrange("p b h -> p (b h)"), s.ident[:, :])
            pe.transpose(ps[0:AH, 4, 0:DQK], pn[:, :], s.ident[:, :]).then_inc(v.n_turned, 1)
            pe.wait_ge(v.norm_done, 1)
            for n in range(2 * NT):
                i, rows = n // 2, ROWS[n // 2]
                if n >= 4:
                    pe.wait_ge([v.y_even, v.y_odd][n % 2], (n - 4) // 2 + 1)
                for c in range(4):
                    fc = 4 * (n % 2) + c
                    last = pe.transpose(ps[:, n % 4, c * P:c * P + rows], s.on[0:rows, i, fc * P:(fc + 1) * P],
                                        s.ident[0:rows, 0:rows])
                last.then_inc(v.y_psum, 1)

        def y_out(eng, copy, parity, done):
            for n in range(parity, 2 * NT, 2):
                i, rows = n // 2, ROWS[n // 2]
                eng.wait_ge(v.y_psum, n + 1)
                src = ps[:, n % 4, :].rearrange("p (c t) -> p c t", c=4)[:, :, 0:rows]
                copy(s.yaT[:, 4 * parity:4 * parity + 4, i * P:i * P + rows], src).then_inc(done, 1)

        @block.vector
        def _(dve):
            step = Count()

            def link(ins):
                ins.then_inc(v.chain, 1)
                dve.wait_ge(v.chain, step.add())

            f = s.ifn[:, :, AH:2 * AH]
            link(dve.tensor_scalar(t1[:, :, :], f, -1.0, None, ALU.mult))
            link(dve.tensor_tensor(t1[:, :, :], t1[:, :, :], f, ALU.max))
            dve.tensor_scalar(t2[:, :, :], f, 0.0, None, ALU.min).then_inc(v.gate_ready, 1)
            dve.memset(qb[:, :], 0.0)
            dve.wait_ge(v.act_chain, 2)
            dve.tensor_tensor(lf[:, :, :], t2[:, :, :], lf[:, :, :], ALU.subtract).then_inc(v.lf_ready, 1)
            dve.wait_ge(v.rows_psum, 1)
            dve.wait_ge(v.b_psum, 1)
            dve.tensor_copy(brow[:, 0:TP], ps[0:AH, 1, :])
            link(dve.tensor_copy(brow[:, TP:T], ps[0:AH, 2, TS:2 * TS]))
            dve.tensor_tensor(ping[:, 0:TP], ps[0:AH, 0, :], brow[:, 0:TP], ALU.subtract)
            dve.tensor_tensor(ping[:, TP:T], ps[0:AH, 2, 0:TS], brow[:, TP:T], ALU.subtract)
            dve.tensor_tensor(an[:, 0:4, :], s.ifn[:, 0:4, 0:AH], ps[:, 3, 0:16].rearrange("p (j h) -> p j h", j=4),
                              ALU.subtract)
            link(dve.tensor_tensor(an[0:TS, 4, :], s.ifn[0:TS, 4, 0:AH], ps[0:TS, 3, 16:20], ALU.subtract))
            a, b = ping, pong
            w = 1
            while w < TP:
                dve.tensor_tensor(b[:, w:TP], a[:, w:TP], a[:, 0:TP - w], ALU.max)
                if w < DS:
                    sa = a[:, TP:T].rearrange("h (b t) -> h b t", b=DB)
                    sb = b[:, TP:T].rearrange("h (b t) -> h b t", b=DB)
                    dve.tensor_tensor(sb[:, :, w:DS], sa[:, :, w:DS], sa[:, :, 0:DS - w], ALU.max)
                    dve.tensor_copy(sb[:, :, 0:w], sa[:, :, 0:w])
                elif w == DS:
                    dve.tensor_copy(irow[:, TP:T], a[:, TP:T])
                link(dve.tensor_copy(b[:, 0:w], a[:, 0:w]))
                a, b = b, a
                w *= 2
            dve.tensor_scalar(mrow[:, 0:TP], a[:, 0:TP], 0.0, None, ALU.max)
            dve.wait_ge(v.m0_in, 16)
            ms = mrow[:, TP:T].rearrange("h (b t) -> h b t", b=DB)
            m0b = m0[:, :].unsqueeze(2).broadcast_to([AH, DB, DS])
            link(dve.tensor_tensor(ms, irow[:, TP:T].rearrange("h (b t) -> h b t", b=DB), m0b, ALU.max))
            link(dve.tensor_tensor(brow[:, :], brow[:, :], mrow[:, :], ALU.add))
            mtb = ms[:, :, DS - 1:DS].broadcast_to([AH, DB, DS])
            dve.tensor_copy(srow[:, 0, :].rearrange("h (b t) -> h b t", b=DB), mtb)
            dve.tensor_tensor(srow[:, 1, :].rearrange("h (b t) -> h b t", b=DB), m0b, ms, ALU.subtract)
            dve.tensor_tensor(abr[:, :], m0[:, :], ms[:, :, DS - 1], ALU.subtract).then_inc(v.m_ready, 1)
            dve.wait_ge(v.cols_psum, 1)
            dve.tensor_tensor(wsl[:, :], an[0:TS, 4, :], ps[0:TS, 4, 20:24], ALU.subtract)
            dve.tensor_copy(n0T[:, :, :].rearrange("p b h -> p (b h)"), ps[:, 5, TS:2 * TS]).then_inc(v.mrow_done, 1)
            dve.wait_ge(v.mrow_done, 1)
            out = 0
            for h in range(AH):
                dve.wait_ge(v.m_bcast, h + 1)
                if h:
                    dve.wait_ge(v.out_psum, 6 * h)
                    dve.wait_ge(v.upd_psum, DB * h)
                for i in range(4):
                    dve.tensor_scalar(ew[:, offs[i]:offs[i] + widths[i]], ps[:, 0, i * P:TP], an[:, i, h:h + 1], 0.0,
                                      ALU.subtract, ALU.max).then_inc(v.dist_ready, 1)
                dve.tensor_scalar(ews[:, :], ps[0:TS, 1, 0:TS], an[0:TS, 4, h:h + 1], 0.0, ALU.subtract, ALU.max)\
                   .then_inc(v.dist_ready, 1)
                link(dve.tensor_copy(mT[:, :], ps[:, 0, TP - 1:TP]))
                dve.tensor_scalar(wt[:, :], an[:, 0:4, h], mT[:, 0:1], None, ALU.subtract).then_inc(v.wt_in, 1)
                dve.wait_ge(v.wt_ready, h + 1)
                for i in range(4):
                    dve.tensor_scalar(kw[:, i, :], s.kn[:, i, h * DQK:(h + 1) * DQK], wt[:, i:i + 1], DQK ** -0.5,
                                      ALU.mult, ALU.mult)
                dve.tensor_copy(qb[:, :].rearrange("p (b x) -> p b x", b=DB)[:, :, 0:DS],
                                s.qT[:, h, TP:T].rearrange("p (b t) -> p b t", b=DB))
                link(dve.tensor_scalar(kws[:, :], s.kn[0:TS, 4, h * DQK:(h + 1) * DQK], wsi[:, 0, h:h + 1], DQK ** -0.5,
                                       ALU.mult, ALU.mult))
                dve.tensor_tensor(kwb[:, :, :], kws[:, :].unsqueeze(1).broadcast_to([TS, DB, DQK]),
                                  s.member[:, :].unsqueeze(2).broadcast_to([TS, DB, DQK]), ALU.mult)
                dve.wait_ge(c_in[h % 2], 16 * (h // 2 + 1))
                dve.tensor_copy(c0[:, h % 2, :, DV:DV + 1], n0T[:, :, h:h + 1]).then_inc(v.kw_ready, 1)
                dve.wait_ge(v.scores, h + 1)
                dve.wait_ge(v.weight_ready, 5 * h + 5)
                for i in range(4):
                    dve.tensor_tensor(ew[:, offs[i]:offs[i] + P], ew[:, offs[i]:offs[i] + P], s.upper[:, :], ALU.mult)
                link(dve.tensor_tensor(ews[:, :], ews[:, :], s.pairs[:, :], ALU.mult))
                for i in range(4):
                    bank, o = score_at[i]
                    dst = ew[:, offs[i]:offs[i] + widths[i]]
                    dve.tensor_tensor(dst, ps[:, bank, o:o + widths[i]], dst, ALU.mult)
                dve.tensor_tensor(ews[:, :], ps[0:TS, 4, 384:384 + TS], ews[:, :], ALU.mult).then_inc(v.p_ready, 1)
                dve.wait_ge(v.c_psum, h + 1)
                dve.tensor_copy(pn[:, h:h + 1], ps[:, 5, DV:DV + 1])
                dve.tensor_copy(s.kn[:, 0:4, h * DQK:h * DQK + 64], ps[:, 5, 0:DV].rearrange("p (a b) -> p a b", a=4))\
                   .then_inc(v.pc_ready, 1)

                def normalise(num, j, rows):
                    den = num[:, DV:DV + 1]
                    link(dve.tensor_scalar(dd[0:rows, 0:1], den, -1.0, None, ALU.mult))
                    link(dve.scalar_tensor_tensor(out=dd[0:rows, 1:2], in0=dd[0:rows, 0:1], scalar=den,
                                                  in1=en[0:rows, j, h:h + 1], op0=ALU.max, op1=ALU.max))
                    link(dve.reciprocal(dd[0:rows, 2:3], dd[0:rows, 1:2]))
                    dst = s.vn[0:rows, j, h, 0:DV]
                    return dve.tensor_scalar(dst, num[:, 0:DV], dd[0:rows, 2:3], None, ALU.mult)

                def stats(j, rows):
                    link(dve.bn_stats(st6[0:rows, :], s.vn[0:rows, j, h, 0:DV]))
                    return dve.bn_aggr(mv[0:rows, h, j, :], st6[0:rows, :])

                for j in (3, 2, 1, 0):
                    dve.wait_ge(v.out_psum, out + 1)
                    normalise(ps[:, 6 + out % 2, 0:DV + 1], j, P).then_inc(v.out_used, 1)
                    out += 1
                    dve.wait_ge(v.out_used, out)
                    stats(j, P)
                dve.wait_ge(v.out_psum, out + 2)
                link(dve.tensor_scalar(nds[:, :], ps[0:TS, 7, 0:DV + 1], wsi[:, 1, h:h + 1], None, ALU.mult))
                link(dve.tensor_tensor(nds[:, :], ps[0:TS, 6, 0:DV + 1], nds[:, :], ALU.add))
                for b in range(DB):
                    dve.wait_ge(v.upd_psum, DB * h + b + 1)
                    dve.scalar_tensor_tensor(out=c0[:, h % 2, b, :], in0=c0[:, h % 2, b, :], scalar=ab[:, h, b:b + 1],
                                             in1=ps[:, b % 2, 0:DV + 1], op0=ALU.mult, op1=ALU.add)\
                       .then_inc(v.upd_used, 1)
                dve.wait_ge(v.upd_used, DB * (h + 1))
                dve.tensor_copy(nout[:, :, h:h + 1], c0[:, h % 2, :, DV:DV + 1]).then_inc(v.c_new, 1)
                normalise(nds[:, :], 4, TS).then_inc(v.out_used, 1)
                dve.wait_ge(v.out_used, out + 1)
                stats(4, TS).then_inc(v.out_used, 1)
                out += 2
            dve.wait_ge(v.c_new, AH)
            dve.wait_ge(v.out_used, out)
            link(dve.tensor_scalar(rstd[:, :, 0:4], mv[:, :, 0:4, 1], LN_EPS, None, ALU.add))
            dve.tensor_scalar(rstd[0:TS, :, 4], mv[0:TS, :, 4, 1], LN_EPS, None, ALU.add).then_inc(v.stat_done, 1)
            dve.wait_ge(v.sqrt_done, 1)
            dve.reciprocal(rstd[:, :, 0:4], rstd[:, :, 0:4])
            link(dve.reciprocal(rstd[0:TS, :, 4], rstd[0:TS, :, 4]))
            dve.wait_ge(v.gn_in, 16)
            dve.wait_ge(v.sig_ready, NT)
            for j in range(NT):
                r = ROWS[j]
                dve.tensor_tensor(s.on[0:r, j, :], s.on[0:r, j, :], gn[0:r, :], ALU.mult)
                for h in range(AH):
                    x = s.vn[0:r, j, h, 0:DV]
                    last = dve.tensor_scalar(x, x, mv[0:r, h, j, 0:1], rstd[0:r, h, j:j + 1], ALU.subtract, ALU.mult)
                link(last)
                last = dve.tensor_tensor(s.on[0:r, j, :].rearrange("p (h d) -> p h d", h=AH),
                                         s.on[0:r, j, :].rearrange("p (h d) -> p h d", h=AH), s.vn[0:r, j, :, 0:DV],
                                         ALU.mult)
            last.then_inc(v.norm_done, 1)
            dve.wait_ge(v.n_turned, 1)
            dve.tensor_copy(nrow[:, :], ps[0:TS, 5, 0:DQK])
            dve.tensor_copy(pnrow[:, :], ps[0:AH, 4, 0:DQK]).then_inc(v.n_copied, 1)
            y_out(dve, dve.tensor_copy, 0, v.y_even)

        @block.scalar
        def _(act):
            act.wait_ge(v.gate_ready, 1)
            act.activation(t1[:, :, :], t1[:, :, :], ACT.Exp, scale=-1.0).then_inc(v.act_chain, 1)
            act.wait_ge(v.act_chain, 1)
            act.activation(lf[:, :, :], t1[:, :, :], ACT.Ln, bias=1.0).then_inc(v.act_chain, 1)
            act.wait_ge(v.mrow_done, 1)
            act.activation(en[:, 0:4, :], ps[:, 4, 0:16].rearrange("p (j h) -> p j h", j=4), ACT.Exp, scale=-1.0)
            act.activation(en[0:TS, 4, :], ps[0:TS, 4, 16:20], ACT.Exp, scale=-1.0)
            act.activation(wsi[:, 1, :], ps[0:TS, 4, 24:28], ACT.Exp)
            act.activation(ab[:, :, :], ps[:, 5, 0:TS].rearrange("p (h b) -> p h b", h=AH), ACT.Exp)
            act.activation(wsi[:, 0, :], wsl[:, :], ACT.Exp).then_inc(v.cols_read, 1)
            for h in range(AH):
                for i in range(5):
                    act.wait_ge(v.dist_ready, 5 * h + i + 1)
                    x = ew[:, offs[i]:offs[i] + widths[i]] if i < 4 else ews[:, :]
                    act.activation(x, x, ACT.Exp, scale=-1.0).then_inc(v.weight_ready, 1)
                act.wait_ge(v.wt_in, h + 1)
                act.activation(wt[:, :], wt[:, :], ACT.Exp).then_inc(v.wt_ready, 1)
            for j in range(NT):
                r = ROWS[j]
                if j == 0:
                    act.wait_ge(v.o_in, 32)
                act.activation(s.on[0:r, j, :], s.on[0:r, j, :], ACT.Sigmoid).then_inc(v.sig_ready, 1)
            act.wait_ge(v.stat_done, 1)
            act.activation(rstd[:, :, 0:4], rstd[:, :, 0:4], ACT.Sqrt)
            act.activation(rstd[0:TS, :, 4], rstd[0:TS, :, 4], ACT.Sqrt).then_inc(v.sqrt_done, 1)
            y_out(act, act.copy, 1, v.y_odd)
    sem.clear()


def place_attention(s):
    at = s.at
    s.ybT = at("ybT", 25728, [P, DC, T])
    s.kcP = at("kcP", 30080, [HD, KV, 8])
    s.kcS = at("kcS", 30112, [HD, DB, KV, 4])
    s.vbd = at("vbd", 30240, [P, BH, HD])
    s.vcn = at("vcn", 31264, [8, 4, KV, HD])
    s.hm = at("hm", 32288, [P, BH])
    s.gden = at("gden", 32304, [P, NT, 48])
    s.att = 36992


def stage_compress(nc, s, io):
    place_attention(s)
    at, a0 = s.at, s.att
    NS, NB = DB * KV * 4, KV * 8
    w0 = a0 + CB * (NS + NB + 2)
    xs = at("xs", a0, [HD, CB, NS + NB + 2])
    wc = at("wc", w0, [HD, CB, HD])
    page = at("page", w0 + 4096, [P, 4, KV * HD])
    pes = at("pes", w0 + 5120, [CB, HD])
    vcT = at("vcT", w0 + 5184, [HD, KV, REP, 8])
    vsT = at("vsT", w0 + 5312, [HD, KV, DB, 4])
    pcol = at("pcol", w0 + 5440, [HD, 2])
    table = at("table_c", w0 + 5448, [1, DB * NPG], I32)
    slope_row = s.slope_row = at("slope_row", 936, [P, BH])
    sem = Semaphores(nc)
    with ExitStack() as ctx:
        page_in = [sem(f"page_in{i}") for i in range(4)]
        table_in, w_in, pe_in = sem("table_in"), sem("cmp_w_in"), sem("pos_in")
        page_psum, page_even, page_odd = sem("page_psum"), sem("page_even"), sem("page_odd")
        pos_psum, pos_done = sem("pos_psum"), sem("pos_done")
        sums, sums_read, v_psum, v_read, chain, masks = (sem("cmp_sums"), sem("cmp_read"), sem("vc_psum"),
                                                        sem("vc_read"), sem("cmp_chain"), sem("cmp_masks"))
        vrep_ready, prompt_done = sem("vrep_ready"), sem("cmp_prompt_done")
        ps = ctx.enter_context(nc.psum_tensor("ps_c", [P, 8, 512], F32))
        block = ctx.enter_context(nc.Block())
        NPAGES = DB * NPG

        @block.sync
        def _(sp):
            sp.dma_start(table[:, :], io.page_table.rearrange("b n -> (b n)").unsqueeze(0)).then_inc(table_in, 16)
            sp.wait_ge(table_in, 16)
            for kv in range(2):
                if kv:
                    sp.wait_ge(sums, 1)
                    sp.wait_ge(pos_psum, 1)
                sp.dma_start(pes[:, :], io.nsa_pe[kv]).then_inc(pe_in, 16)
                for i in range(NPAGES):
                    n = NPAGES * kv + i
                    pg = sp.value_load(table[0:1, i:i + 1], min_val=0, max_val=io.cache_cmp_kv.shape[0] - 1)
                    if n >= 4:
                        sp.wait_ge(page_psum, n - 3)
                    src = io.cache_cmp_kv[bass.ds(pg, 1), :, kv].rearrange("o t g d -> (o t) (g d)")
                    sp.dma_start(page[:, n % 4, :], src).then_inc(page_in[n % 4], 16)
                    if i == 3:
                        sp.dma_start(wc[:, :, :], io.nsa_w_cmp[kv].rearrange("l d e -> d l e")).then_inc(w_in, 16)

        @block.gpsimd
        def _(pool):
            pool.affine_select(out=s.hm[:, :], in_=s.ones[:, 0:BH], compare_op=ALU.is_ge, fill=0.0, base=0,
                               pattern=[[-8, BH]], channel_multiplier=1).then_inc(masks, 1)
            pool.wait_ge(masks, 1)
            pool.affine_select(out=s.hm[:, :], in_=s.hm[:, :], compare_op=ALU.is_ge, fill=0.0, base=7,
                               pattern=[[8, BH]], channel_multiplier=-1)
            for h in range(BH):
                last = pool.memset(slope_row[:, h:h + 1], -SLOPES[h])
            last.then_inc(masks, 1)
            for kv in range(2):
                if kv:
                    pool.wait_ge(sums, 1)
                pool.tensor_copy(xs[:, :, NS:NS + NB].rearrange("d l n -> d n l"), s.cmpT[:, kv, 0:NB, :])\
                    .then_inc(prompt_done, 1)

        @block.tensor
        def _(pe):
            for kv in range(2):
                pe.wait_ge(pe_in, 16 * (kv + 1))
                if kv:
                    pe.wait_ge(pos_done, 1)
                pe.transpose(ps[0:HD, 6, 0:CB], pes[:, :], s.ident[0:CB, 0:CB]).then_inc(pos_psum, 1)
                for i in range(NPAGES):
                    n = NPAGES * kv + i
                    pe.wait_ge(page_in[n % 4], 16 * (n // 4 + 1))
                    if n >= 4:
                        pe.wait_ge([page_even, page_odd][n % 2], (n - 4) // 2 + 1)
                    for g in range(KV):
                        last = pe.transpose(ps[0:HD, n % 4, g * P:(g + 1) * P], page[:, n % 4, g * HD:(g + 1) * HD],
                                            s.ident[:, :])
                    last.then_inc(page_psum, 1)
                pe.wait_ge(w_in, 16 * (kv + 1))
                pe.wait_ge(page_even, (kv + 1) * NPAGES // 2)
                pe.wait_ge(page_odd, (kv + 1) * NPAGES // 2)
                pe.wait_ge(pos_done, kv + 1)
                pe.wait_ge(prompt_done, kv + 1)
                if kv:
                    pe.wait_ge(sums_read, 1)
                for l in range(CB):
                    last = pe.matmul(ps[0:HD, 4, 0:NS + NB + 1], wc[:, l, :], xs[:, l, 0:NS + NB + 1],
                                     start=(l == 0), stop=(l == CB - 1))
                last.then_inc(sums, 1)
            pe.wait_ge(vrep_ready, 1)
            pe.transpose(ps[:, 7, 0:HD], vcT[:, :, :, :].rearrange("e g r n -> e (g r n)"), s.ident[0:HD, 0:HD])
            for j in range(4):
                for g in range(KV):
                    last = pe.transpose(ps[0:8, j // 2, ((j % 2) * KV + g) * HD:((j % 2) * KV + g + 1) * HD],
                                        vsT[:, g, 2 * j:2 * j + 2, :].rearrange("e b n -> e (b n)"), s.ident[0:HD, 0:HD])
            last.then_inc(v_psum, 1)

        def pages_out(eng, copy, parity, done, kv):
            for i in range(parity, NPAGES, 2):
                n = NPAGES * kv + i
                b, half = i // NPG, i % NPG
                eng.wait_ge(page_psum, n + 1)
                if kv and i == parity:
                    eng.wait_ge(sums, 1)
                dst = xs[:, :, 0:NS].rearrange("d l (b g n) -> d b g n l", b=DB, g=KV)[:, b, :, 2 * half:2 * half + 2, :]
                copy(dst, ps[0:HD, n % 4, :].rearrange("d (g n l) -> d g n l", g=KV, n=2)).then_inc(done, 1)

        @block.vector
        def _(dve):
            step = Count()

            def link(ins):
                ins.then_inc(chain, 1)
                dve.wait_ge(chain, step.add())

            for kv in range(2):
                dve.wait_ge(pos_psum, kv + 1)
                if kv:
                    dve.wait_ge(sums, 1)
                dve.tensor_copy(xs[:, :, NS + NB], ps[0:HD, 6, 0:CB]).then_inc(pos_done, 1)
                pages_out(dve, dve.tensor_copy, 0, page_even, kv)
                dve.wait_ge(sums, kv + 1)
                link(dve.tensor_copy(pcol[:, kv:kv + 1], ps[0:HD, 4, NS + NB:NS + NB + 1]))
                pos = pcol[:, kv:kv + 1]
                if kv == 0:
                    dve.tensor_scalar(s.kcP[:, :, :], ps[0:HD, 4, NS:NS + NB].rearrange("e (g n) -> e g n", g=KV), pos, None,
                                      ALU.add)
                    dve.tensor_scalar(s.kcS[:, :, :, :].rearrange("e b g n -> e (b g n)"), ps[0:HD, 4, 0:P], pos, None,
                                      ALU.add).then_inc(sums_read, 1)
                    continue
                src = ps[0:HD, 4, NS:NS + NB].rearrange("e (g n) -> e g n", g=KV)
                for r in range(REP):
                    dve.tensor_scalar(vcT[:, :, r, :], src, pos, None, ALU.add)
                dve.tensor_scalar(vsT[:, :, :, :].rearrange("e g b n -> e b g n"),
                                  ps[0:HD, 4, 0:P].rearrange("e (b g n) -> e b g n", b=DB, g=KV), pos, None,
                                  ALU.add).then_inc(vrep_ready, 1)
            dve.wait_ge(v_psum, 1)
            dve.wait_ge(masks, 2)
            link(dve.tensor_copy(s.vbd[:, 0, :], ps[:, 7, 0:HD]))
            for h in range(BH - 1, -1, -1):
                dve.tensor_scalar(s.vbd[:, h, :], s.vbd[:, 0, :], s.hm[:, h:h + 1], None, ALU.mult)
            last = None
            for q in range(2):
                last = dve.tensor_copy(s.vcn[:, 2 * q:2 * q + 2, :, :].rearrange("k j g e -> k (j g e)"), ps[0:8, q, :])
            last.then_inc(v_read, 1)

        @block.scalar
        def _(act):
            for kv in range(2):
                pages_out(act, act.copy, 1, page_odd, kv)
    sem.clear()


def stage_attend_prompt(nc, s, io):
    at, a0 = s.at, s.att
    dist = at("dist", a0, [P, TP])
    bias = at("abias", a0 + 512, [P, 2, TP])
    EB = 3
    ex = at("ex", a0 + 7352, [P, EB, 2, TP])
    pt = at("pt", a0 + 3584, [P, 2, 2, TP])
    pc = at("pc", a0 + 5632, [P, 4, BH, 8])
    pcT = at("pcT", a0 + 6144, [P, TP])
    cdist = at("cdist", a0 + 6656, [P, 4, 8])
    valid = at("cvalid", a0 + 6688, [P, 4, 8])
    cb = at("cbias", a0 + 6720, [P, 4, BH, 8])
    cm = at("cmax", a0 + 7232, [P, 4, BH])
    mx = at("amx", a0 + 7296, [P, 2 * EB])
    nm = at("anm", a0 + 7304, [P, 2 * EB])
    rs = at("ars", a0 + 7312, [P, 2 * EB])
    rr = at("arr", a0 + 7320, [P, 2 * EB])
    keysT = [s.kslT, s.kwiT]
    vals = [s.vsl, s.vwi]
    units = [(h, i) for h in range(BH) for i in range(4)]
    NU = len(units)
    sem = Semaphores(nc)
    with ExitStack() as ctx:
        made, dist_ready, chain = sem("dist_made"), sem("dist_ready2"), sem("att_chain")
        cs_psum, cexp_in, cexp_done, pc_ready, pcT_psum, pcT_ready = (sem("cs_psum"), sem("cexp_in"), sem("cexp_done"),
                                                                     sem("pc_ready2"), sem("pcT_psum"), sem("pcT_ready"))
        gate_exp, bias_ready = sem("gate_exp"), sem("bias_ready")
        s_psum, s_max, s_exp, s_scaled, t_psum, t_done, o_psum, o_done = (
            sem("s_psum"), sem("s_max"), sem("s_exp"), sem("s_scaled"), sem("t_psum"), sem("t_done"), sem("o_psum"),
            sem("o_done"))
        ps = ctx.enter_context(nc.psum_tensor("ps_a", [P, 8, 512], F32))
        block = ctx.enter_context(nc.Block())

        @block.gpsimd
        def _(pool):
            pool.iota(dist[:, :], pattern=[[-1, TP]], base=384, channel_multiplier=1,
                      allow_small_or_imprecise_dtypes=True)
            pool.iota(cdist[:, :, :], pattern=[[P, 4], [-CB, 8]], base=1 - CB, channel_multiplier=1,
                      allow_small_or_imprecise_dtypes=True).then_inc(made, 1)
            pool.wait_ge(made, 1)
            pool.affine_select(out=dist[:, :], in_=dist[:, :], compare_op=ALU.is_ge, fill=BIG, base=384,
                               pattern=[[-1, TP]], channel_multiplier=1)
            pool.affine_select(out=valid[:, :, :], in_=s.ones[:, 0:32].rearrange("p (i n) -> p i n", i=4),
                               compare_op=ALU.is_ge, fill=0.0, base=1 - CB, pattern=[[P, 4], [-CB, 8]],
                               channel_multiplier=1)
            pool.affine_select(out=cdist[:, :, :], in_=cdist[:, :, :], compare_op=ALU.is_ge, fill=BIG, base=1 - CB,
                               pattern=[[P, 4], [-CB, 8]], channel_multiplier=1).then_inc(dist_ready, 1)

        @block.tensor
        def _(pe):
            for i in range(4):
                for h in range(BH):
                    last = pe.matmul(ps[:, 6, (i * BH + h) * 8:(i * BH + h + 1) * 8], s.bqT[:, h, i * P:(i + 1) * P],
                                     s.kcP[:, h // REP, :], start=True, stop=True)
            last.then_inc(cs_psum, 1)

            def scores(u):
                h, i = units[u]
                if u >= 2:
                    pe.wait_ge(s_max, u - 1)
                for br in range(2):
                    last = pe.matmul(ps[:, 2 * (u % 2) + br, 0:(i + 1) * P], s.bqT[:, h, i * P:(i + 1) * P],
                                     keysT[br][:, h // REP, 0:(i + 1) * P], start=True, stop=True)
                last.then_inc(s_psum, 1)

            def turn(u):
                h, i = units[u]
                pe.wait_ge(s_scaled, u + 1)
                if u >= 1:
                    pe.wait_ge(t_done, u)
                for br in range(2):
                    for c in range(i + 1):
                        last = pe.transpose(ps[:, 4 + br, c * P:(c + 1) * P], ex[:, u % EB, br, c * P:(c + 1) * P],
                                            s.ident[:, :])
                last.then_inc(t_psum, 1)

            def output(u):
                h, i = units[u]
                pair = h // 2
                if u == 0:
                    pe.wait_ge(pcT_ready, 1)
                if h % 2 == 0 and i == 0 and pair >= 2:
                    pe.wait_ge(o_done, pair - 1)
                pe.wait_ge(t_done, u + 1)
                out = ps[64 * (h % 2):64 * (h % 2) + HD, 6 + pair % 2, i * P:(i + 1) * P]
                pe.matmul(out, s.vbd[:, h, :], pcT[:, i * P:(i + 1) * P], start=True, stop=False)
                g = h // REP
                for br in range(2):
                    for c in range(i + 1):
                        last = pe.matmul(out, vals[br][:, c, g * HD:(g + 1) * HD], pt[:, u % 2, br, c * P:(c + 1) * P],
                                         start=False, stop=(br == 1 and c == i))
                last.then_inc(o_psum, 1)

            scores(0)
            scores(1)
            pe.wait_ge(pc_ready, 1)
            for i in range(4):
                last = pe.transpose(ps[:, 7, i * P:(i + 1) * P], pc[:, i, :, :].rearrange("p h n -> p (h n)"),
                                    s.ident[:, :])
            last.then_inc(pcT_psum, 1)
            for u in range(NU):
                if u + 2 < NU:
                    scores(u + 2)
                turn(u)
                if u >= 1:
                    output(u - 1)
            output(NU - 1)

        @block.vector
        def _(dve):
            step = Count()

            def link(ins):
                ins.then_inc(chain, 1)
                dve.wait_ge(chain, step.add())

            dve.wait_ge(gate_exp, 1)
            dve.tensor_scalar(s.gden[:, 0:4, :], s.gden[:, 0:4, :], 1.0, None, ALU.add)
            link(dve.tensor_scalar(s.gden[0:TS, 4, :], s.gden[0:TS, 4, :], 1.0, None, ALU.add))
            dve.wait_ge(dist_ready, 1)
            for i in range(4):
                last = dve.tensor_tensor(cb[:, i, :, :], cdist[:, i, :].unsqueeze(1).broadcast_to([P, BH, 8]),
                                         s.slope_row[:, :].unsqueeze(2).broadcast_to([P, BH, 8]), ALU.mult)
            link(last)

            def flat(x):
                return x[:, :, :, :].rearrange("p i h n -> p (i h) n")

            dve.wait_ge(cs_psum, 1)
            link(dve.tensor_tensor(flat(pc), ps[:, 6, :].rearrange("p (x n) -> p x n", n=8), flat(cb), ALU.add))
            cmf = cm[:, :, :].rearrange("p i h -> p (i h)")
            link(dve.tensor_reduce(cmf, flat(pc), AX.X, ALU.max))
            dve.tensor_tensor(flat(pc), flat(pc), cmf.unsqueeze(2).broadcast_to([P, 64, 8]), ALU.subtract)\
               .then_inc(cexp_in, 1)
            dve.wait_ge(cexp_done, 1)
            link(dve.tensor_reduce(cmf, flat(pc), AX.X, ALU.add))
            link(dve.tensor_tensor(cm[:, :, :], cm[:, :, :], s.gden[:, 0:4, 0:BH], ALU.mult))
            link(dve.reciprocal(cmf, cmf))
            link(dve.tensor_tensor(flat(pc), flat(pc), cmf.unsqueeze(2).broadcast_to([P, 64, 8]), ALU.mult))
            for i in range(4):
                last = dve.tensor_tensor(pc[:, i, :, :], pc[:, i, :, :],
                                         valid[:, i, :].unsqueeze(1).broadcast_to([P, BH, 8]), ALU.mult)
            last.then_inc(pc_ready, 1)

            def maxima(u):
                h, i = units[u]
                w = (i + 1) * P
                if i == 0:
                    dve.wait_ge(bias_ready, h + 1)
                dve.wait_ge(s_psum, u + 1)
                if u >= EB:
                    dve.wait_ge(t_psum, u - EB + 1)
                o = 2 * (u % EB)
                for br in range(2):
                    last = dve.tensor_tensor_reduce(out=ex[:, u % EB, br, 0:w], in0=ps[:, 2 * (u % 2) + br, 0:w],
                                                    in1=bias[:, h % 2, TP - w:TP], scale=1.0, scalar=-3e38, op0=ALU.add,
                                                    op1=ALU.max, accum_out=mx[:, o + br:o + br + 1])
                link(last)
                dve.tensor_scalar(nm[:, o:o + 2], mx[:, o:o + 2], -1.0, None, ALU.mult).then_inc(s_max, 1)

            def scale(u):
                h, i = units[u]
                w, o = (i + 1) * P, 2 * (u % EB)
                dve.wait_ge(s_exp, u + 1)
                gd = s.gden[:, i, :].rearrange("p (b h) -> p b h", b=3)[:, 1:3, h]
                link(dve.tensor_tensor(rr[:, o:o + 2], rs[:, o:o + 2], gd, ALU.mult))
                link(dve.reciprocal(rr[:, o:o + 2], rr[:, o:o + 2]))
                for br in range(2):
                    x = ex[:, u % EB, br, 0:w]
                    last = dve.tensor_scalar(x, x, rr[:, o + br:o + br + 1], None, ALU.mult)
                last.then_inc(s_scaled, 1)

            dve.wait_ge(pcT_psum, 1)
            dve.tensor_copy(pcT[:, :], ps[:, 7, :]).then_inc(pcT_ready, 1)
            maxima(0)
            for u in range(NU):
                if u + 1 < NU:
                    maxima(u + 1)
                scale(u)

        @block.scalar
        def _(act):
            act.activation(s.gden[:, 0:4, :], s.gat[:, 0:4, :], ACT.Exp, scale=-1.0)
            act.activation(s.gden[0:TS, 4, :], s.gat[0:TS, 4, :], ACT.Exp, scale=-1.0).then_inc(gate_exp, 1)
            act.wait_ge(cexp_in, 1)
            act.activation(pc[:, :, :, :], pc[:, :, :, :], ACT.Exp).then_inc(cexp_done, 1)
            act.wait_ge(dist_ready, 1)
            for h in range(2):
                act.mul(bias[:, h, :], dist[:, :], -SLOPES[h]).then_inc(bias_ready, 1)

            def copy_turned(u):
                h, i = units[u]
                w = (i + 1) * P
                act.wait_ge(t_psum, u + 1)
                if u >= 2:
                    act.wait_ge(o_psum, u - 1)
                for br in range(2):
                    last = act.copy(pt[:, u % 2, br, 0:w], ps[:, 4 + br, 0:w])
                last.then_inc(t_done, 1)
                if h % 2 == 1 and i == 3:
                    pair = h // 2
                    act.wait_ge(o_psum, u + 1)
                    act.copy(s.ybT[:, pair, 0:TP], ps[:, 6 + pair % 2, :]).then_inc(o_done, 1)

            for u, (h, i) in enumerate(units):
                act.wait_ge(s_max, u + 1)
                w, o = (i + 1) * P, 2 * (u % EB)
                for br in range(2):
                    x = ex[:, u % EB, br, 0:w]
                    last = act.activation(x, x, ACT.Exp, bias=nm[:, o + br:o + br + 1],
                                          accum_out=rs[:, o + br:o + br + 1])
                last.then_inc(s_exp, 1)
                if i == 3 and h + 2 < BH:
                    act.mul(bias[:, h % 2, :], dist[:, :], -SLOPES[h + 2]).then_inc(bias_ready, 1)
                if u >= 1:
                    copy_turned(u - 1)
            copy_turned(NU - 1)
    sem.clear()


def stage_attend_samples(nc, s, io):
    at, a0, f0 = s.at, s.att, 30240
    W = 2 * PAST + TS
    qs = at("qs", a0, [HD, 4, BH, 8])
    rows = at("kv_rows", a0 + 512, [P, 2, 2, 4, 2 * KV * HD])
    kt = at("kt_s", a0 + 8704, [HD, 2, 2, KV, PAST])
    ex = at("ex_s", a0 + 12800, [P, 2, W])
    pt = at("pt_s", a0 + 13888, [P, 2, 4 * P])
    ptn = at("ptn", a0 + 14912, [TS, 2, P])
    pcs = at("pcs", a0 + 15168, [P, 8])
    pctT = at("pcsT", a0 + 15176, [8, P])
    bias = at("bias_s", a0 + 15304, [P, W])
    newd = at("newd", a0 + 15848, [P, 4, TS])
    gd = at("gd", a0 + 15976, [P, 4, 4])
    tmp = at("gtmp", a0 + 15992, [P, 3, BH])
    cbias = at("cbias_s", a0 + 16040, [P, 8])
    cols = at("cols_s", a0 + 16048, [P, 16])
    icol = at("icol", a0 + 16064, [P, 8], I32)
    mx = at("mx_s", a0 + 16072, [P, 8])
    table = at("table_s", a0 + 16080, [1, DB * NPG], I32)
    mark = at("gd_mark", a0 + 16096, [P, 4])
    sel = at("sel", f0, [TS, 4, BH, 8])
    v1 = at("nv1", f0 + 512, [P, 4, TS])
    v2 = at("nv2", f0 + 640, [P, 4, TS])
    keysT = [s.kslT, s.kwiT]
    vals = [s.vsl, s.vwi]
    slope, t4, b2, nb2, t8 = (cols[:, i:i + 1] for i in range(5))
    sem = Semaphores(nc)
    with ExitStack() as ctx:
        made, sel_ready, chain, table_in = sem("s_made"), sem("sel_ready"), sem("s_chain"), sem("s_table")
        rows_in = [sem("kv_in0"), sem("kv_in1")]
        gd_psum, gd_read, qs_ready = sem("gd_psum"), sem("gd_read"), sem("qs_ready")
        k_psum, k_even, k_odd = sem("k_psum"), sem("k_even"), sem("k_odd")
        c_psum, s_psum, s_max, s_exp, s_scaled = sem("sc_psum"), sem("ss_psum"), sem("ss_max"), sem("ss_exp"), sem("ss_scaled")
        t_psum, t_dve, t_act, o_psum, o_done = sem("st_psum"), sem("st_dve"), sem("st_act"), sem("so_psum"), sem("so_done")
        ps = ctx.enter_context(nc.psum_tensor("ps_s", [P, 8 * 512], F32))
        block = ctx.enter_context(nc.Block())

        @block.sync
        def _(sp):
            sp.dma_start(table[:, :], io.page_table.rearrange("b n -> (b n)").unsqueeze(0)).then_inc(table_in, 16)
            sp.wait_ge(table_in, 16)
            for j in range(4):
                if j >= 2:
                    sp.wait_ge(o_psum, j - 1)
                for c in range(4):
                    i = 4 * j + c
                    pg = sp.value_load(table[0:1, i:i + 1], min_val=0, max_val=io.cache_slc_kv.shape[0] - 1)
                    src = io.cache_slc_kv[bass.ds(pg, 1)].rearrange("o t a g d -> (o t) (a g d)")
                    sp.dma_start(rows[:, j % 2, 0, c, :], src).then_inc(rows_in[j % 2], 16)
                src = io.cache_win_kv[2 * j:2 * j + 2].rearrange("b (c p) a g d -> p (b c) (a g d)", p=P)
                sp.dma_start(rows[:, j % 2, 1, :, :], src).then_inc(rows_in[j % 2], 16)

        @block.gpsimd
        def _(pool):
            pool.iota(icol[:, 0:1], pattern=[[0, 1]], base=0, channel_multiplier=1)
            pool.iota(bias[:, 0:512], pattern=[[0, 2], [-1, PAST]], base=PAST, channel_multiplier=0,
                      allow_small_or_imprecise_dtypes=True)
            pool.iota(newd[:, :, :], pattern=[[8, 4], [-1, TS]], base=0, channel_multiplier=0,
                      allow_small_or_imprecise_dtypes=True)
            pool.iota(cbias[:, :], pattern=[[0, 2], [-CB, 4]], base=PAST - CB + 1, channel_multiplier=0,
                      allow_small_or_imprecise_dtypes=True).then_inc(made, 1)
            pool.memset(sel[:, :, :, :], 1.0).then_inc(sel_ready, 1)
            pool.wait_ge(sel_ready, 1)
            pool.affine_select(out=sel[:, :, :, :], in_=sel[:, :, :, :], compare_op=ALU.is_equal, fill=0.0, base=0,
                               pattern=[[-8, 4], [0, BH], [-1, 8]], channel_multiplier=1).then_inc(sel_ready, 1)

        @block.tensor
        def _(pe):
            pe.wait_ge(sel_ready, 2)
            for j in range(4):
                last = pe.matmul(ps[:, 6 * 512 + 48 * j:6 * 512 + 48 * (j + 1)],
                                 sel[:, j, :, :].rearrange("w h t -> w (h t)"), s.gden[0:TS, 4, :], start=True, stop=True)
            last.then_inc(gd_psum, 1)
            for j in range(4):
                pe.wait_ge(rows_in[j % 2], 80 * (j // 2 + 1))
                for n in range(16):
                    br, c = n // 8, (n // 2) % 4
                    m = 8 * j + n // 2
                    if n % 2 == 0:
                        if j and n < 4:
                            pe.wait_ge(t_dve, j)
                            pe.wait_ge(t_act, j)
                        if m >= 2:
                            pe.wait_ge([k_even, k_odd][m % 2], (m - 2) // 2 + 1)
                    for g in (2 * (n % 2), 2 * (n % 2) + 1):
                        last = pe.transpose(ps[0:HD, (m % 2) * 512 + g * P:(m % 2) * 512 + (g + 1) * P],
                                            rows[:, j % 2, br, c, g * HD:(g + 1) * HD], s.ident[:, :])
                    if n % 2:
                        last.then_inc(k_psum, 1)
                if j == 0:
                    pe.wait_ge(qs_ready, 1)
                for g in range(KV):
                    q = qs[:, j, 4 * g:4 * g + 4, :].rearrange("d h t -> d (h t)")
                    last = pe.matmul(ps[32 * g:32 * g + 32, 7 * 512 + 384:7 * 512 + 392], q,
                                     s.kcS[:, 2 * j:2 * j + 2, g, :], start=True, stop=True)
                last.then_inc(c_psum, 1)
                pe.wait_ge(k_even, 4 * (j + 1))
                pe.wait_ge(k_odd, 4 * (j + 1))
                if j:
                    pe.wait_ge(s_max, j)
                for br in range(2):
                    o = (2 + 2 * br) * 512
                    for g in range(KV):
                        q = qs[:, j, 4 * g:4 * g + 4, :].rearrange("d h t -> d (h t)")
                        pe.matmul(ps[32 * g:32 * g + 32, o:o + 512], q, kt[:, br, :, g, :], start=True, stop=True)
                        last = pe.matmul(ps[32 * g:32 * g + 32, o + 512:o + W], q, keysT[br][:, g, TP:T], start=True,
                                         stop=True)
                last.then_inc(s_psum, 1)
                pe.wait_ge(s_scaled, j + 1)
                for br in range(2):
                    for c in range(4):
                        pe.transpose(ps[:, br * 512 + c * P:br * 512 + (c + 1) * P], ex[:, br, c * P:(c + 1) * P],
                                     s.ident[:, :])
                    pe.transpose(ps[0:TS, 7 * 512 + br * P:7 * 512 + (br + 1) * P], ex[:, br, 512:W], s.ident[:, :])
                pe.transpose(ps[0:8, 7 * 512 + 256:7 * 512 + 384], pcs[:, :], s.ident[:, :]).then_inc(t_psum, 1)
                pe.wait_ge(t_dve, j + 1)
                pe.wait_ge(t_act, j + 1)
                if j:
                    pe.wait_ge(o_done, j)
                else:
                    pe.wait_ge(gd_read, 1)
                for g in range(KV):
                    out = ps[0:HD, 6 * 512 + 32 * g:6 * 512 + 32 * (g + 1)]
                    r = slice(32 * g, 32 * (g + 1))
                    pe.matmul(out, s.vcn[:, j, g, :], pctT[:, r], start=True, stop=False)
                    for br in range(2):
                        for c in range(4):
                            pe.matmul(out, rows[:, j % 2, br, c, (KV + g) * HD:(KV + g + 1) * HD],
                                      pt[:, br, c * P + 32 * g:c * P + 32 * (g + 1)], start=False, stop=False)
                        last = pe.matmul(out, vals[br][0:TS, 4, g * HD:(g + 1) * HD], ptn[:, br, r], start=False,
                                         stop=(br == 1))
                last.then_inc(o_psum, 1)

        def keys_out(eng, copy, j, parity, done):
            for m in range(8 * j + parity, 8 * (j + 1), 2):
                eng.wait_ge(k_psum, m + 1)
                if j:
                    eng.wait_ge(s_psum, j)
                br, c = (m % 8) // 4, m % 4
                dst = kt[:, br, c // 2, :, (c % 2) * P:(c % 2 + 1) * P]
                copy(dst, ps[0:HD, (m % 2) * 512:(m % 2 + 1) * 512].rearrange("d (g t) -> d g t", g=KV)).then_inc(done, 1)

        @block.vector
        def _(dve):
            step = Count()

            def link(ins):
                ins.then_inc(chain, 1)
                dve.wait_ge(chain, step.add())

            for j in range(4):
                last = dve.tensor_copy(qs[:, j, :, :], s.bqT[:, :, TP + 8 * j:TP + 8 * (j + 1)])
            last.then_inc(qs_ready, 1)
            dve.wait_ge(made, 1)
            dve.tensor_scalar(icol[:, 1:2], icol[:, 0:1], 3, None, ALU.bitwise_and)
            dve.tensor_scalar(icol[:, 2:3], icol[:, 0:1], 2, 1, ALU.logical_shift_right, ALU.bitwise_and)
            dve.tensor_scalar(icol[:, 3:4], icol[:, 0:1], 7, None, ALU.bitwise_and)
            link(dve.tensor_tensor(tmp[:, 0, :], s.hm[:, :], s.slope_row[:, :], ALU.mult))
            dve.tensor_copy(t4, icol[:, 1:2])
            dve.tensor_copy(b2, icol[:, 2:3])
            dve.tensor_copy(t8, icol[:, 3:4])
            link(dve.tensor_reduce(slope, tmp[:, 0, :], AX.X, ALU.add))
            dve.tensor_scalar(b2, b2, BIG, None, ALU.mult)
            link(dve.tensor_scalar(newd[:, :, :], newd[:, :, :], t8, None, ALU.add))
            link(dve.tensor_scalar(nb2, b2, -1.0, BIG, ALU.mult, ALU.add))
            for wrong, c in ((b2, 0), (nb2, 1)):
                x = bias[:, c * PAST:(c + 1) * PAST]
                link(dve.tensor_scalar(x, x, t4, wrong, ALU.add, ALU.add))
                link(dve.tensor_scalar(x, x, slope, None, ALU.mult))
                x = cbias[:, 4 * c:4 * c + 4]
                link(dve.tensor_scalar(x, x, t4, wrong, ALU.add, ALU.add))
                link(dve.tensor_scalar(x, x, slope, None, ALU.mult))
            dve.tensor_scalar(v1[:, :, :], newd[:, :, :], 0.0, BIG, ALU.is_lt, ALU.mult)
            link(dve.tensor_scalar(v2[:, :, :], newd[:, :, :], t4, BIG, ALU.is_gt, ALU.mult))
            link(dve.tensor_tensor(newd[:, :, :], newd[:, :, :], v1[:, :, :], ALU.add))
            link(dve.tensor_tensor(newd[:, :, :], newd[:, :, :], v2[:, :, :], ALU.add))
            link(dve.tensor_scalar(newd[:, :, :], newd[:, :, :], slope, None, ALU.mult))
            dve.wait_ge(gd_psum, 1)
            for j in range(4):
                link(dve.tensor_tensor(tmp[:, :, :], ps[:, 6 * 512 + 48 * j:6 * 512 + 48 * (j + 1)]
                                       .rearrange("p (b h) -> p b h", b=3),
                                       s.hm[:, :].unsqueeze(1).broadcast_to([P, 3, BH]), ALU.mult))
                link(dve.tensor_reduce(gd[:, j, 0:3], tmp[:, :, :], AX.X, ALU.add))
            dve.tensor_copy(mark[:, 0:1], gd[:, 0, 0:1]).then_inc(gd_read, 1)
            for j in range(4):
                keys_out(dve, dve.tensor_copy, j, 0, k_even)
                link(dve.tensor_copy(bias[:, 512:W], newd[:, j, :]))
                dve.wait_ge(c_psum, j + 1)
                dve.tensor_tensor_reduce(out=pcs[:, :], in0=ps[:, 7 * 512 + 384:7 * 512 + 392], in1=cbias[:, :],
                                         scale=1.0, scalar=-3e38, op0=ALU.add, op1=ALU.max, accum_out=mx[:, 0:1])
                dve.wait_ge(s_psum, j + 1)
                for br in range(2):
                    o = (2 + 2 * br) * 512
                    last = dve.tensor_tensor_reduce(out=ex[:, br, :], in0=ps[:, o:o + W], in1=bias[:, :], scale=1.0,
                                                    scalar=-3e38, op0=ALU.add, op1=ALU.max,
                                                    accum_out=mx[:, 1 + br:2 + br])
                link(last)
                dve.tensor_scalar(mx[:, 0:3], mx[:, 0:3], -1.0, None, ALU.mult).then_inc(s_max, 1)
                dve.wait_ge(s_exp, j + 1)
                link(dve.tensor_tensor(cols[:, 8:11], cols[:, 8:11], gd[:, j, 0:3], ALU.mult))
                link(dve.reciprocal(cols[:, 8:11], cols[:, 8:11]))
                dve.tensor_scalar(pcs[:, :], pcs[:, :], cols[:, 8:9], None, ALU.mult)
                for br in range(2):
                    last = dve.tensor_scalar(ex[:, br, :], ex[:, br, :], cols[:, 9 + br:10 + br], None, ALU.mult)
                last.then_inc(s_scaled, 1)
                dve.wait_ge(t_psum, j + 1)
                dve.tensor_copy(pt[:, 0, :], ps[:, 0:512])
                dve.tensor_copy(pctT[:, :], ps[0:8, 7 * 512 + 256:7 * 512 + 384])
                dve.tensor_copy(ptn[:, :, :], ps[0:TS, 7 * 512:7 * 512 + 256].rearrange("w (b r) -> w b r", b=2))\
                   .then_inc(t_dve, 1)
                dve.wait_ge(o_psum, j + 1)
                o = ps[0:HD, 6 * 512:6 * 512 + P].rearrange("d (q e t) -> d q e t", q=BH // 2, e=2)
                for e in range(2):
                    last = dve.tensor_copy(s.ybT[HD * e:HD * (e + 1), :, TP + 8 * j:TP + 8 * (j + 1)], o[:, :, e, :])
                last.then_inc(o_done, 1)

        @block.scalar
        def _(act):
            for j in range(4):
                keys_out(act, act.copy, j, 1, k_odd)
                act.wait_ge(s_max, j + 1)
                act.activation(pcs[:, :], pcs[:, :], ACT.Exp, bias=mx[:, 0:1], accum_out=cols[:, 8:9])
                for br in range(2):
                    last = act.activation(ex[:, br, :], ex[:, br, :], ACT.Exp, bias=mx[:, 1 + br:2 + br],
                                          accum_out=cols[:, 9 + br:10 + br])
                last.then_inc(s_exp, 1)
                act.wait_ge(t_psum, j + 1)
                act.copy(pt[:, 1, :], ps[:, 512:1024]).then_inc(t_act, 1)
    sem.clear()


def stage_merge(nc, s, io):
    at = s.at
    w_raw = at("m_raw", 5632, [P, 2, 4, DC, P])
    w_lo = at("m_lo", 5632, [P, 2, 4, DC, P], F32R)
    w_hi = at("m_hi", 13824, [P, 2, 4, DC, P], F32R)
    s.mT = mT = at("mT", 36992, [P, DC, T])
    sg = at("m_gate", 50048, [P, 2, 2, HALF])
    pr = at("m_prod", 51136, [P, 2, 2, HALF])
    lows = [at("m_xlo", 1280, [P, DC, T], F32R), at("m_yalo", 32640, [P, DC, T], F32R),
            at("m_yblo", 25728, [P, DC, T], F32R)]
    XA = 6
    x_hi = [at("m_xhi_a", 22016, [P, XA, T], F32R), at("m_xhi_b", 30080, [P, DC - XA, T], F32R)]
    y_hi = [at("m_yahi", 41344, [P, DC, T], F32R), at("m_ybhi", 45696, [P, DC, T], F32R)]
    pieces = [(s.xT, lows[0], [(x_hi[0], 0, XA), (x_hi[1], XA, DC - XA)]), (s.yaT, lows[1], [(y_hi[0], 0, DC)]),
              (s.ybT, lows[2], [(y_hi[1], 0, DC)])]
    s.wo = at("wo", 43520, [P, DC, D])
    mats = [io.w_merge[:, 0:D], io.w_merge[:, D:2 * D], io.w_br_a, io.w_br_b]
    moving = [0, 0, 1, 2]
    first_use = {0: 0, 2: 1, 3: 2}

    def high_of(x, dc):
        for tensor, c0, n in pieces[x][2]:
            if c0 <= dc < c0 + n:
                return tensor[:, dc - c0, :]

    sem = Semaphores(nc)
    with ExitStack() as ctx:
        w_in = [[sem(f"m_w{i}_{m}") for m in range(4)] for i in range(2)]
        wh_done, wl_done, xh_done, xl_done = sem("m_wh"), sem("m_wl"), sem("m_xh"), sem("m_xl")
        m_psum, g_done, p_done, m_done = sem("m_psum"), sem("m_gates"), sem("m_prods"), sem("m_done")
        ps = ctx.enter_context(nc.psum_tensor("ps_g", [P, 8, 512], F32))
        block = ctx.enter_context(nc.Block())

        @block.sync
        def _(sp):
            for q in range(DC):
                if q >= 2:
                    sp.wait_ge(m_psum, 2 * (q - 1))
                for m in range(4):
                    src = mats[m][:, q * P:(q + 1) * P].rearrange("(c p) n -> p c n", p=P)
                    sp.dma_start(w_raw[:, q % 2, m, :, :], src).then_inc(w_in[q % 2][m], 16)

        @block.tensor
        def _(pe):
            for u in range(2 * DC):
                q, half = u // 2, u % 2
                toks = slice(half * HALF, (half + 1) * HALF)
                if u >= 2:
                    pe.wait_ge(p_done, u - 1)
                for m in range(4):
                    if half == 0:
                        pe.wait_ge(wl_done, 4 * q + m + 1)
                    x = moving[m]
                    if u == 0 and m in first_use:
                        pe.wait_ge(xl_done, x + 1)
                    out = ps[:, 4 * (u % 2) + m, 0:HALF]
                    for dc in range(DC):
                        pe.matmul(out, w_hi[:, q % 2, m, dc, :], high_of(x, dc)[:, toks], start=(dc == 0), stop=False)
                        pe.matmul(out, w_hi[:, q % 2, m, dc, :], lows[x][:, dc, toks], start=False, stop=False)
                        last = pe.matmul(out, w_lo[:, q % 2, m, dc, :], high_of(x, dc)[:, toks], start=False,
                                         stop=(dc == DC - 1))
                last.then_inc(m_psum, 1)

        @block.scalar
        def _(act):
            def high(q, m):
                act.wait_ge(w_in[q % 2][m], 16 * (q // 2 + 1))
                if q >= 2 and m == 0:
                    act.wait_ge(m_psum, 2 * (q - 1))
                act.copy(w_hi[:, q % 2, m, :, :], w_raw[:, q % 2, m, :, :]).then_inc(wh_done, 1)

            for m in range(4):
                if m in first_use:
                    src, _, parts = pieces[first_use[m]]
                    for tensor, c0, n in parts:
                        last = act.copy(tensor[:, :, :], src[:, c0:c0 + n, :])
                    last.then_inc(xh_done, 1)
                high(0, m)
            for u in range(2 * DC):
                if u % 2 == 0 and u // 2 + 1 < DC:
                    for m in range(4):
                        high(u // 2 + 1, m)
                act.wait_ge(m_psum, u + 1)
                if u >= 2:
                    act.wait_ge(p_done, u - 1)
                for b in range(2):
                    last = act.activation(sg[:, u % 2, b, :], ps[:, 4 * (u % 2) + b, 0:HALF], ACT.Sigmoid)
                last.then_inc(g_done, 1)

        @block.vector
        def _(dve):
            def low(q, m):
                dve.wait_ge(wh_done, 4 * q + m + 1)
                dve.tensor_tensor(w_lo[:, q % 2, m, :, :], w_raw[:, q % 2, m, :, :], w_hi[:, q % 2, m, :, :].bitcast(F32),
                                  ALU.subtract).then_inc(wl_done, 1)

            for m in range(4):
                if m in first_use:
                    x = first_use[m]
                    src, low_part, parts = pieces[x]
                    dve.wait_ge(xh_done, x + 1)
                    for tensor, c0, n in parts:
                        last = dve.tensor_tensor(low_part[:, c0:c0 + n, :], src[:, c0:c0 + n, :],
                                                 tensor[:, :, :].bitcast(F32), ALU.subtract)
                    last.then_inc(xl_done, 1)
                low(0, m)
            for u in range(2 * DC):
                ec, half = u // 2, u % 2
                if half == 0 and ec + 1 < DC:
                    for m in range(4):
                        low(ec + 1, m)
                dve.wait_ge(g_done, u + 1)
                if u >= 2:
                    dve.wait_ge(m_done, u - 1)
                for b in range(2):
                    last = dve.tensor_tensor(pr[:, u % 2, b, :], ps[:, 4 * (u % 2) + 2 + b, 0:HALF], sg[:, u % 2, b, :],
                                             ALU.mult)
                last.then_inc(p_done, 1)
                dve.wait_ge(p_done, u + 1)
                dve.tensor_tensor(mT[:, ec, half * HALF:(half + 1) * HALF], pr[:, u % 2, 0, :], pr[:, u % 2, 1, :],
                                  ALU.add).then_inc(m_done, 1)
    sem.clear()


def norm_rows(dve, link, x, st, mv, rs, eps_done, sqrt_done, n, g, b, rows):
    link(dve.bn_stats(st[0:rows, 0, :], x[:, 0:512]))
    link(dve.bn_stats(st[0:rows, 1, :], x[:, 512:D]))
    link(dve.bn_aggr(mv[0:rows, :], st[0:rows, :, :].rearrange("p a b -> p (a b)")))
    dve.tensor_scalar(rs[0:rows, 0:1], mv[0:rows, 1:2], LN_EPS, None, ALU.add).then_inc(eps_done, 1)
    dve.wait_ge(sqrt_done, n + 1)
    link(dve.reciprocal(rs[0:rows, 1:2], rs[0:rows, 0:1]))
    link(dve.tensor_scalar(x, x, mv[0:rows, 0:1], rs[0:rows, 1:2], ALU.subtract, ALU.mult))
    link(dve.tensor_tensor(x, x, g[0:rows, :], ALU.mult))
    return dve.tensor_tensor(x, x, b[0:rows, :], ALU.add)


QW = 256
NQ = PH * 2


def stage_norm1(nc, s, io):
    at = s.at
    s.q_ring = at("q_ring", 14000, [P, 3, DC, QW])
    s.keys = at("keys", 20144, [P, NQ, P])
    xr = at("xr", 22704, [P, 2, D])
    hr = at("hr", 24752, [P, 2, D])
    gb = at("ln1_gb", 26800, [P, 2, D])
    st = at("ln1_st", 28848, [P, 2, 6])
    mv = at("ln1_mv", 28864, [P, 2])
    rs = at("ln1_rs", 28872, [P, 2])
    s.hT = at("hT", 9648, [P, DC, T])
    s.hTh = at("hTh", 944, [P, DC, T], F32R)
    s.hTl = at("hTl", 5296, [P, DC, T], F32R)
    sem = Semaphores(nc)
    with ExitStack() as ctx:
        x_in, gb_in, o_psum, o_read, chain, eps_done, sqrt_done = ([sem("n_x0"), sem("n_x1")], sem("n_gb"), sem("n_psum"),
                                                                  sem("n_read"), sem("n_chain"), sem("n_eps"), sem("n_sqrt"))
        h_ready, h_sent, t_psum, t_hi, t_lo = sem("n_h"), [sem("n_sent0"), sem("n_sent1")], sem("n_tp"), sem("n_hi"), sem("n_lo")
        wo_in = [sem("wo_in0"), sem("wo_in1")]
        ps = ctx.enter_context(nc.psum_tensor("ps_n", [P, 8, 512], F32))
        block = ctx.enter_context(nc.Block())

        def x_rows(t):
            return io.x_prompt[0, t * P:(t + 1) * P, :] if t < 4 else io.x_sample.rearrange("b t d -> (b t) d")

        @block.sync
        def _(sp):
            for q in range(2):
                src = io.w_out[:, q * 512:(q + 1) * 512].rearrange("(c p) n -> p c n", p=P)
                sp.dma_start(s.wo[:, :, q * 512:(q + 1) * 512], src).then_inc(wo_in[q], 16)
            sp.dma_start(gb[:, 0, :], io.ln1_g.partition_broadcast(P)).then_inc(gb_in, 16)
            sp.dma_start(gb[:, 1, :], io.ln1_b.partition_broadcast(P)).then_inc(gb_in, 16)
            for t in range(NT):
                if t >= 2:
                    sp.wait_ge(h_ready, t - 1)
                sp.dma_start(xr[0:ROWS[t], t % 2, :], x_rows(t)).then_inc(x_in[t % 2], 16)
            for q in range(3):
                sp.dma_start(s.q_ring[:, q, :, :], io.peer_wq[:, q * QW:(q + 1) * QW].rearrange("(c p) n -> p c n", p=P))\
                  .then_inc(s.wq_in[q], 16)
                if q == 0:
                    sp.dma_start(s.keys[:, :, :], io.peer_keys.rearrange("h c n d -> n (h c) d")).then_inc(s.keys_in, 16)

        @block.gpsimd
        def _(pool):
            for t in range(NT):
                pool.wait_ge(h_ready, t + 1)
                pool.dma_start(io.h_rows[t * P:t * P + ROWS[t], :], hr[0:ROWS[t], t % 2, :]).then_inc(h_sent[t % 2], 16)
            pool.wait_ge(h_sent[0], 48)
            pool.wait_ge(h_sent[1], 32)

        @block.tensor
        def _(pe):
            def turn(t):
                pe.wait_ge(h_ready, t + 1)
                for q in range(2):
                    n = 2 * t + q
                    if n >= 4:
                        pe.wait_ge(t_lo, n - 3)
                    for c in range(4):
                        last = pe.transpose(ps[:, 4 + n % 4, c * P:c * P + ROWS[t]],
                                            hr[0:ROWS[t], t % 2, (4 * q + c) * P:(4 * q + c + 1) * P],
                                            s.ident[0:ROWS[t], 0:ROWS[t]])
                    last.then_inc(t_psum, 1)

            for t in range(NT):
                if t >= 2:
                    pe.wait_ge(o_read, t - 1)
                for q in range(2):
                    if t == 0:
                        pe.wait_ge(wo_in[q], 16)
                    for dc in range(DC):
                        last = pe.matmul(ps[0:ROWS[t], 2 * (t % 2) + q, :], s.mT[:, dc, t * P:t * P + ROWS[t]],
                                         s.wo[:, dc, q * 512:(q + 1) * 512], start=(dc == 0), stop=(dc == DC - 1))
                last.then_inc(o_psum, 1)
                if t:
                    turn(t - 1)
            turn(NT - 1)

        @block.vector
        def _(dve):
            step = Count()

            def link(ins):
                ins.then_inc(chain, 1)
                dve.wait_ge(chain, step.add())

            def low(t):
                for q in range(2):
                    n = 2 * t + q
                    dve.wait_ge(t_hi, n + 1)
                    src = ps[:, 4 + n % 4, :].rearrange("p (c t) -> p c t", c=4)[:, :, 0:ROWS[t]]
                    cs, ts = slice(4 * q, 4 * q + 4), slice(t * P, t * P + ROWS[t])
                    dve.tensor_tensor(s.hTl[:, cs, ts], src, s.hTh[:, cs, ts].bitcast(F32), ALU.subtract).then_inc(t_lo, 1)

            dve.wait_ge(gb_in, 32)
            for t in range(NT):
                r = ROWS[t]
                dve.wait_ge(o_psum, t + 1)
                dve.wait_ge(x_in[t % 2], 16 * (t // 2 + 1))
                if t >= 2:
                    dve.wait_ge(h_sent[t % 2], 16 * (t // 2))
                    dve.wait_ge(t_psum, 2 * (t - 1))
                for q in range(2):
                    last = dve.scalar_tensor_tensor(out=hr[0:r, t % 2, q * 512:(q + 1) * 512],
                                                    in0=xr[0:r, t % 2, q * 512:(q + 1) * 512], scalar=DN_ALPHA,
                                                    in1=ps[0:r, 2 * (t % 2) + q, :], op0=ALU.mult, op1=ALU.add)
                last.then_inc(o_read, 1)
                dve.wait_ge(o_read, t + 1)
                norm_rows(dve, link, hr[0:r, t % 2, :], st, mv, rs, eps_done, sqrt_done, t, gb[:, 0, :], gb[:, 1, :], r)\
                    .then_inc(h_ready, 1)
                if t:
                    low(t - 1)
            low(NT - 1)

        @block.scalar
        def _(act):
            def high(t):
                for q in range(2):
                    n = 2 * t + q
                    act.wait_ge(t_psum, n + 1)
                    src = ps[:, 4 + n % 4, :].rearrange("p (c t) -> p c t", c=4)[:, :, 0:ROWS[t]]
                    cs, ts = slice(4 * q, 4 * q + 4), slice(t * P, t * P + ROWS[t])
                    act.copy(s.hT[:, cs, ts], src)
                    act.copy(s.hTh[:, cs, ts], src).then_inc(t_hi, 1)

            for t in range(NT):
                r = ROWS[t]
                act.wait_ge(eps_done, t + 1)
                act.activation(rs[0:r, 0:1], rs[0:r, 0:1], ACT.Sqrt).then_inc(sqrt_done, 1)
                if t:
                    high(t - 1)
            high(NT - 1)
    sem.clear()


def top_two(dve, link, values, tops, idxs):
    def every(f):
        for i in range(len(values)):
            last = f(i)
        link(last)

    every(lambda i: dve.max(out=tops[i][:, 0:8], in_=values[i]))
    every(lambda i: dve.max_index(out=idxs[i][:, 0:8], in_max=tops[i][:, 0:8], in_values=values[i]))
    every(lambda i: dve.match_replace(out=values[i], in_to_replace=tops[i][:, 0:8], in_values=values[i],
                                      imm_value=-3.4e38))
    every(lambda i: dve.max(out=tops[i][:, 8:16], in_=values[i]))
    every(lambda i: dve.max_index(out=idxs[i][:, 8:16], in_max=tops[i][:, 8:16], in_values=values[i]))


def stage_query(nc, s, io):
    at = s.at
    f0 = 14000
    ring, keys = s.q_ring, s.keys
    keysT = at("keysT", f0 + 8192, [P, NQ, P])
    qt = at("q_T", f0 + 10240, [P, 4, T])
    sc = at("key_scores", f0 + 12416, [P, NT, NQ, PK])
    s.top1 = top1 = at("top1", f0 + 22656, [P, NT, NQ, TOPK])
    s.idx1 = idx1 = at("idx1", f0 + 23936, [P, NT, NQ, TOPK], U32)
    NC = 16 + 7 * 8 + 8
    s.chosen = chosen = at("chosen", f0, [P, 3, T])
    b0 = f0 + 25224
    res = at("res", b0, [P, NT, 3, PH, TOPK])
    top2 = at("top2", b0 + 1920, [P, NT, PH, TOPK])
    HC = 4
    cand = at("cand", b0 + 2560, [P, HC, NC])
    idx2 = at("idx2", b0 + 2880, [P, HC * TOPK], U32)
    part = at("part", b0 + 2944, [P, HC * TOPK], U32)
    placef = at("placef", b0 + 3008, [P, 2, HC * TOPK])
    partf = at("partf", b0 + 3136, [P, 2, HC * TOPK])
    shift = at("shift", b0 + 3264, [P, HC * TOPK])
    idxf = at("idxf", b0 + 3328, [P, 2, 2, HC, TOPK])
    oh = at("oh", b0 + 3584, [P, 2, 2, HC * TOPK, TOPK])
    sums = at("sums", b0 + 7680, [P, PH])
    i16 = at("i16", b0 + 7688, [P, TOPK])
    picks = [(h0, t) for h0 in range(0, PH, HC) for t in range(NT)]
    sem = Semaphores(nc)
    with ExitStack() as ctx:
        i_ready, e_in, e_done, res_ready, r_psum, r_done = (sem("sel_iota"), sem("sel_ein"), sem("sel_edone"),
                                                            sem("sel_res"), sem("sel_psum"), sem("sel_done"))
        w_in, keys_in, kt_psum, kt_done = s.wq_in, s.keys_in, sem("kt_psum"), sem("kt_done")
        q_psum, q_done, sc_psum, sc_done = sem("q_psum"), sem("q_done"), sem("ksc_psum"), sem("ksc_done")
        chain, oh_ready, oh_done = sem("q_chain"), sem("oh_ready"), sem("oh_done")
        ps = ctx.enter_context(nc.psum_tensor("ps_q", [P, 8, 512], F32))
        block = ctx.enter_context(nc.Block())

        @block.sync
        def _(sp):
            for q in range(3, NQ // 2):
                sp.wait_ge(q_psum, 4 * (q - 2))
                sp.dma_start(ring[:, q % 3, :, :], io.peer_wq[:, q * QW:(q + 1) * QW].rearrange("(c p) n -> p c n", p=P))\
                  .then_inc(w_in[q % 3], 16)

        @block.gpsimd
        def _(pool):
            pool.iota(i16[:, :], pattern=[[1, TOPK]], base=0, channel_multiplier=0,
                      allow_small_or_imprecise_dtypes=True).then_inc(i_ready, 1)
            for m, (_, t) in enumerate(picks):
                pool.wait_ge(oh_ready, m + 1)
                for c in range(2):
                    o = oh[0:ROWS[t], m % 2, c, :, :].rearrange("p (h k) n -> p h k n", h=HC)
                    num = idxf[0:ROWS[t], m % 2, c, :, :].unsqueeze(2).broadcast_to([ROWS[t], HC, TOPK, TOPK])
                    last = pool.tensor_tensor(o, o, num, ALU.mult)
                last.then_inc(oh_done, 1)

        @block.tensor
        def _(pe):
            pe.wait_ge(keys_in, 16)
            for n in range(4):
                for c in range(4):
                    last = pe.transpose(ps[:, 4 + n, c * P:(c + 1) * P], keys[:, 4 * n + c, :], s.ident[:, :])
                last.then_inc(kt_psum, 1)

            def score(grp):
                pe.wait_ge(q_done, 8 * (grp + 1))
                pe.wait_ge(kt_done, 4)
                for t in range(NT):
                    n = NT * grp + t
                    if n >= 4:
                        pe.wait_ge(sc_done, n - 3)
                    for c in range(4):
                        last = pe.matmul(ps[0:ROWS[t], 4 + n % 4, c * P:(c + 1) * P], qt[:, c, t * P:t * P + ROWS[t]],
                                         keysT[:, 4 * grp + c, :], start=True, stop=True)
                    last.then_inc(sc_psum, 1)

            for x in range(NQ):
                if x % 2 == 0:
                    pe.wait_ge(w_in[(x // 2) % 3], 16 * (x // 6 + 1))
                for half in range(2):
                    u = 2 * x + half
                    if u >= 4:
                        pe.wait_ge(q_done, u - 3)
                    for dc in range(DC):
                        last = pe.matmul(ps[:, u % 4, 0:HALF], ring[:, (x // 2) % 3, dc, (x % 2) * P:(x % 2 + 1) * P],
                                         s.hT[:, dc, half * HALF:(half + 1) * HALF], start=(dc == 0), stop=(dc == DC - 1))
                    last.then_inc(q_psum, 1)
                if x % 4 == 3:
                    score(x // 4)
            for t in range(NT):
                r = ROWS[t]
                pe.wait_ge(res_ready, t + 1)
                if t >= 4:
                    pe.wait_ge(r_done, t - 3)
                for i in range(3):
                    last = pe.transpose(ps[:, t % 4, i * P:i * P + r],
                                        res[0:r, t, i, :, :].rearrange("p h k -> p (h k)"), s.ident[0:r, 0:r])
                last.then_inc(r_psum, 1)

        @block.scalar
        def _(act):
            for u in range(2 * NQ):
                act.wait_ge(q_psum, u + 1)
                x = u // 2
                if x >= 4:
                    act.wait_ge(sc_psum, NT * (x // 4))
                act.copy(qt[:, x % 4, (u % 2) * HALF:(u % 2 + 1) * HALF], ps[:, u % 4, 0:HALF]).then_inc(q_done, 1)
                if u % 8 == 7:
                    grp = u // 8
                    for t in range(NT):
                        n = NT * grp + t
                        act.wait_ge(sc_psum, n + 1)
                        act.copy(sc[0:ROWS[t], t, 4 * grp:4 * grp + 4, :],
                                 ps[0:ROWS[t], 4 + n % 4, :].rearrange("p (c k) -> p c k", c=4)).then_inc(sc_done, 1)
            for t in range(NT):
                r = ROWS[t]
                act.wait_ge(e_in, t + 1)
                act.activation(res[0:r, t, 0, :, :], res[0:r, t, 0, :, :], ACT.Exp).then_inc(e_done, 1)
                act.wait_ge(r_psum, t + 1)
                act.copy(chosen[:, :, t * P:t * P + r],
                         ps[:, t % 4, 0:384].rearrange("p (i t) -> p i t", i=3)[:, :, 0:r]).then_inc(r_done, 1)

        @block.vector
        def _(dve):
            step = Count()

            def link(ins):
                ins.then_inc(chain, 1)
                dve.wait_ge(chain, step.add())

            for n in range(4):
                dve.wait_ge(kt_psum, n + 1)
                dve.tensor_copy(keysT[:, 4 * n:4 * n + 4, :], ps[:, 4 + n, :].rearrange("p (c k) -> p c k", c=4))\
                   .then_inc(kt_done, 1)

            def choose(m, h0, t, r):
                v = top1[0:r, t, 2 * h0:2 * (h0 + HC), :].rearrange("p (h c) k -> p h c k", c=2)
                first, second = v[:, :, 0, :], v[:, :, 1, :]
                dve.tensor_tensor(cand[0:r, :, 0:16], first[:, :, 0:1].broadcast_to([r, HC, 16]), second, ALU.add)
                dve.tensor_tensor(cand[0:r, :, 16:72].rearrange("p h (a b) -> p h a b", b=8),
                                  first[:, :, 1:8].unsqueeze(3).broadcast_to([r, HC, 7, 8]),
                                  second[:, :, 0:8].unsqueeze(2).broadcast_to([r, HC, 7, 8]), ALU.add)
                dve.tensor_copy(idxf[0:r, m % 2, :, :, :].rearrange("p c h k -> p h c k"),
                                idx1[0:r, t, 2 * h0:2 * (h0 + HC), :].rearrange("p (h c) k -> p h c k", c=2))
                link(dve.tensor_tensor(cand[0:r, :, 72:80], first[:, :, 8:16],
                                       second[:, :, 0:1].broadcast_to([r, HC, 8]), ALU.add))
                top_two(dve, link, [cand[0:r, h, :] for h in range(HC)], [top2[0:r, t, h0 + h, :] for h in range(HC)],
                        [idx2[0:r, h * TOPK:(h + 1) * TOPK] for h in range(HC)])
                p_f, p_8, a_f, b_f = placef[0:r, 0, :], placef[0:r, 1, :], partf[0:r, 0, :], partf[0:r, 1, :]
                link(dve.tensor_copy(p_f, idx2[0:r, :]))
                dve.tensor_scalar(shift[0:r, :], p_f, 16.0, -8.0, ALU.is_ge, ALU.mult)
                link(dve.tensor_scalar(p_8, p_f, -8.0, 0.0, ALU.add, ALU.max))
                link(dve.tensor_copy(part[0:r, :], p_8))
                link(dve.tensor_scalar(part[0:r, :], part[0:r, :], 3, None, ALU.logical_shift_right))
                link(dve.tensor_copy(p_8, part[0:r, :]))
                link(dve.scalar_tensor_tensor(out=a_f, in0=p_f, scalar=-64.0, in1=p_8, op0=ALU.add, op1=ALU.max))
                link(dve.scalar_tensor_tensor(out=b_f, in0=a_f, scalar=-8.0, in1=p_f, op0=ALU.mult, op1=ALU.add))
                link(dve.tensor_tensor(b_f, b_f, shift[0:r, :], ALU.add))
                link(dve.tensor_scalar(b_f, b_f, 0.0, None, ALU.max))
                full = [r, 2, HC * TOPK, TOPK]
                dve.tensor_tensor(oh[0:r, m % 2, :, :, :], partf[0:r, :, :].unsqueeze(3).broadcast_to(full),
                                  i16[0:r, :].unsqueeze(1).unsqueeze(1).broadcast_to(full), ALU.is_equal)\
                   .then_inc(oh_ready, 1)

            def finish(m, h0, t, r):
                dve.wait_ge(oh_done, m + 1)
                link(dve.tensor_reduce(res[0:r, t, 1:3, h0:h0 + HC, :].rearrange("p c h k -> p c (h k)"),
                                       oh[0:r, m % 2, :, :, :], AX.X, ALU.add))
                if h0 + HC == PH:
                    gate_softmax(t, r)

            def gate_softmax(t, r):
                dve.tensor_tensor(res[0:r, t, 0, :, :], top2[0:r, t, :, :],
                                  top2[0:r, t, :, 0:1].broadcast_to([r, PH, TOPK]), ALU.subtract).then_inc(e_in, 1)
                dve.wait_ge(e_done, t + 1)
                link(dve.tensor_reduce(sums[0:r, :], res[0:r, t, 0, :, :], AX.X, ALU.add))
                link(dve.reciprocal(sums[0:r, :], sums[0:r, :]))
                dve.tensor_tensor(res[0:r, t, 0, :, :], res[0:r, t, 0, :, :],
                                  sums[0:r, :].unsqueeze(2).broadcast_to([r, PH, TOPK]), ALU.mult).then_inc(res_ready, 1)

            dve.wait_ge(i_ready, 1)
            for n in range(NT * NQ // 4):
                grp, t = n // NT, n % NT
                r = ROWS[t]
                dve.wait_ge(sc_done, n + 1)
                xs = range(4 * grp, 4 * grp + 4)
                top_two(dve, link, [sc[0:r, t, x, :] for x in xs], [top1[0:r, t, x, :] for x in xs],
                        [idx1[0:r, t, x, :] for x in xs])
                if grp % 2 == 1:
                    m = picks.index((2 * grp - 2, t))
                    choose(m, *picks[m], r)
                    if m:
                        finish(m - 1, *picks[m - 1], ROWS[picks[m - 1][1]])
            finish(len(picks) - 1, *picks[-1], r)
    sem.clear()




TB = 32
GJ = 4
NG = PK // GJ


def stage_gates(nc, s, io):
    at = s.at
    c0 = 15632
    cols = at("g_cols", c0, [P, 2, 3, TB])
    one_a = at("one_a", c0 + 192, [P, 2, 4, PK])
    one_b = at("one_b", c0 + 1216, [P, 2, 4, PK])
    i128 = at("i128", c0 + 2240, [P, PK])
    scratch = at("g_scratch", c0 + 2368 + 2 * NG * TB * GJ, [P, 2])
    buf = at("g_buf", c0 + 2368, [P, 2, NG, TB, GJ])
    NB = T // TB
    QD = TB // 4
    sem = Semaphores(nc)
    with ExitStack() as ctx:
        i_ready, cols_ready, a_ready, b_ready, g_psum, g_done = (sem("gt_iota"), sem("gt_cols"), sem("gt_a"), sem("gt_b"),
                                                                sem("gt_psum"), sem("gt_done"))
        sent = [sem("gt_sent0"), sem("gt_sent1")]
        ps = ctx.enter_context(nc.psum_tensor("ps_t", [P, 4, 512], F32))
        block = ctx.enter_context(nc.Block())

        def blocks(eng, body):
            body(0, 0, True)
            body(1, 0, True)
            with eng.Fori(1, NB // 2) as i:
                body(0, i, False)
                body(1, i, False)
            body(0, NB // 2, False)

        @block.gpsimd
        def _(pool):
            pool.iota(i128[:, :], pattern=[[1, PK]], base=0, channel_multiplier=0,
                      allow_small_or_imprecise_dtypes=True).then_inc(i_ready, 1)
            pool.wait_ge(i_ready, 1)

            def body(u, i, first):
                pool.wait_ge(cols_ready, i * 2 + (u + 1))
                for q in range(QD):
                    if not (first and u == 0 and q < 2):
                        pool.wait_ge(g_psum, i * (2 * QD) + (u * QD + q - 1))
                    pool.tensor_tensor(scratch[:, q % 2:q % 2 + 1], i128[:, 0:1], i128[:, 0:1], ALU.add)
                    for c in range(2):
                        t = 4 * q + c
                        last = pool.tensor_scalar(one_a[:, q % 2, c, :], i128[:, :], cols[:, u, 1, t:t + 1], None,
                                                  ALU.is_equal)
                    last.then_inc(a_ready, 1)

            blocks(pool, body)

        @block.vector
        def _(dve):
            dve.wait_ge(i_ready, 1)

            def body(u, i, first):
                if not first:
                    dve.wait_ge(a_ready, i * (2 * QD) + (u - 1) * QD)
                    dve.wait_ge(b_ready, i * (2 * QD) + (u - 1) * QD)
                dve.tensor_copy(cols[:, u, :, :], s.chosen[:, :, bass.ds(i * (2 * TB) + u * TB, TB)])\
                   .then_inc(cols_ready, 1)
                dve.wait_ge(cols_ready, i * 2 + (u + 1))
                for q in range(QD):
                    if not (first and u == 0 and q < 2):
                        dve.wait_ge(g_psum, i * (2 * QD) + (u * QD + q - 1))
                    for c in range(4):
                        t = 4 * q + c
                        dve.tensor_scalar(one_b[:, q % 2, c, :], i128[:, :], cols[:, u, 2, t:t + 1],
                                          cols[:, u, 0, t:t + 1], ALU.is_equal, ALU.mult)
                    full = [P, 2, PK]
                    dve.tensor_tensor(one_a[:, q % 2, 2:4, :], i128[:, :].unsqueeze(1).broadcast_to(full),
                                      cols[:, u, 1, 4 * q + 2:4 * q + 4].unsqueeze(2).broadcast_to(full),
                                      ALU.is_equal).then_inc(b_ready, 1)

            blocks(dve, body)

        @block.tensor
        def _(pe):
            def body(u, i, first):
                for q in range(QD):
                    pe.wait_ge(a_ready, i * (2 * QD) + (u * QD + q + 1))
                    pe.wait_ge(b_ready, i * (2 * QD) + (u * QD + q + 1))
                    if not (first and u == 0 and q < 4):
                        pe.wait_ge(g_done, i * (2 * QD) + (u * QD + q - 3))
                    for c in range(4):
                        last = pe.matmul(ps[:, q % 4, c * P:(c + 1) * P], one_a[:, q % 2, c, :], one_b[:, q % 2, c, :],
                                         start=True, stop=True)
                    last.then_inc(g_psum, 1)

            blocks(pe, body)

        @block.scalar
        def _(act):
            def body(u, i, first):
                if not first:
                    act.wait_ge(sent[u], i * 16)
                for q in range(QD):
                    act.wait_ge(g_psum, i * (2 * QD) + (u * QD + q + 1))
                    act.copy(buf[:, u, :, 4 * q:4 * q + 4, :].rearrange("p g t j -> p t g j"),
                             ps[:, q % 4, :].rearrange("p (t g j) -> p t g j", t=4, j=GJ)).then_inc(g_done, 1)

            blocks(act, body)

        @block.sync
        def _(sp):
            def body(u, i, first):
                sp.wait_ge(g_done, i * (2 * QD) + (u + 1) * QD)
                dst = io.gates[:, :, bass.ds(i * (2 * TB * GJ) + u * TB * GJ, TB * GJ)].rearrange("g p x -> p g x")
                sp.dma_start(dst, buf[:, u, :, :, :].rearrange("p g t j -> p g (t j)")).then_inc(sent[u], 16)

            blocks(sp, body)
            sp.wait_ge(sent[0], 16 * (NB - NB // 2))
            sp.wait_ge(sent[1], 16 * (NB // 2))
    sem.clear()


def stage_experts(nc, s, io):
    at = s.at
    s.outT = outT = at("outT", 9648, [P, DC, T])
    vlo_raw = [at(f"v_raw{i}", 14000 + 4096 * i, [P, GJ, D]) for i in range(2)]
    vlo = [at(f"v_lo{i}", 14000 + 4096 * i, [P, GJ, D], F32R) for i in range(2)]
    vhi = [at(f"v_hi{i}", 22192 + 4096 * i, [P, GJ, D], F32R) for i in range(2)]
    u_raw = at("u_raw", 30384, [P, 2, D])
    u_lo = at("u_lo", 30384, [P, 2, D], F32R)
    u_hi = at("u_hi", 32432, [P, 2, D], F32R)
    uT_hi = at("uT_hi", 34480, [P, 2, DC, P], F32R)
    uT_lo = at("uT_lo", 36528, [P, 2, DC, P], F32R)
    ga = at("gelu", 38576, [P, 2, HALF])
    wt = at("e_w", 39120, [P, 2, HALF])
    whi = at("e_whi", 39664, [P, 2, GJ, T], F32R)
    wlo = at("e_wlo", 44016, [P, 2, GJ, T], F32R)
    gt = at("e_gate", 48368, [P, 2, T, GJ])
    ident_r = at("ident_r", 52720, [P, P], F32R)
    hTh, hTl = s.hTh, s.hTl
    u_v = io.peer_u.rearrange("(a b) d -> a b d", a=PK)
    v_v = io.peer_v.rearrange("(a b) d -> a b d", a=PK)
    sem = Semaphores(nc)
    with ExitStack() as ctx:
        u_in = [sem(f"u_in{i}") for i in range(2)]
        uh_done, ul_done = sem("u_high_done"), sem("u_low_done")
        hi_psum, lo_psum, hT_done, lT_done = sem("u_hi_psum"), sem("u_lo_psum"), sem("uT_hi_done"), sem("uT_lo_done")
        h_psum, gelu_done, w_mul, wh_done, w_done = (sem("eh_psum"), sem("gelu_done"), sem("w_mul"), sem("wh_done"),
                                                     sem("w_done"))
        v_in = [sem(f"v_in{i}") for i in range(2)]
        g_in = [sem(f"g_in{i}") for i in range(2)]
        vh_done, vl_done, o_psum, o_done = sem("vh_done"), sem("vl_done"), sem("eo_psum"), sem("eo_done")
        zeroed, ident_done = sem("zeroed"), sem("ident_r_done")
        ps = ctx.enter_context(nc.psum_tensor("ps_ex", [P, 8, 512], F32))
        block = ctx.enter_context(nc.Block())
        NO = 2 * DC

        def of(per, i, u, c, off=0):
            return i * (2 * GJ * per) + ((u * GJ + c) * per + off)

        def due(value):
            return not isinstance(value, int) or value > 0

        @block.sync
        def _(sp):
            def load(i, u, c):
                if due(of(2, i, u, c, -2)):
                    sp.wait_ge(lo_psum, of(2, i, u, c, -2))
                src = u_v[:, bass.ds(of(1, i, u, c), 1), :].rearrange("a o d -> a (o d)")
                sp.dma_start(u_raw[:, c % 2, :], src).then_inc(u_in[c % 2], 16)

            for c in range(2 * GJ):
                load(0, 0, c)
            with sp.Fori(1, NG // 2) as i:
                for c in range(2 * GJ):
                    load(i, 0, c)

        @block.gpsimd
        def _(pool):
            def body(u, i):
                if due(of(2, i, u, 0, -2 * GJ)):
                    pool.wait_ge(w_mul, of(2, i, u, 0, -2 * GJ))
                src = io.gates[bass.ds(i * 2 + u, 1)].rearrange("o p x -> (o p) x")
                pool.dma_start(gt[:, u, :, :].rearrange("p t j -> p (t j)"), src).then_inc(g_in[u], 16)
                if due(i * (2 * NO) + (u * NO - NO)):
                    pool.wait_ge(o_psum, i * (2 * NO) + (u * NO - NO))
                src = v_v[:, bass.ds(i * (2 * GJ) + u * GJ, GJ), :]
                pool.dma_start(vlo_raw[u][:, :, :], src).then_inc(v_in[u], 16)

            body(0, 0)
            body(1, 0)
            with pool.Fori(1, NG // 2) as i:
                body(0, i)
                body(1, i)

        @block.tensor
        def _(pe):
            def turn_high(i, u, c):
                pe.wait_ge(uh_done, of(1, i, u, c, 1))
                for b in range(2):
                    if due(of(2, i, u, c, b - 1)):
                        pe.wait_ge(lT_done, of(2, i, u, c, b - 1))
                    for q in range(4):
                        dc = 4 * b + q
                        last = pe.matmul(ps[:, b, q * P:(q + 1) * P], u_hi[:, c % 2, dc * P:(dc + 1) * P],
                                         ident_r[:, :], start=True, stop=True)
                    last.then_inc(hi_psum, 1)

            def turn_low(i, u, c):
                pe.wait_ge(ul_done, of(1, i, u, c, 1))
                for b in range(2):
                    pe.wait_ge(hT_done, of(2, i, u, c, b + 1))
                    for q in range(4):
                        dc = 4 * b + q
                        last = pe.matmul(ps[:, b, q * P:(q + 1) * P], u_lo[:, c % 2, dc * P:(dc + 1) * P],
                                         ident_r[:, :], start=True, stop=True)
                    last.then_inc(lo_psum, 1)

            def hidden(i, u, c, half):
                pe.wait_ge(hT_done, of(2, i, u, c, 2))
                if due(of(2, i, u, c, half - 3)):
                    pe.wait_ge(gelu_done, of(2, i, u, c, half - 3))
                out = ps[:, 2 + 2 * (c % 2) + half, 0:HALF]
                cols = slice(half * HALF, (half + 1) * HALF)
                pairs = [(uT_hi, hTh, dc) for dc in range(DC)] + [(uT_hi, hTl, dc) for dc in range(DC)] + \
                        [(uT_lo, hTh, dc) for dc in range(DC)]
                for n, (ut, ht, dc) in enumerate(pairs):
                    if n == 2 * DC:
                        pe.wait_ge(lT_done, of(2, i, u, c, 2))
                    last = pe.matmul(out, ut[:, c % 2, dc, :], ht[:, dc, cols], start=(n == 0), stop=(n == 3 * DC - 1))
                last.then_inc(h_psum, 1)

            def outputs(i, u):
                pe.wait_ge(w_done, of(2, i, u, GJ))
                pe.wait_ge(vl_done, of(1, i, u, GJ))
                for n in range(NO):
                    dc, half = n // 2, n % 2
                    if due(i * (2 * NO) + (u * NO + n - 1)):
                        pe.wait_ge(o_done, i * (2 * NO) + (u * NO + n - 1))
                    out = ps[:, 6 + n % 2, 0:HALF]
                    cols, rows = slice(half * HALF, (half + 1) * HALF), slice(dc * P, (dc + 1) * P)
                    for c in range(GJ):
                        pe.matmul(out, vhi[u][:, c, rows], whi[:, u, c, cols], start=(c == 0), stop=False)
                        pe.matmul(out, vhi[u][:, c, rows], wlo[:, u, c, cols], start=False, stop=False)
                        last = pe.matmul(out, vlo[u][:, c, rows], whi[:, u, c, cols], start=False, stop=(c == GJ - 1))
                    last.then_inc(o_psum, 1)

            def body(u, i, end):
                for c in range(GJ):
                    ahead = not (end and c == GJ - 1)
                    if ahead:
                        turn_high(i, u, c + 1)
                    hidden(i, u, c, 0)
                    if ahead:
                        turn_low(i, u, c + 1)
                    hidden(i, u, c, 1)
                    if c == 0 and not (isinstance(i, int) and i == 0 and u == 0):
                        outputs(i if u == 1 else i - 1, 1 - u)

            pe.wait_ge(ident_done, 1)
            turn_high(0, 0, 0)
            turn_low(0, 0, 0)
            body(0, 0, False)
            body(1, 0, False)
            with pe.Fori(1, NG // 2 - 1) as i:
                body(0, i, False)
                body(1, i, False)
            body(0, NG // 2 - 1, False)
            body(1, NG // 2 - 1, True)
            outputs(NG // 2 - 1, 1)

        @block.scalar
        def _(act):
            def high(i, u, c):
                act.wait_ge(u_in[c % 2], i * (16 * GJ) + 16 * ((u * GJ + c) // 2 + 1))
                if due(of(2, i, u, c, -2)):
                    act.wait_ge(hi_psum, of(2, i, u, c, -2))
                    act.wait_ge(ul_done, of(1, i, u, c, -1))
                act.copy(u_hi[:, c % 2, :], u_raw[:, c % 2, :]).then_inc(uh_done, 1)

            def high_turned(i, u, c):
                for b in range(2):
                    act.wait_ge(hi_psum, of(2, i, u, c, b + 1))
                    if b == 0 and due(of(2, i, u, c, -2)):
                        act.wait_ge(h_psum, of(2, i, u, c, -2))
                    act.copy(uT_hi[:, c % 2, 4 * b:4 * b + 4, :].rearrange("p c e -> p (c e)"), ps[:, b, :])\
                       .then_inc(hT_done, 1)

            def gelu(i, u, c, half):
                act.wait_ge(h_psum, of(2, i, u, c, half + 1))
                if due(of(2, i, u, c, half - 1)):
                    act.wait_ge(w_mul, of(2, i, u, c, half - 1))
                act.activation(ga[:, half, :], ps[:, 2 + 2 * (c % 2) + half, 0:HALF], ACT.Gelu).then_inc(gelu_done, 1)

            def body(u, i, end):
                act.wait_ge(v_in[u], i * 16 + 16)
                for c in range(GJ):
                    if not (end and c == GJ - 1):
                        high_turned(i, u, c + 1)
                    if not (end and c >= GJ - 2):
                        high(i, u, c + 2)
                    gelu(i, u, c, 0)
                    if c == 0 and due(i * (2 * NO) + (u * NO - NO)):
                        act.wait_ge(o_psum, i * (2 * NO) + (u * NO - NO))
                    act.copy(vhi[u][:, c, :], vlo_raw[u][:, c, :]).then_inc(vh_done, 1)
                    gelu(i, u, c, 1)

            act.copy(ident_r[:, :], s.ident[:, :]).then_inc(ident_done, 1)
            high(0, 0, 0)
            high(0, 0, 1)
            high_turned(0, 0, 0)
            body(0, 0, False)
            body(1, 0, False)
            with act.Fori(1, NG // 2 - 1) as i:
                body(0, i, False)
                body(1, i, False)
            body(0, NG // 2 - 1, False)
            body(1, NG // 2 - 1, True)

        @block.vector
        def _(dve):
            def low(i, u, c):
                dve.wait_ge(uh_done, of(1, i, u, c, 1))
                dve.tensor_tensor(u_lo[:, c % 2, :], u_raw[:, c % 2, :], u_hi[:, c % 2, :].bitcast(F32), ALU.subtract)\
                   .then_inc(ul_done, 1)

            def low_turned(i, u, c):
                for b in range(2):
                    dve.wait_ge(lo_psum, of(2, i, u, c, b + 1))
                    if b == 0 and due(of(2, i, u, c, -2)):
                        dve.wait_ge(h_psum, of(2, i, u, c, -2))
                    dve.tensor_copy(uT_lo[:, c % 2, 4 * b:4 * b + 4, :].rearrange("p c e -> p (c e)"), ps[:, b, :])\
                       .then_inc(lT_done, 1)

            def weights(i, u, c, half):
                cols = slice(half * HALF, (half + 1) * HALF)
                dve.wait_ge(gelu_done, of(2, i, u, c, half + 1))
                if c == 0 and half == 0 and due(i * (2 * NO) + (u * NO - NO)):
                    dve.wait_ge(o_psum, i * (2 * NO) + (u * NO - NO))
                dve.tensor_tensor(wt[:, half, :], ga[:, half, :], gt[:, u, cols, c], ALU.mult).then_inc(w_mul, 1)
                dve.wait_ge(w_mul, of(2, i, u, c, half + 1))
                dve.tensor_copy(whi[:, u, c, cols], wt[:, half, :]).then_inc(wh_done, 1)
                dve.wait_ge(wh_done, of(2, i, u, c, half + 1))
                dve.tensor_tensor(wlo[:, u, c, cols], wt[:, half, :], whi[:, u, c, cols].bitcast(F32),
                                  ALU.subtract).then_inc(w_done, 1)

            def gather(i, u):
                for n in range(NO):
                    dc, half = n // 2, n % 2
                    dve.wait_ge(o_psum, i * (2 * NO) + (u * NO + n + 1))
                    x = outT[:, dc, half * HALF:(half + 1) * HALF]
                    dve.tensor_tensor(x, x, ps[:, 6 + n % 2, 0:HALF], ALU.add).then_inc(o_done, 1)

            def body(u, i, end):
                dve.wait_ge(g_in[u], i * 16 + 16)
                for c in range(GJ):
                    if not (end and c == GJ - 1):
                        low_turned(i, u, c + 1)
                    if not (end and c >= GJ - 2):
                        low(i, u, c + 2)
                    weights(i, u, c, 0)
                    dve.wait_ge(vh_done, of(1, i, u, c, 1))
                    dve.tensor_tensor(vlo[u][:, c, :], vlo_raw[u][:, c, :], vhi[u][:, c, :].bitcast(F32), ALU.subtract)\
                       .then_inc(vl_done, 1)
                    weights(i, u, c, 1)
                    if c == 0 and not (isinstance(i, int) and i == 0 and u == 0):
                        gather(i if u == 1 else i - 1, 1 - u)

            dve.memset(outT[:, :, :], 0.0).then_inc(zeroed, 1)
            dve.wait_ge(zeroed, 1)
            low(0, 0, 0)
            low(0, 0, 1)
            low_turned(0, 0, 0)
            body(0, 0, False)
            body(1, 0, False)
            with dve.Fori(1, NG // 2 - 1) as i:
                body(0, i, False)
                body(1, i, False)
            body(0, NG // 2 - 1, False)
            body(1, NG // 2 - 1, True)
            gather(NG // 2 - 1, 1)
    sem.clear()


def stage_norm2(nc, s, io):
    at = s.at
    hr = at("h2", 14000, [P, 2, D])
    yr = at("y2", 16048, [P, 2, D])
    gb = at("ln2_gb", 18096, [P, 2, D])
    st = at("ln2_st", 20144, [P, 2, 6])
    mv = at("ln2_mv", 20160, [P, 2])
    rs = at("ln2_rs", 20168, [P, 2])
    sem = Semaphores(nc)
    with ExitStack() as ctx:
        h_in, gb_in, t_psum, t_read, chain, eps_done, sqrt_done = ([sem("y_h0"), sem("y_h1")], sem("y_gb"), sem("y_tp"),
                                                                  sem("y_read"), sem("y_chain"), sem("y_eps"), sem("y_sqrt"))
        y_ready, y_sent = sem("y_ready"), [sem("y_sent0"), sem("y_sent1")]
        ps = ctx.enter_context(nc.psum_tensor("ps_y", [P, 8, 512], F32))
        block = ctx.enter_context(nc.Block())

        @block.sync
        def _(sp):
            sp.dma_start(gb[:, 0, :], io.ln2_g.partition_broadcast(P)).then_inc(gb_in, 16)
            sp.dma_start(gb[:, 1, :], io.ln2_b.partition_broadcast(P)).then_inc(gb_in, 16)
            for t in range(NT):
                if t >= 2:
                    sp.wait_ge(t_read, t - 1)
                sp.dma_start(hr[0:ROWS[t], t % 2, :], io.h_rows[t * P:t * P + ROWS[t], :]).then_inc(h_in[t % 2], 16)

        @block.gpsimd
        def _(pool):
            for t in range(NT):
                pool.wait_ge(y_ready, t + 1)
                out = io.y_prompt[0, t * P:(t + 1) * P, :] if t < 4 else io.y_sample.rearrange("b t d -> (b t) d")
                pool.dma_start(out, yr[0:ROWS[t], t % 2, :]).then_inc(y_sent[t % 2], 16)
            pool.wait_ge(y_sent[0], 48)
            pool.wait_ge(y_sent[1], 32)

        @block.tensor
        def _(pe):
            for t in range(NT):
                if t >= 2:
                    pe.wait_ge(t_read, t - 1)
                for dc in range(DC):
                    b, q = 2 * (t % 2) + dc // 4, dc % 4
                    last = pe.transpose(ps[0:ROWS[t], b, q * P:(q + 1) * P], s.outT[:, dc, t * P:t * P + ROWS[t]],
                                        s.ident[:, :])
                last.then_inc(t_psum, 1)

        @block.scalar
        def _(act):
            for t in range(NT):
                act.wait_ge(eps_done, t + 1)
                act.activation(rs[0:ROWS[t], 0:1], rs[0:ROWS[t], 0:1], ACT.Sqrt).then_inc(sqrt_done, 1)

        @block.vector
        def _(dve):
            step = Count()

            def link(ins):
                ins.then_inc(chain, 1)
                dve.wait_ge(chain, step.add())

            dve.wait_ge(gb_in, 32)
            for t in range(NT):
                r = ROWS[t]
                dve.wait_ge(t_psum, t + 1)
                dve.wait_ge(h_in[t % 2], 16 * (t // 2 + 1))
                if t >= 2:
                    dve.wait_ge(y_sent[t % 2], 16 * (t // 2))
                for q in range(2):
                    last = dve.scalar_tensor_tensor(out=yr[0:r, t % 2, q * 512:(q + 1) * 512],
                                                    in0=hr[0:r, t % 2, q * 512:(q + 1) * 512], scalar=DN_ALPHA,
                                                    in1=ps[0:r, 2 * (t % 2) + q, :], op0=ALU.mult, op1=ALU.add)
                last.then_inc(t_read, 1)
                dve.wait_ge(t_read, t + 1)
                norm_rows(dve, link, yr[0:r, t % 2, :], st, mv, rs, eps_done, sqrt_done, t, gb[:, 0, :], gb[:, 1, :], r)\
                    .then_inc(y_ready, 1)
    sem.clear()


OUTS = [("y_prompt", (1, TP, D)), ("y_sample", (DB, DS, D)),
        ("p_cmp", (1, TP, 2, KV, HD)), ("p_slc", (1, TP, 2, KV, HD)), ("p_win", (1, TP, 2, KV, HD)),
        ("p_C", (1, AH, DQK, DV)), ("p_n", (1, AH, DQK)), ("p_m", (1, AH)),
        ("s_cmp", (DB, DS, 2, KV, HD)), ("s_slc", (DB, DS, 2, KV, HD)), ("s_win", (DB, PAST, 2, KV, HD)),
        ("s_C", (DB, AH, DQK, DV)), ("s_n", (DB, AH, DQK)), ("s_m", (DB, AH))]
STAGES = [stage_load, stage_project, stage_mlstm, stage_compress, stage_attend_prompt, stage_attend_samples,
          stage_merge, stage_norm1, stage_query, stage_gates, stage_experts, stage_norm2]


def program(nc, tensors):
    io = Names()
    io.x_prompt = tensors["x_prompt"]
    io.x_sample = tensors["x_sample"]
    io.cache_cmp_kv = tensors["cache_cmp_kv"]
    io.cache_slc_kv = tensors["cache_slc_kv"]
    io.cache_win_kv = tensors["cache_win_kv"]
    io.state_C = tensors["state_C"]
    io.state_n = tensors["state_n"]
    io.state_m = tensors["state_m"]
    io.page_table = tensors["page_table"]
    io.w_in = tensors["w_in"]
    io.b_in = tensors["b_in"]
    io.norm_a_g = tensors["norm_a_g"]
    io.nsa_pe = tensors["nsa_pe"]
    io.nsa_w_cmp = tensors["nsa_w_cmp"]
    io.w_br_a = tensors["w_br_a"]
    io.w_br_b = tensors["w_br_b"]
    io.w_merge = tensors["w_merge"]
    io.w_out = tensors["w_out"]
    io.ln1_g = tensors["ln1_g"]
    io.ln1_b = tensors["ln1_b"]
    io.peer_wq = tensors["peer_wq"]
    io.peer_keys = tensors["peer_keys"]
    io.peer_u = tensors["peer_u"]
    io.peer_v = tensors["peer_v"]
    io.ln2_g = tensors["ln2_g"]
    io.ln2_b = tensors["ln2_b"]
    io.y_prompt = tensors["y_prompt"]
    io.y_sample = tensors["y_sample"]
    io.p_cmp = tensors["p_cmp"]
    io.p_slc = tensors["p_slc"]
    io.p_win = tensors["p_win"]
    io.p_C = tensors["p_C"]
    io.p_n = tensors["p_n"]
    io.p_m = tensors["p_m"]
    io.s_cmp = tensors["s_cmp"]
    io.s_slc = tensors["s_slc"]
    io.s_win = tensors["s_win"]
    io.s_C = tensors["s_C"]
    io.s_n = tensors["s_n"]
    io.s_m = tensors["s_m"]
    s = place(nc)
    io.o_rows = nc.dram_tensor("o_rows", (T, AH * DV), F32, kind="Internal").ap()
    io.h_rows = nc.dram_tensor("h_rows", (T, D), F32, kind="Internal").ap()
    io.gates = nc.dram_tensor("gate_tables", (NG, P, T * GJ), F32, kind="Internal").ap()
    with ExitStack() as ctx:
        s.wq_in = [ctx.enter_context(nc.semaphore(f"wq_in{i}")) for i in range(3)]
        s.keys_in = ctx.enter_context(nc.semaphore("keys_in"))
        for stage in STAGES:
            stage(nc, s, io)


def kernel(**inputs):
    import concourse.bacc as bacc
    from concourse.bass_utils import run_bass_kernel_spmd

    nc = bacc.Bacc("TRN2", target_bir_lowering=False, num_devices=1)
    arrays, tensors = {}, {}
    for name, a in inputs.items():
        a = np.ascontiguousarray(a)
        arrays[f"in_{name}"] = a
        tensors[name] = nc.dram_tensor(f"in_{name}", a.shape, mybir.dt.from_np(a.dtype), kind="ExternalInput").ap()
    for name, shape in OUTS:
        tensors[name] = nc.dram_tensor(f"out_{name}", shape, F32, kind="ExternalOutput").ap()
    program(nc, tensors)
    r = run_bass_kernel_spmd(nc, [arrays], core_ids=[0])
    return tuple(r.results[0][f"out_{name}"] for name, _ in OUTS)
```
